# Optimizing a Trainium2 kernel written in Bass

```python
import math
import jax, jax.numpy as jnp
from jax import lax
import numpy as np

D_MODEL = 1024
BATCH = 1
SEQ = 1024
DEPTH = 1

D_MIX = 2 * D_MODEL
ATTN_WIDTH = D_MIX // 2
V_HEAD_DIM = 128
QK_HEAD_DIM = V_HEAD_DIM // 2
ATTN_HEADS = ATTN_WIDTH // V_HEAD_DIM
Q_WIDTH = ATTN_HEADS * 2 * QK_HEAD_DIM
K_WIDTH = ATTN_HEADS * 2 * QK_HEAD_DIM
V_WIDTH = ATTN_HEADS * V_HEAD_DIM
LRU_WIDTH = D_MIX - ATTN_WIDTH
LRU_BLOCKS = 8
LRU_BLOCK = LRU_WIDTH // LRU_BLOCKS
LRU_C = 8.0
CONV_WIDTH = 4
Q_BLOCK = 128
NORM_EPS = 1e-6
IN_SPLITS = (Q_WIDTH, K_WIDTH, V_WIDTH, ATTN_WIDTH, LRU_WIDTH, LRU_WIDTH)
D_IN_PROJ = sum(IN_SPLITS)
SPLIT_POINTS = tuple(int(v) for v in np.cumsum(IN_SPLITS)[:-1])


def rmsnorm(x, g):
    xf = x.astype(jnp.float32)
    y = xf * lax.rsqrt(jnp.mean(xf * xf, axis=-1, keepdims=True) + NORM_EPS)
    return (y * g.astype(jnp.float32)).astype(x.dtype)

def lambda_init_for(layer_idx):
    return 0.8 - 0.6 * math.exp(-0.3 * layer_idx)

def diff_attention(q, k, v, lam):
    S = q.shape[1]
    scale = QK_HEAD_DIM ** -0.5
    outs = []
    for i in range(S // Q_BLOCK):
        q0 = i * Q_BLOCK
        end = q0 + Q_BLOCK
        s = jnp.einsum('bqhcd,bkhcd->bhcqk', q[:, q0:end], k[:, :end],
                       preferred_element_type=jnp.float32) * scale
        qpos = q0 + jnp.arange(Q_BLOCK)
        kpos = jnp.arange(end)
        causal = kpos[None, :] <= qpos[:, None]
        p = jax.nn.softmax(jnp.where(causal, s, -jnp.inf), axis=-1)
        w = p[:, :, 0] - lam * p[:, :, 1]
        outs.append(jnp.einsum('bhqk,bkhe->bqhe', w, v[:, :end].astype(jnp.float32)))
    return jnp.concatenate(outs, axis=1)

def causal_depthwise_conv(x, w, b):
    y = lax.conv_general_dilated(
        x, w[:, None, :].astype(x.dtype), window_strides=(1,), padding=[(CONV_WIDTH - 1, 0)],
        dimension_numbers=('NWC', 'WIO', 'NWC'), feature_group_count=x.shape[-1])
    return y + b.astype(x.dtype)

def _lin_combine(c1, c2):
    a1, b1 = c1
    a2, b2 = c2
    return a1 * a2, a2 * b1 + b2

def rg_lru(xc, w_r, b_r, w_i, b_i, lam_param):
    B, S, _ = xc.shape
    xb = xc.reshape(B, S, LRU_BLOCKS, LRU_BLOCK).astype(jnp.float32)
    r = jax.nn.sigmoid(jnp.einsum('bsnc,ncd->bsnd', xb, w_r.astype(jnp.float32)).reshape(B, S, LRU_WIDTH)
                       + b_r.astype(jnp.float32))
    gi = jax.nn.sigmoid(jnp.einsum('bsnc,ncd->bsnd', xb, w_i.astype(jnp.float32)).reshape(B, S, LRU_WIDTH)
                        + b_i.astype(jnp.float32))
    log_a = -LRU_C * r * jax.nn.softplus(-lam_param.astype(jnp.float32))
    a = jnp.exp(log_a)
    mult = jnp.sqrt(jnp.maximum(-jnp.expm1(2.0 * log_a), 0.0))
    bterm = mult * gi * xc.astype(jnp.float32)
    _, h = lax.associative_scan(_lin_combine, (a, bterm), axis=1)
    return h

def first_inputs(seed: int = 0) -> dict:
    key = jax.random.key(seed)
    ks = jax.random.split(key, 20)
    f32 = jnp.float32
    x = jax.random.normal(ks[0], (BATCH, SEQ, D_MODEL), f32)
    pre_norm_g = 1.0 + 0.05 * jax.random.normal(ks[1], (DEPTH, D_MODEL), f32)
    w_in = jax.random.normal(ks[2], (DEPTH, D_MODEL, D_IN_PROJ), f32) * D_MODEL ** -0.5
    lambda_q1 = 0.1 * jax.random.normal(ks[3], (DEPTH, QK_HEAD_DIM), f32)
    lambda_k1 = 0.1 * jax.random.normal(ks[4], (DEPTH, QK_HEAD_DIM), f32)
    lambda_q2 = 0.1 * jax.random.normal(ks[5], (DEPTH, QK_HEAD_DIM), f32)
    lambda_k2 = 0.1 * jax.random.normal(ks[6], (DEPTH, QK_HEAD_DIM), f32)
    subln_g = 1.0 + 0.05 * jax.random.normal(ks[7], (DEPTH, V_HEAD_DIM), f32)
    conv_w = jax.random.normal(ks[8], (DEPTH, CONV_WIDTH, LRU_WIDTH), f32) * CONV_WIDTH ** -0.5
    conv_b = 0.02 * jax.random.normal(ks[9], (DEPTH, LRU_WIDTH), f32)
    w_rgate = jax.random.normal(ks[10], (DEPTH, LRU_BLOCKS, LRU_BLOCK, LRU_BLOCK), f32) * LRU_BLOCK ** -0.5
    b_rgate = 0.02 * jax.random.normal(ks[11], (DEPTH, LRU_WIDTH), f32)
    w_igate = jax.random.normal(ks[12], (DEPTH, LRU_BLOCKS, LRU_BLOCK, LRU_BLOCK), f32) * LRU_BLOCK ** -0.5
    b_igate = 0.02 * jax.random.normal(ks[13], (DEPTH, LRU_WIDTH), f32)
    a0 = jax.random.uniform(ks[14], (DEPTH, LRU_WIDTH), f32, 0.9, 0.999)
    s0 = a0 ** (1.0 / LRU_C)
    lru_lambda = jnp.log(s0) - jnp.log1p(-s0)
    w_out = jax.random.normal(ks[15], (DEPTH, D_MIX, D_MODEL), f32) * D_MIX ** -0.5
    post_norm_g = 1.0 + 0.05 * jax.random.normal(ks[16], (DEPTH, D_MODEL), f32)
    return {"x": x, "pre_norm_g": pre_norm_g, "w_in": w_in,
            "lambda_q1": lambda_q1, "lambda_k1": lambda_k1,
            "lambda_q2": lambda_q2, "lambda_k2": lambda_k2, "subln_g": subln_g,
            "conv_w": conv_w, "conv_b": conv_b,
            "w_rgate": w_rgate, "b_rgate": b_rgate, "w_igate": w_igate, "b_igate": b_igate,
            "lru_lambda": lru_lambda, "w_out": w_out, "post_norm_g": post_norm_g}

def first_block(x, pre_norm_g, w_in, lambda_q1, lambda_k1, lambda_q2, lambda_k2, subln_g,
              conv_w, conv_b, w_rgate, b_rgate, w_igate, b_igate, lru_lambda, w_out, post_norm_g):
    B, S, _ = x.shape
    for l in range(DEPTH):
        h = rmsnorm(x, pre_norm_g[l])
        proj = jnp.einsum('bsd,de->bse', h, w_in[l])
        q, k, v, g_attn, x_lru, g_lru = jnp.split(proj, SPLIT_POINTS, axis=-1)

        lam_init = lambda_init_for(l)
        lam = (jnp.exp(jnp.sum(lambda_q1[l].astype(jnp.float32) * lambda_k1[l].astype(jnp.float32)))
               - jnp.exp(jnp.sum(lambda_q2[l].astype(jnp.float32) * lambda_k2[l].astype(jnp.float32)))
               + lam_init)
        qh = q.reshape(B, S, ATTN_HEADS, 2, QK_HEAD_DIM)
        kh = k.reshape(B, S, ATTN_HEADS, 2, QK_HEAD_DIM)
        vh = v.reshape(B, S, ATTN_HEADS, V_HEAD_DIM)
        o = diff_attention(qh, kh, vh, lam)
        o = rmsnorm(o, subln_g[l]) * (1.0 - lam_init)
        y_attn = o.reshape(B, S, ATTN_WIDTH).astype(x.dtype) * jax.nn.silu(g_attn)

        xc = causal_depthwise_conv(x_lru, conv_w[l], conv_b[l])
        hr = rg_lru(xc, w_rgate[l], b_rgate[l], w_igate[l], b_igate[l], lru_lambda[l])
        y_lru = hr.astype(x.dtype) * jax.nn.silu(g_lru)

        y = jnp.concatenate([y_attn, y_lru], axis=-1)
        y = jnp.einsum('bse,ed->bsd', y, w_out[l])
        x = x + rmsnorm(y, post_norm_g[l])
    return x


SSD_D_INNER = 1024
SSD_HEAD_DIM = 64
SSD_HEADS = SSD_D_INNER // SSD_HEAD_DIM
SSD_GROUPS = 2
SSD_STATE = 128
SSD_CONV = 4
SSD_CHUNK = 128
SSD_CONV_DIM = SSD_D_INNER + 2 * SSD_GROUPS * SSD_STATE

ATTN_HEAD_DIM = 128
ATTN_HEADS_PER_GROUP = 4
DILATED_GROUPS = ((128, 1), (512, 4), (2048, 16))
ATTN_HEADS_2 = ATTN_HEADS_PER_GROUP * len(DILATED_GROUPS)
ATTN_WIDTH_2 = ATTN_HEADS_2 * ATTN_HEAD_DIM
ATTN_OUT_WIDTH = ATTN_HEADS_PER_GROUP * ATTN_HEAD_DIM

POOL_WINDOWS = (2, 4, 8, 16)
POOL_WIDTH = 1024
POOL_GROUP_WIDTH = POOL_WIDTH // len(POOL_WINDOWS)

N_BRANCHES = 3
D_FF = 4 * D_MODEL
EPS = 1e-6
IN_SIZES = (SSD_D_INNER, SSD_CONV_DIM, SSD_HEADS, ATTN_WIDTH_2, ATTN_WIDTH_2, ATTN_WIDTH_2, POOL_WIDTH, N_BRANCHES * D_MODEL)
IN_WIDTH = SSD_D_INNER + SSD_CONV_DIM + SSD_HEADS + 3 * ATTN_WIDTH_2 + POOL_WIDTH + N_BRANCHES * D_MODEL


def _rms(x, w):
    xf = x.astype(jnp.float32)
    y = xf * lax.rsqrt(jnp.mean(xf * xf, axis=-1, keepdims=True) + EPS)
    return (y * w.astype(jnp.float32)).astype(x.dtype)

def _alibi_slopes(n):
    def pow2(k):
        start = 2.0 ** (-8.0 / k)
        return [start ** (i + 1) for i in range(k)]
    if math.log2(n).is_integer():
        s = pow2(n)
    else:
        c = 2 ** math.floor(math.log2(n))
        s = pow2(c) + pow2(2 * c)[0::2][: n - c]
    return np.sort(np.asarray(s, np.float32))[::-1].copy()

def _causal_dwconv(x, w, bias):
    ch = x.shape[-1]
    y = lax.conv_general_dilated(x, w[:, None, :].astype(x.dtype), window_strides=(1,),
                                 padding=[(SSD_CONV - 1, 0)],
                                 dimension_numbers=('NWC', 'WIO', 'NWC'),
                                 feature_group_count=ch)
    return y + bias

def _ssd(xs, dt, A, B, C, D):
    b, S, H, P = xs.shape
    G, N, L = SSD_GROUPS, SSD_STATE, SSD_CHUNK
    J = H // G
    nc = S // L
    xc = xs.reshape(b, nc, L, G, J, P)
    X = xc * dt.reshape(b, nc, L, G, J)[..., None]
    a_cum = jnp.cumsum((dt * A).reshape(b, nc, L, G, J), axis=2)
    Bc = B.reshape(b, nc, L, G, N)
    Cc = C.reshape(b, nc, L, G, N)
    seg = a_cum[:, :, :, None] - a_cum[:, :, None, :]
    causal = jnp.tril(jnp.ones((L, L), bool))[:, :, None, None]
    decay = jnp.exp(jnp.where(causal, seg, -jnp.inf))
    cb = jnp.einsum('bclgn,bcsgn->bclsg', Cc, Bc)
    y_diag = jnp.einsum('bclsgj,bcsgjp->bclgjp', cb[..., None] * decay, X)
    Xd = X * jnp.exp(a_cum[:, :, -1:] - a_cum)[..., None]
    states = jnp.einsum('bclgn,bclgjp->bcgjpn', Bc, Xd)
    chunk_decay = jnp.exp(a_cum[:, :, -1])

    def step(h, inp):
        st, dec = inp
        return dec[..., None, None] * h + st, h

    h0 = jnp.zeros((b, G, J, P, N), X.dtype)
    _, prev = lax.scan(step, h0, (jnp.moveaxis(states, 1, 0), jnp.moveaxis(chunk_decay, 1, 0)))
    prev = jnp.moveaxis(prev, 0, 1)
    y_off = jnp.einsum('bclgn,bcgjpn->bclgjp', Cc, prev) * jnp.exp(a_cum)[..., None]
    y = y_diag + y_off + D.reshape(G, J)[:, :, None] * xc
    return y.reshape(b, S, H * P)

def _dilated_window_attn(q, k, v, steps, dilation, slopes):
    b, S, h, e = q.shape
    n = S // dilation
    nb = -(-n // steps)
    n_pad = nb * steps

    def to_sub(t):
        t = t.reshape(b, n, dilation, h, e).transpose(0, 3, 2, 1, 4)
        return jnp.pad(t, ((0, 0), (0, 0), (0, 0), (0, n_pad - n), (0, 0)))

    qs, ks, vs = to_sub(q), to_sub(k), to_sub(v)
    qb = qs.reshape(b, h, dilation, nb, steps, e)

    def band(t):
        tp = jnp.pad(t, ((0, 0), (0, 0), (0, 0), (steps, 0), (0, 0)))
        prev = tp[:, :, :, :n_pad].reshape(b, h, dilation, nb, steps, e)
        cur = t.reshape(b, h, dilation, nb, steps, e)
        return jnp.concatenate([prev, cur], axis=4)

    kb, vb = band(ks), band(vs)
    s = jnp.einsum('bhdnqe,bhdnke->bhdnqk', qb, kb) * (e ** -0.5)
    qi = jnp.arange(steps)[:, None]
    kj = jnp.arange(2 * steps)[None, :]
    rel = qi + steps - kj
    blk = jnp.arange(nb)[:, None, None]
    valid = (rel >= 0) & (rel <= steps) & (blk * steps + kj - steps >= 0)
    alibi = -slopes[:, None, None] * (rel * dilation).astype(jnp.float32)
    s = jnp.where(valid, s + alibi[:, None, None], -jnp.inf)
    lse = jax.nn.logsumexp(s, axis=-1)
    p = jnp.exp(s - lse[..., None])
    o = jnp.einsum('bhdnqk,bhdnke->bhdnqe', p, vb)
    o = o.reshape(b, h, dilation, n_pad, e)[:, :, :, :n].transpose(0, 3, 2, 1, 4).reshape(b, S, h, e)
    lse = lse.reshape(b, h, dilation, n_pad)[:, :, :, :n].transpose(0, 3, 2, 1).reshape(b, S, h)
    return o, lse

def _multi_scale_pool(u, w_mix):
    b, S, _ = u.shape
    ug = u.reshape(b, S, len(POOL_WINDOWS), POOL_GROUP_WIDTH)
    cs = jnp.cumsum(ug, axis=1)
    t = jnp.arange(S)
    outs = []
    for gi, w in enumerate(POOL_WINDOWS):
        csg = cs[:, :, gi]
        shifted = jnp.pad(csg, ((0, 0), (w, 0), (0, 0)))[:, :S]
        count = jnp.minimum(t + 1, w).astype(jnp.float32)[None, :, None]
        outs.append((csg - shifted) / count - ug[:, :, gi])
    pooled = jnp.stack(outs, axis=2)
    return jnp.einsum('bsgi,gio->bsgo', pooled, w_mix).reshape(b, S, POOL_WIDTH)

def _hybrid_mixer(h, w_in, conv_w, conv_b, dt_bias, a_log, d_skip, ssd_norm_w, w_ssd_out,
                  q_norm_w, k_norm_w, w_attn_out, w_pool_mix, pool_scale, w_pool_out, w_out, slopes):
    f32 = jnp.float32
    dtype = h.dtype
    b, S, _ = h.shape
    splits = np.cumsum(IN_SIZES)[:-1].tolist()
    z, xbc, dt_raw, q, k, v, u, gates = jnp.split(h @ w_in, splits, axis=-1)

    xbc = jax.nn.silu(_causal_dwconv(xbc, conv_w, conv_b)).astype(f32)
    xs, Bm, Cm = jnp.split(xbc, [SSD_D_INNER, SSD_D_INNER + SSD_GROUPS * SSD_STATE], axis=-1)
    dt = jax.nn.softplus(dt_raw.astype(f32) + dt_bias.astype(f32))
    A = -jnp.exp(a_log.astype(f32))
    y = _ssd(xs.reshape(b, S, SSD_HEADS, SSD_HEAD_DIM), dt, A,
             Bm.reshape(b, S, SSD_GROUPS, SSD_STATE), Cm.reshape(b, S, SSD_GROUPS, SSD_STATE),
             d_skip.astype(f32))
    y = (y * jax.nn.silu(z.astype(f32))).reshape(b, S, SSD_GROUPS, SSD_D_INNER // SSD_GROUPS)
    y = (y * lax.rsqrt(jnp.mean(y * y, axis=-1, keepdims=True) + EPS)).reshape(b, S, SSD_D_INNER)
    y_ssd = (y * ssd_norm_w.astype(f32)).astype(dtype) @ w_ssd_out

    qh = _rms(q.reshape(b, S, ATTN_HEADS_2, ATTN_HEAD_DIM).astype(f32), q_norm_w)
    kh = _rms(k.reshape(b, S, ATTN_HEADS_2, ATTN_HEAD_DIM).astype(f32), k_norm_w)
    vh = v.reshape(b, S, ATTN_HEADS_2, ATTN_HEAD_DIM).astype(f32)
    outs, lses = [], []
    for gi, (win, dil) in enumerate(DILATED_GROUPS):
        sl = slice(gi * ATTN_HEADS_PER_GROUP, (gi + 1) * ATTN_HEADS_PER_GROUP)
        o, lse = _dilated_window_attn(qh[:, :, sl], kh[:, :, sl], vh[:, :, sl], win // dil, dil, slopes[gi])
        outs.append(o)
        lses.append(lse)
    wts = jax.nn.softmax(jnp.stack(lses, axis=0), axis=0)
    o = jnp.sum(wts[..., None] * jnp.stack(outs, axis=0), axis=0).reshape(b, S, ATTN_OUT_WIDTH)
    y_attn = o.astype(dtype) @ w_attn_out

    y_pool = (_multi_scale_pool(u.astype(f32), w_pool_mix) * pool_scale).astype(dtype) @ w_pool_out

    g_ssd, g_attn, g_pool = jnp.split(jax.nn.sigmoid(gates.astype(f32)).astype(dtype), N_BRANCHES, axis=-1)
    return (g_ssd * y_ssd + g_attn * y_attn + g_pool * y_pool) @ w_out

def second_inputs(seed: int = 0) -> dict:
    key = jax.random.key(seed)
    ks = jax.random.split(key, 24)
    n = jax.random.normal
    L, D = DEPTH, D_MODEL
    u01 = jax.random.uniform(ks[9], (L, SSD_HEADS))
    dt0 = jnp.exp(u01 * (math.log(0.1) - math.log(0.001)) + math.log(0.001))
    return {
        "x": n(ks[0], (BATCH, SEQ, D), jnp.float32),
        "c": n(ks[1], (BATCH, D), jnp.float32),
        "w_ada": n(ks[2], (L, D, 6 * D)) * D ** -0.5,
        "b_ada": n(ks[3], (L, 6 * D)) * 0.01,
        "norm1_w": 1.0 + 0.05 * n(ks[4], (L, D)),
        "norm2_w": 1.0 + 0.05 * n(ks[5], (L, D)),
        "w_in": n(ks[6], (L, D, IN_WIDTH)) * D ** -0.5,
        "conv_w": n(ks[7], (L, SSD_CONV, SSD_CONV_DIM)) * SSD_CONV ** -0.5,
        "conv_b": n(ks[8], (L, SSD_CONV_DIM)) * 0.01,
        "dt_bias": dt0 + jnp.log(-jnp.expm1(-dt0)),
        "a_log": jnp.log(jax.random.uniform(ks[10], (L, SSD_HEADS), minval=1.0, maxval=16.0)),
        "d_skip": 1.0 + 0.05 * n(ks[11], (L, SSD_HEADS)),
        "ssd_norm_w": 1.0 + 0.05 * n(ks[12], (L, SSD_D_INNER)),
        "w_ssd_out": n(ks[13], (L, SSD_D_INNER, D)) * SSD_D_INNER ** -0.5,
        "q_norm_w": 1.0 + 0.05 * n(ks[14], (L, ATTN_HEAD_DIM)),
        "k_norm_w": 1.0 + 0.05 * n(ks[15], (L, ATTN_HEAD_DIM)),
        "w_attn_out": n(ks[16], (L, ATTN_OUT_WIDTH, D)) * ATTN_OUT_WIDTH ** -0.5,
        "w_pool_mix": n(ks[17], (L, len(POOL_WINDOWS), POOL_GROUP_WIDTH, POOL_GROUP_WIDTH)) * POOL_GROUP_WIDTH ** -0.5,
        "pool_scale": 1.0 + 0.05 * n(ks[18], (L, POOL_WIDTH)),
        "w_pool_out": n(ks[19], (L, POOL_WIDTH, D)) * POOL_WIDTH ** -0.5,
        "w_out": n(ks[20], (L, D, D)) * D ** -0.5,
        "w_ff1": n(ks[21], (L, D, D_FF)) * D ** -0.5,
        "w_ff2": n(ks[22], (L, D_FF, D)) * D_FF ** -0.5,
    }

def second_block(x, c, w_ada, b_ada, norm1_w, norm2_w, w_in, conv_w, conv_b, dt_bias, a_log, d_skip,
              ssd_norm_w, w_ssd_out, q_norm_w, k_norm_w, w_attn_out, w_pool_mix, pool_scale,
              w_pool_out, w_out, w_ff1, w_ff2):
    cond = jax.nn.silu(c)
    slopes = jnp.asarray(_alibi_slopes(ATTN_HEADS_2)).reshape(len(DILATED_GROUPS), ATTN_HEADS_PER_GROUP)
    for l in range(DEPTH):
        mod = (cond @ w_ada[l] + b_ada[l])[:, None, :]
        sh1, sc1, g1, sh2, sc2, g2 = jnp.split(mod, 6, axis=-1)
        h = _rms(x, norm1_w[l]) * (1 + sc1) + sh1
        x = x + g1 * _hybrid_mixer(h, w_in[l], conv_w[l], conv_b[l], dt_bias[l], a_log[l], d_skip[l],
                                   ssd_norm_w[l], w_ssd_out[l], q_norm_w[l], k_norm_w[l], w_attn_out[l],
                                   w_pool_mix[l], pool_scale[l], w_pool_out[l], w_out[l], slopes)
        h = _rms(x, norm2_w[l]) * (1 + sc2) + sh2
        x = x + g2 * (jnp.square(jax.nn.relu(h @ w_ff1[l])) @ w_ff2[l])
    return x


def setup_inputs(seed=0):
    out = dict(first_inputs(seed))
    for name, value in second_inputs(seed + 1).items():
        if name != "x":
            out[name + "_2"] = value
    return out


def reference(
    x, pre_norm_g, w_in, lambda_q1, lambda_k1, lambda_q2, lambda_k2, subln_g, conv_w, conv_b,
    w_rgate, b_rgate, w_igate, b_igate, lru_lambda, w_out, post_norm_g, c_2, w_ada_2, b_ada_2,
    norm1_w_2, norm2_w_2, w_in_2, conv_w_2, conv_b_2, dt_bias_2, a_log_2, d_skip_2,
    ssd_norm_w_2, w_ssd_out_2, q_norm_w_2, k_norm_w_2, w_attn_out_2, w_pool_mix_2, pool_scale_2,
    w_pool_out_2, w_out_2, w_ff1_2, w_ff2_2,
):
    x = first_block(
        x, pre_norm_g, w_in, lambda_q1, lambda_k1, lambda_q2, lambda_k2, subln_g, conv_w,
        conv_b, w_rgate, b_rgate, w_igate, b_igate, lru_lambda, w_out, post_norm_g,
    )
    return second_block(
        x, c_2, w_ada_2, b_ada_2, norm1_w_2, norm2_w_2, w_in_2, conv_w_2, conv_b_2, dt_bias_2,
        a_log_2, d_skip_2, ssd_norm_w_2, w_ssd_out_2, q_norm_w_2, k_norm_w_2, w_attn_out_2,
        w_pool_mix_2, pool_scale_2, w_pool_out_2, w_out_2, w_ff1_2, w_ff2_2,
    )


_drawn_inputs = setup_inputs


def setup_inputs(seed=0):
    import zlib

    import numpy as np

    out = dict(_drawn_inputs(seed))
    spreads = {}
    factors = {'lambda_q1': 3.446,
     'lambda_q2': 8.0,
     'b_rgate': 8.0,
     'b_igate': 8.0,
     'b_ada_2': 3.487,
     'conv_b_2': 8.0,
     'd_skip_2': 8.0,
     'ssd_norm_w_2': 5.191,
     'q_norm_w_2': 8.0,
     'k_norm_w_2': 8.0,
     'pool_scale_2': 4.861}
    for name, (base, spread) in spreads.items():
        noise = np.random.default_rng([zlib.crc32(name.encode()), seed]).standard_normal(out[name].shape)
        drawn = base * np.exp(spread * noise) if base else spread * noise
        out[name] = __import__('jax').numpy.asarray(drawn.astype(out[name].dtype))
    for name, factor in factors.items():
        out[name] = (out[name] * factor).astype(out[name].dtype)
    return out
```

```python
import math
from contextlib import ExitStack

import concourse.bass as bass
import numpy as np
from concourse import mybir

F32 = mybir.dt.float32
F32R = mybir.dt.float32r
ALU = mybir.AluOpType
ACT = mybir.ActivationFunctionType
AX = mybir.AxisListType.X
ds = bass.ds

P = 128
D = 1024
T = 1024
KT = D // P
TT = T // P
HALF = 512
HEADS = 8
QK = 64
LRU_BLOCKS = 8
TAPS = 4
EPS = 1e-6
LAM_INIT = 0.8 - 0.6 * math.exp(0.0)
NEG = -1e30
ADA = 6 * D
X_TILES = 2
ADA_COLS = ADA // LRU_BLOCKS

LRU_SLABS = 2 * LRU_BLOCKS
ATT_SLABS = 4 * HEADS
OUT1_SLABS = 2 * KT
LRU_0 = 0
ATT_0 = LRU_0 + LRU_SLABS
OUT1_0 = ATT_0 + ATT_SLABS
DT_0 = OUT1_0 + OUT1_SLABS
CV_TILES = 12
CV_0 = DT_0 + 1
Z_0 = CV_0 + CV_TILES
SO_0 = Z_0 + KT
DIL_HEADS = 12
DL_0 = SO_0 + 2 * KT
DL_ROUNDS = 4
DL_ROUND = 10
AO_0 = DL_0 + DL_ROUNDS * DL_ROUND
U_0 = AO_0 + 2 * KT
MX_0 = U_0 + KT
PO_0 = MX_0 + 2
WO_0 = PO_0 + 2 * KT
FF_0 = WO_0 + KT
FF_QUARTERS = 4
N_SLABS = FF_0 + FF_QUARTERS * 2 * KT

SSD_HEADS = 16
SSD_P = 64
CHUNKS = T // P

PARAM_COLS = {}


def _columns():
    at = 0
    for name, n in (
        ("pre_g", 8), ("conv1_w", 32), ("conv1_b", 8), ("b_r", 8), ("b_i", 8), ("lru_lam", 8), ("post_g", 8),
        ("subln_g", 1), ("lq", 2), ("lk", 2), ("c", 8), ("b_ada", 48),
        ("conv2_w", CV_TILES * TAPS), ("conv2_b", CV_TILES), ("dt_bias", 1), ("a_log", 1), ("d_skip", 8), ("ssd_norm", 8),
        ("norm1", 8), ("norm2", 8), ("q_norm", 1), ("k_norm", 1), ("pool_scale", 8),
    ):
        PARAM_COLS[name] = (at, n)
        at += n
    return at


N_PARAMS = _columns()
IDENT, CAUSAL, TRI, LASTROW, INV, N_CONST = 0, 128, 256, 384, 512, 528


class Count:

    def __init__(self, sem):
        self.sem, self.base, self.off, self.var, self.per = sem, 0, 0, None, 0

    def enter(self, var, per):
        self.base, self.off, self.var, self.per = self.base + self.off, 0, var, per

    def leave(self, rounds):
        assert self.off == self.per, (self.sem, self.off, self.per)
        self.base, self.off, self.var = self.base + self.per * rounds, 0, None

    def up(self, ins):
        ins.then_inc(self.sem, 1)
        self.off += 1

    def value(self):
        fixed = self.base + self.off
        return fixed if self.var is None else self.var * self.per + fixed

    def settle(self, eng, ins):
        self.up(ins)
        eng.wait_ge(self.sem, self.value())


class Core:
    pass


def make_core(nc, ctx):
    k = Core()
    k.nc = nc
    base = -(-nc.sbuf_base // 64) * 64
    k.top = 207 * 1024

    def at(name, kb, shape, dt=F32):
        size = 4 * int(np.prod(shape[1:]))
        assert kb * 1024 + size <= k.top, (name, kb, size)
        return nc.alloc_sbuf_tensor_at(name, shape, dt, offset=base + int(kb * 1024))[:]

    def sem(name):
        return ctx.enter_context(nc.semaphore(name))

    k.at, k.sem = at, sem
    k.raw = at("slab_raw", 0, [P, 2, KT, P])
    k.whi = at("slab_hi", 8, [P, 2, KT, P], F32R)
    k.wlo = at("slab_lo", 16, [P, 2, KT, P], F32R)
    k.const = at("const", 24, [P, N_CONST])
    k.par = at("params", 26.0625, [P, N_PARAMS])
    k.mod_all = at("mod", 27.5, [P, ADA_COLS // P + 48])
    k.mod = k.mod_all[:, ADA_COLS // P:]
    k.small = at("small", 27.75, [P, 128])
    k.H, k.Y, k.W = 30, 94, 158
    k.F = k.Y
    k.hhi = at("h_hi", k.H, [P, KT, T], F32R)
    k.hlo = at("h_lo", k.H + 32, [P, KT, T], F32R)
    k.bank = [ctx.enter_context(nc.psum_tensor(f"proj_bank{c}", [P, HALF], F32)) for c in range(2)]
    k.aux = ctx.enter_context(nc.psum_tensor("aux_banks", [P, 6, HALF], F32))
    k.ident = k.const[:, IDENT:IDENT + P]
    k.causal = k.const[:, CAUSAL:CAUSAL + P]
    k.tri = k.const[:, TRI:TRI + P]
    k.lastrow = k.const[:, LASTROW:LASTROW + P]
    k.inv_count = k.const[:, INV:N_CONST]
    k.ones = k.small[:, 0:1]
    k.cn, k.ncn = k.small[:, 1:9], k.small[:, 9:17]
    k.cond, k.lam, k.subg = k.small[:, 17:25], k.small[:, 25:26], k.small[:, 26:27]
    k.stat, k.rstd = k.small[:, 27:35], k.small[:, 35:43]
    k.s_raw = [sem("raw_loaded_0"), sem("raw_loaded_1")]
    k.s_hi = sem("slab_hi_made")
    k.s_begun = sem("slab_begun")
    k.s_split = sem("slab_split")
    k.s_proj = sem("chunk_projected")
    k.s_stage = sem("stage_ended")
    k.s_vstep = sem("dve_step")
    k.s_astep = sem("act_step")
    k.vstep, k.astep = Count(k.s_vstep), Count(k.s_astep)
    k.s_sum, k.s_var, k.s_col, k.s_spread = sem("norm_summed"), sem("norm_var"), sem("norm_rstd"), sem("norm_spread")
    k.s_normed, k.s_high, k.s_low = sem("normed"), sem("normed_high"), sem("normed_low")
    k.s_gates, k.s_mixed = sem("branch_gates"), sem("branch_mixed")
    k.s_x = [sem(f"x_loaded_{i}") for i in range(KT // X_TILES)]
    k.norms, k.splits, k.branches = 0, 0, 0
    k.stage = 0
    return k


def param(k, name, i=0, n=1):
    a, _ = PARAM_COLS[name]
    return k.par[:, a + i:a + i + n]


def param_dyn(k, name, i, step=1):
    a, _ = PARAM_COLS[name]
    return k.par[:, ds(i * step + a, 1)]


def begin(k, eng):
    if k.stage:
        eng.wait_ge(k.s_stage, 3 * k.stage)


def end(k, eng):
    eng.drain().then_inc(k.s_stage, 1)


def project(k, pe, slab, slot, chunk, bank, hi, lo, ks=range(KT), first=True, last=True, counts=True):
    if chunk == 0:
        pe.wait_ge(k.s_split, slab + 1)
    cols = slice(chunk * HALF, (chunk + 1) * HALF)
    ks = list(ks)
    for a, (wk, xk) in enumerate((i, i) if isinstance(i, int) else i for i in ks):
        pe.matmul(bank, k.whi[:, slot, wk, :], hi[:, xk, cols], start=first and a == 0, stop=False)
        pe.matmul(bank, k.whi[:, slot, wk, :], lo[:, xk, cols], start=False, stop=False)
        mm = pe.matmul(bank, k.wlo[:, slot, wk, :], hi[:, xk, cols], start=False, stop=last and a == len(ks) - 1)
    if counts:
        mm.then_inc(k.s_proj, 1)


def weight_split(k, block):
    nc = k.nc

    @block.gpsimd
    def _(pool):
        def one(slab, slot, round_, reuse):
            pool.wait_ge(k.s_raw[slot], (round_ + 1) * 16)
            if reuse:
                pool.wait_ge(k.s_proj, slab * 2 - 2)
            pool.sem_inc(k.s_begun, 1)
            pool.tensor_copy(k.whi[:, slot], k.raw[:, slot]).then_inc(k.s_hi, 1)
            pool.wait_ge(k.s_hi, slab + 1)
            pool.tensor_tensor(k.wlo[:, slot], k.raw[:, slot], k.whi[:, slot].bitcast(F32), ALU.subtract).then_inc(k.s_split, 1)

        one(0, 0, 0, False)
        one(1, 1, 0, False)
        with pool.Fori(1, N_SLABS // 2) as i:
            for s in range(2):
                one(i * 2 + s, s, i, True)
        if N_SLABS % 2:
            one(N_SLABS - 1, 0, N_SLABS // 2, True)


def load_slab(k, sp, wts, slab, slot, reuse):
    if reuse:
        sp.wait_ge(k.s_split, slab - 1)
    src = wts[slab] if isinstance(slab, int) else wts[ds(slab, 1)].rearrange("a p k m -> (a p) k m")
    sp.dma_start(k.raw[:, slot], src).then_inc(k.s_raw[slot], 16)




def softplus_dve(k, dve, act_exp_done, out, e, relu, s, s2, p):
    v = k.vstep
    dve.wait_ge(*act_exp_done)
    v.settle(dve, dve.tensor_scalar(s, e, 2.0, None, ALU.add))
    v.settle(dve, dve.reciprocal(s2, s))
    v.settle(dve, dve.tensor_tensor(s, e, s2, ALU.mult))
    v.settle(dve, dve.tensor_tensor(s2, s, s, ALU.mult))
    v.settle(dve, dve.tensor_scalar(p, s2, 2.0 / 19.0, None, ALU.mult))
    for n in range(17, 1, -2):
        v.settle(dve, dve.scalar_tensor_tensor(p, p, 2.0 / n, s2, ALU.add, ALU.mult))
    v.settle(dve, dve.scalar_tensor_tensor(p, p, 2.0, s, ALU.add, ALU.mult))
    v.settle(dve, dve.tensor_tensor(out, p, relu, ALU.add))


def rstd_stage(k, block, ssum, feats, bank0):
    n = k.norms
    k.norms += 1

    @block.tensor
    def _(pe):
        begin(k, pe)
        for j in range(TT):
            mm = pe.matmul(k.aux[:, bank0 + 1, j:j + 1], ssum[:, j * P:(j + 1) * P], k.ones, start=True, stop=True)
        mm.then_inc(k.s_sum, 1)
        pe.wait_ge(k.s_col, n + 1)
        for j in range(TT):
            mm = pe.matmul(k.aux[:, bank0 + j // 4, (j % 4) * P:(j % 4 + 1) * P],
                           k.rstd[:, j:j + 1].to_broadcast([P, P]), k.ident, start=True, stop=True)
        mm.then_inc(k.s_spread, 1)

    @block.vector
    def _(dve):
        begin(k, dve)
        dve.wait_ge(k.s_sum, n + 1)
        dve.tensor_scalar(k.stat, k.aux[:, bank0 + 1, 0:TT], 1.0 / feats, EPS, ALU.mult, ALU.add).then_inc(k.s_var, 1)
        dve.wait_ge(k.s_var, 2 * n + 2)
        dve.reciprocal(k.rstd, k.stat).then_inc(k.s_col, 1)

    @block.scalar
    def _(act):
        begin(k, act)
        act.wait_ge(k.s_var, 2 * n + 1)
        act.activation(k.stat, k.stat, ACT.Sqrt).then_inc(k.s_var, 1)

    return n + 1, k.aux[:, bank0:bank0 + 2, :].rearrange("p a b -> p (a b)")


def square_sum_stage(k, name, block, src, sq, ssum, loaded=None):
    s_sq, s_free = k.sem(f"{name}_squared"), k.sem(f"{name}_square_used")

    @block.scalar
    def _(act):
        begin(k, act)
        for t in range(KT):
            if loaded is not None:
                act.wait_ge(loaded[t // X_TILES], 16)
            if t >= 2:
                act.wait_ge(s_free, t - 1)
            act.activation(ssum if t == 0 else sq[:, t % 2], src(t), ACT.Square).then_inc(s_sq, 1)
        end(k, act)

    @block.vector
    def _(dve):
        begin(k, dve)
        dve.wait_ge(s_sq, 1)
        for t in range(1, KT):
            dve.wait_ge(s_sq, t + 1)
            ins = dve.tensor_tensor(ssum, ssum, sq[:, t % 2], ALU.add)
            ins.then_inc(s_free, 2 if t == 1 else 1)
            dve.wait_ge(s_free, t + 1)
        end(k, dve)

    @block.tensor
    def _(pe):
        begin(k, pe)
        end(k, pe)

    k.stage += 1


def norm_split_stage(k, block, src, ssum, gain, shift, tmp):
    spread, rb = rstd_stage(k, block, ssum, D, 0)
    done = k.splits * KT
    k.splits += 1

    @block.tensor
    def _(pe):
        end(k, pe)

    @block.vector
    def _(dve):
        dve.wait_ge(k.s_spread, spread)

        def low(t):
            dve.wait_ge(k.s_high, done + t + 1)
            hi = k.hhi[:, t, :].bitcast(F32)
            if shift is None:
                ins = dve.tensor_tensor(k.hlo[:, t, :], tmp[:, t % 2], hi, ALU.subtract)
            else:
                ins = dve.scalar_tensor_tensor(k.hlo[:, t, :], tmp[:, t % 2], shift(t), hi, ALU.add, ALU.subtract)
            ins.then_inc(k.s_low, 1)

        for t in range(KT):
            if t >= 2:
                dve.wait_ge(k.s_low, done + t - 1)
            dve.scalar_tensor_tensor(tmp[:, t % 2], src(t), gain(t), rb, ALU.mult, ALU.mult).then_inc(k.s_normed, 1)
            if t >= 1:
                low(t - 1)
        low(KT - 1)
        end(k, dve)

    @block.scalar
    def _(act):
        for t in range(KT):
            act.wait_ge(k.s_normed, done + t + 1)
            if shift is None:
                ins = act.activation(k.hhi[:, t, :], tmp[:, t % 2], ACT.Copy)
            else:
                ins = act.activation(k.hhi[:, t, :], tmp[:, t % 2], ACT.Identity, bias=shift(t))
            ins.then_inc(k.s_high, 1)
        end(k, act)

    k.stage += 1




def setup_stage(k, block, xT, params, consts, wts):
    k.xt = k.at("x_first", k.W, [P, KT, T])
    s_par, s_e, s_l, s_p = k.sem("params_loaded"), k.sem("setup_exp"), k.sem("lambda_summed"), k.sem("setup_products")
    t = k.at("setup_tmp", k.Y, [P, 8, 8])
    one64 = k.at("ones_square", k.Y + 1, [P, P])
    x, ab, e, relu, s, s2, p = (t[:, i] for i in range(7))
    lamt = t[:, 7]

    @block.sync
    def _(sp):
        for i in range(KT // X_TILES):
            sp.dma_start(k.xt[:, i * X_TILES:(i + 1) * X_TILES], xT[i * X_TILES:(i + 1) * X_TILES].rearrange("k p t -> p k t")).then_inc(k.s_x[i], 16)
        load_slab(k, sp, wts, 0, 0, False)
        load_slab(k, sp, wts, 1, 1, False)

    @block.scalar
    def _(act):
        act.dma_start(k.par[:], params).then_inc(s_par, 16)
        act.dma_start(k.const[:], consts).then_inc(s_par, 16)
        act.wait_ge(s_par, 32)
        act.activation(k.cond, param(k, "c", 0, 8), ACT.Silu).then_inc(s_e, 1)
        act.activation(ab, param(k, "lru_lam", 0, 8), ACT.Abs).then_inc(s_e, 1)
        act.wait_ge(s_e, 2)
        act.activation(e, ab, ACT.Exp, scale=-1.0).then_inc(s_e, 1)
        act.wait_ge(s_l, 1)
        act.activation(lamt[:, 0:2], k.aux[:, 0, 0:2], ACT.Exp).then_inc(s_e, 1)

    @block.tensor
    def _(pe):
        pe.wait_ge(s_p, 3)
        pe.matmul(k.aux[:, 0, 0:2], one64[0:QK, :], lamt[0:QK, 2:4], start=True, stop=True).then_inc(s_l, 1)

    @block.vector
    def _(dve):
        dve.memset(k.ones, 1.0).then_inc(s_p, 1)
        dve.memset(one64[:], 1.0).then_inc(s_p, 1)
        dve.wait_ge(s_par, 32)
        dve.tensor_tensor(lamt[0:QK, 2:4], param(k, "lq", 0, 2)[0:QK], param(k, "lk", 0, 2)[0:QK], ALU.mult).then_inc(s_p, 1)
        dve.tensor_scalar(relu, param(k, "lru_lam", 0, 8), -1.0, 0.0, ALU.mult, ALU.max).then_inc(s_p, 1)
        dve.tensor_scalar(k.subg, param(k, "subln_g"), 1.0 - LAM_INIT, None, ALU.mult).then_inc(s_p, 1)
        dve.wait_ge(s_p, 5)
        softplus_dve(k, dve, (s_e, 3), x, e, relu, s, s2, p)
        dve.tensor_scalar(k.cn, x, -8.0, None, ALU.mult).then_inc(s_p, 1)
        dve.tensor_scalar(k.ncn, x, 8.0, None, ALU.mult).then_inc(s_p, 1)
        dve.wait_ge(s_e, 4)
        dve.tensor_scalar(lamt[:, 4:5], lamt[:, 1:2], -1.0, LAM_INIT, ALU.mult, ALU.add).then_inc(s_p, 1)
        dve.wait_ge(s_p, 8)
        dve.tensor_tensor(k.lam, lamt[:, 4:5], lamt[:, 0:1], ALU.add).then_inc(s_p, 1)




def lru_stage(k, block, wts, gate_w, ada_w):
    xpad = k.at("lru_x", k.W, [P, T + 8])
    xc, r, g, a, u = (k.at(n, k.W + 4.25 + 4 * i, [P, T]) for i, n in enumerate(("lru_conv", "lru_r", "lru_i", "lru_a", "lru_u")))
    gw_all = k.at("gate_w_all", k.W + 24.25, [P, LRU_BLOCKS, 2, P])
    gw = k.at("gate_w", k.W + 32.25, [P, 2, P])
    adaw = k.at("ada_w", k.W + 33.25, [P, 2, ADA_COLS])
    acc = k.at("ada_acc", k.W + 39.25, [P, ADA_COLS])
    k.y = k.at("y", k.Y, [P, 2 * KT, T])
    s_gw, s_ada, s_ada_used = k.sem("gate_w_loaded"), [k.sem(f"ada_loaded_{i}") for i in range(2)], k.sem("ada_used")
    s_evac, s_conv, s_gates, s_sig = k.sem("lru_evacuated"), k.sem("lru_conv_made"), k.sem("lru_gates"), k.sem("lru_sigmoids")
    s_au, s_m2, s_mult, s_col, s_y = k.sem("lru_a_made"), k.sem("lru_m2"), k.sem("lru_root"), k.sem("ada_columns"), k.sem("lru_y_made")
    v = k.vstep
    EV, AD = 2, 6

    @block.sync
    def _(sp):
        with sp.Fori(0, LRU_BLOCKS) as n:
            for kt in range(KT):
                sp.wait_ge(s_ada_used, n * KT + (kt + 2))
                sp.dma_start(adaw[:, kt % 2], ada_w[ds(n, 1), kt].rearrange("a p m -> (a p) m")).then_inc(s_ada[kt % 2], 16)
            for s in range(2):
                load_slab(k, sp, wts, n * 2 + (2 + s), s, True)

    @block.tensor
    def _(pe):
        begin(k, pe)

        def columns(n):
            pe.wait_ge(s_ada_used, n * KT + 3)
            pe.wait_ge(s_col, n * 2 + 1)
            for j in range(AD):
                mm = pe.matmul(k.aux[:, 4, j:j + 1], acc[:, j * P:(j + 1) * P], k.ones, start=True, stop=True)
            mm.then_inc(s_col, 1)

        with pe.Fori(0, LRU_BLOCKS) as n:
            for s in range(2):
                for c in range(2):
                    pe.wait_ge(s_evac, n * 4 + (2 * s + c + 1))
                    project(k, pe, n * 2 + (LRU_0 + s), s, c, k.bank[c][:], k.hhi, k.hlo)
                if s == 0:
                    columns(n)
            pe.wait_ge(s_conv, n + 2)
            pe.wait_ge(s_sig, n + 1)
            for i in range(2):
                for c in range(2):
                    mm = pe.matmul(k.aux[:, 2 * i + c, :], gw[:, i, :], xc[:, c * HALF:(c + 1) * HALF], start=True, stop=True)
            mm.then_inc(s_gates, 1)
        columns(LRU_BLOCKS)
        end(k, pe)

    @block.scalar
    def _(act):
        begin(k, act)
        act.dma_start(gw_all[:], gate_w).then_inc(s_gw, 16)
        act.sem_inc(s_evac, EV)
        act.sem_inc(s_sig, 1)
        flat = k.aux[:].rearrange("p a b -> p (a b)")

        def x_in(n):
            act.wait_ge(s_conv, n + 1)
            for c in range(2):
                act.wait_ge(k.s_proj, n * 4 + (2 * LRU_0 + c + 1))
                act.activation(xpad[:, 3 + c * HALF:3 + (c + 1) * HALF], k.bank[c][:], ACT.Copy).then_inc(s_evac, 1)

        def rest(n, last):
            for c in range(2):
                act.wait_ge(k.s_proj, n * 4 + (2 * LRU_0 + 3 + c))
                act.activation(k.y[:, ds(n + KT, 1), c * HALF:(c + 1) * HALF].rearrange("p a b -> p (a b)"),
                               k.bank[c][:], ACT.Silu).then_inc(s_evac, 1)
            act.wait_ge(s_gates, n + 1)
            act.wait_ge(s_y, n + 1)
            act.activation(r[:], flat[:, 0:T], ACT.Sigmoid, bias=param_dyn(k, "b_r", n))
            act.activation(g[:], flat[:, T:2 * T], ACT.Sigmoid, bias=param_dyn(k, "b_i", n)).then_inc(s_sig, 1)
            act.wait_ge(s_sig, n + 2)
            act.activation(a[:], r[:], ACT.Exp, scale=k.cn[:, ds(n, 1)])
            act.activation(u[:], r[:], ACT.Tanh, scale=k.ncn[:, ds(n, 1)]).then_inc(s_au, 1)
            if not last:
                x_in(n + 1)
            act.wait_ge(s_m2, n + 1)
            act.activation(r[:], u[:], ACT.Sqrt).then_inc(s_mult, 1)

        x_in(0)
        with act.Fori(0, LRU_BLOCKS - 1) as n:
            rest(n, False)
        rest(LRU_BLOCKS - 1, True)
        end(k, act)

    @block.vector
    def _(dve):
        begin(k, dve)
        dve.sem_inc(s_ada_used, 2)
        dve.memset(acc[:], 0.0).then_inc(s_ada_used, 1)
        dve.sem_inc(s_conv, 1)
        dve.sem_inc(s_y, 1)
        dve.sem_inc(s_col, 1)
        v.settle(dve, dve.memset(xpad[:, 0:3], 0.0))
        dve.wait_ge(s_gw, 16)

        def columns(n):
            dve.wait_ge(s_col, n * 2 + 2)
            b0, _ = PARAM_COLS["b_ada"]
            ins = dve.tensor_tensor(k.mod_all[:, ds(n * AD, AD)], k.aux[:, 4, 0:AD], k.par[:, ds(n * AD + (b0 - AD), AD)], ALU.add)
            ins.then_inc(s_col, 1)

        with dve.Fori(0, LRU_BLOCKS) as n:
            v.enter(n, 7)
            dve.wait_ge(s_evac, n * 4 + (EV + 2))
            dve.tensor_copy(gw[:], gw_all[:, ds(n, 1)].rearrange("p a i d -> p (a i) d"))
            v.settle(dve, dve.tensor_scalar(xc[:], xpad[:, 0:T], param_dyn(k, "conv1_w", n, TAPS), param_dyn(k, "conv1_b", n), ALU.mult, ALU.add))
            for tap in range(1, TAPS):
                a0, _ = PARAM_COLS["conv1_w"]
                ins = dve.scalar_tensor_tensor(xc[:], xpad[:, tap:tap + T], k.par[:, ds(n * TAPS + (a0 + tap), 1)], xc[:], ALU.mult, ALU.add)
                if tap < TAPS - 1:
                    v.settle(dve, ins)
            ins.then_inc(s_conv, 1)
            columns(n)
            for kt in range(KT):
                dve.wait_ge(s_ada[kt % 2], n * 64 + 16 * (kt // 2 + 1))
                if kt == 0:
                    ins = dve.tensor_scalar(acc[:], adaw[:, 0], k.cond[:, 0:1], None, ALU.mult)
                else:
                    ins = dve.scalar_tensor_tensor(acc[:], adaw[:, kt % 2], k.cond[:, kt:kt + 1], acc[:], ALU.mult, ALU.add)
                ins.then_inc(s_ada_used, 1)
                dve.wait_ge(s_ada_used, n * KT + (kt + 4))
            dve.wait_ge(s_au, n + 1)
            v.settle(dve, dve.tensor_tensor(r[:], a[:], a[:], ALU.mult))
            ins = dve.scalar_tensor_tensor(u[:], r[:], 1.0, u[:], ALU.add, ALU.mult)
            ins.then_inc(s_m2, 1)
            v.settle(dve, dve.tensor_tensor(g[:], g[:], xc[:], ALU.mult))
            dve.wait_ge(s_mult, n + 1)
            ins = dve.tensor_tensor(g[:], g[:], r[:], ALU.mult)
            v.settle(dve, ins)
            v.settle(dve, dve.tensor_tensor_scan(u[:], a[:], g[:], 0.0, ALU.mult, ALU.add))
            dve.wait_ge(s_evac, n * 4 + (EV + 4))
            yt = k.y[:, ds(n + KT, 1), :].rearrange("p a b -> p (a b)")
            dve.tensor_tensor(yt, u[:], yt, ALU.mult).then_inc(s_y, 1)
        v.leave(LRU_BLOCKS)
        columns(LRU_BLOCKS)
        end(k, dve)

    k.stage += 1




def attention_stage(k, block):
    qt = k.at("att_q", k.W, [P, 2, T])
    kt = k.at("att_k", k.W + 8, [P, 2, T])
    vtok = k.at("att_v", k.W + 16, [P, 2, TT, P])
    vt = k.at("att_v_features", k.W + 24, [P, T])
    p = k.at("att_p", k.W + 28, [P, 2, T])
    wt = k.at("att_w_turned", k.W + 36, [P, TT, P])
    o = k.at("att_o", k.W + 40, [P, T])
    sq = k.at("att_o_squared", k.W + 44, [P, T])
    nmax, total, inv, lr = (k.small[:, 48 + 4 * i:50 + 4 * i] for i in range(4))
    mx = k.small[:, 64:66]
    score, turn, out = k.aux[:, 0:4, :], k.aux[:, 4, :], k.aux[:, 5, :]
    s_evac = k.sem("att_evacuated")
    s_score = k.sem("att_scored")
    s_nmax = k.sem("att_max")
    s_exp = k.sem("att_exp")
    s_w = k.sem("att_w")
    s_turned, s_turn_free = k.sem("att_turned"), k.sem("att_turn_read")
    s_out, s_out_free = k.sem("att_out"), k.sem("att_out_read")
    s_sq, s_root = k.sem("att_squared"), k.sem("att_root")
    s_var, s_col = k.sem("att_var"), k.sem("att_rstd")
    s_y = k.sem("att_y")
    SCALE = QK ** -0.5
    GROUPS = [-(-(i + 1) // 4) for i in range(TT)]
    FIRST, EACH = 2, sum(GROUPS) + 5

    def uses(h):
        return FIRST if isinstance(h, int) and h == 0 else h * EACH + (FIRST - 3)

    class Turns:

        def __init__(self, h):
            self.start, self.n = uses(h), 0

        def next(self):
            self.n += 1
            return self.start + self.n

        def done(self):
            return self.start + self.n

    def heads(eng, one):
        one(0, 0, False, True)
        with eng.Fori(0, (HEADS - 2) // 2) as m:
            for b in range(2):
                one(m * 2 + (1 + b), 1 - b, True, True)
        one(HEADS - 1, 1, True, False)

    @block.tensor
    def _(pe):
        begin(k, pe)

        def half(h, i):
            use = h * 8 + i
            pe.wait_ge(s_evac, use + 1)
            project(k, pe, h * 4 + (ATT_0 + i // 2), (i // 2) % 2, i % 2, k.bank[i % 2][:], k.hhi, k.hlo)

        def scores(h, par, i, step):
            if i == 0:
                pe.wait_ge(s_evac, h * 8 + (2 + 4))
            pe.wait_ge(s_exp, step * 2 + 2)
            keys = (i + 1) * P
            for c in range(2):
                rows = slice(c * QK, (c + 1) * QK)
                q = qt[rows, par, i * P:(i + 1) * P]
                for a in range(0, i * P, HALF):
                    n = min(HALF, i * P - a)
                    pe.matmul(score[:, 2 * c + a // HALF, 0:n], q, kt[rows, par, a:a + n], start=True, stop=True)
                a = (i * P) % HALF
                own = score[:, 2 * c + i * P // HALF, a:a + P]
                pe.matmul(own, q, kt[rows, par, i * P:keys], start=True, stop=False)
                mm = pe.matmul(own, k.ident, k.causal, start=False, stop=True)
                mm.then_inc(s_score, 1)

        def turn_group(turns, ins):
            pe.wait_ge(s_turn_free, turns.next())
            for a, x in enumerate(ins):
                mm = pe.transpose(turn[:, a * P:(a + 1) * P], x, k.ident)
            mm.then_inc(s_turned, 1)

        def values(turns, h, par):
            pe.wait_ge(s_evac, h * 8 + (2 + 6))
            for a in range(2):
                turn_group(turns, [vt[:, j * P:(j + 1) * P] for j in range(4 * a, 4 * a + 4)])

        def statistics(turns, h):
            pe.wait_ge(s_sq, h + 1)
            pe.wait_ge(s_turn_free, turns.next())
            for j in range(TT):
                mm = pe.matmul(turn[:, j:j + 1], sq[:, j * P:(j + 1) * P], k.ones, start=True, stop=True)
            mm.then_inc(s_turned, 1)

        def spread(turns, h):
            pe.wait_ge(s_col, h + 1)
            for a in range(2):
                pe.wait_ge(s_turn_free, turns.next())
                for j in range(4):
                    mm = pe.matmul(turn[:, j * P:(j + 1) * P], k.rstd[:, 4 * a + j:4 * a + j + 1].to_broadcast([P, P]),
                                   k.ident, start=True, stop=True)
                mm.then_inc(s_turned, 1)

        def one(h, par, after, more):
            turns = Turns(h)
            for i in range(TT):
                pe.wait_ge(s_w, h * TT + (i + 1))
                for a in range(0, i + 1, 4):
                    turn_group(turns, [p[:, 0, j * P:(j + 1) * P] for j in range(a, min(a + 4, i + 1))])
                if i < TT - 1:
                    scores(h, par, i + 1, h * TT + (i + 1))
                elif more:
                    scores(h + 1, 1 - par, 0, h * TT + TT)
                if i % 4 == 0:
                    pe.wait_ge(s_out_free, h * 2 + (i // 4 + 1))
                pe.wait_ge(s_turn_free, turns.done() + 1)
                for j in range(i + 1):
                    mm = pe.matmul(out[:, (i % 4) * P:(i % 4 + 1) * P], vtok[:, par, j, :], wt[:, j, :], start=j == 0, stop=j == i)
                if i % 4 == 3:
                    mm.then_inc(s_out, 1)
                if more:
                    half(h + 1, i)
                if after and i == 0:
                    statistics(turns, h - 1)
                if after and i == 2:
                    spread(turns, h - 1)
                if more and i == 6:
                    values(turns, h + 1, 1 - par)

        for i in range(8):
            half(0, i)
        first = Turns(0)
        first.start = 0
        values(first, 0, 0)
        scores(0, 0, 0, 0)
        heads(pe, one)
        last = Turns(HEADS)
        last.start = uses(HEADS) - 2
        statistics(last, HEADS - 1)
        spread(last, HEADS - 1)
        end(k, pe)

    @block.scalar
    def _(act):
        begin(k, act)
        act.sem_inc(s_evac, 2)
        act.sem_inc(s_exp, 2)
        act.sem_inc(s_out_free, 1)

        def half(h, par, i):
            act.wait_ge(k.s_proj, h * 8 + (2 * ATT_0 + i + 1))
            cols = slice((i % 2) * HALF, (i % 2 + 1) * HALF)
            bank = k.bank[i % 2][:]
            if i // 2 == 3:
                ins = act.activation(k.y[:, ds(h, 1), cols].rearrange("p a b -> p (a b)"), bank, ACT.Silu)
            else:
                ins = act.activation((qt[:, par, cols], kt[:, par, cols], vt[:, cols])[i // 2], bank, ACT.Copy)
            ins.then_inc(s_evac, 1)

        def softmax(step, i, used):
            keys = (i + 1) * P
            act.wait_ge(s_nmax, step + 1)
            act.wait_ge(s_turned, used)
            flat = score.rearrange("p (c a) b -> p c (a b)", c=2)
            for c in range(2):
                act.activation(p[:, c, 0:keys], flat[:, c, 0:keys], ACT.Exp, bias=nmax[:, c:c + 1], scale=SCALE,
                               accum_out=total[:, c:c + 1]).then_inc(s_exp, 1)

        def square(h):
            act.wait_ge(s_out_free, h * 2 + 3)
            act.activation(sq[:], o[:], ACT.Square).then_inc(s_sq, 1)

        def root(h):
            act.wait_ge(s_var, h + 1)
            act.activation(k.stat, k.stat, ACT.Sqrt).then_inc(s_root, 1)

        def one(h, par, after, more):
            used = uses(h)
            for i in range(TT):
                used = used + GROUPS[i]
                if i < TT - 1:
                    softmax(h * TT + (i + 1), i + 1, used)
                elif more:
                    softmax(h * TT + TT, 0, used)
                if i % 4 == 3:
                    act.wait_ge(s_out, h * 2 + (i // 4 + 1))
                    if i == 3:
                        act.wait_ge(s_y, h + 1)
                    act.activation(o[:, (i // 4) * HALF:(i // 4 + 1) * HALF], out, ACT.Copy).then_inc(s_out_free, 1)
                if more:
                    half(h + 1, 1 - par, i)
                if after and i == 0:
                    root(h - 1)
                    used = used + 1
                if after and i == 2:
                    used = used + 2
                if more and i == 6:
                    used = used + 2
            square(h)

        for i in range(8):
            half(0, 0, i)
        softmax(0, 0, 2)
        heads(act, one)
        root(HEADS - 1)
        end(k, act)

    @block.vector
    def _(dve):
        begin(k, dve)
        dve.sem_inc(s_turn_free, 1)
        dve.sem_inc(s_y, 1)
        v = k.vstep

        def maxima(step, i):
            keys = (i + 1) * P
            flat = score.rearrange("p (c a) b -> p c (a b)", c=2)
            for c in range(2):
                dve.wait_ge(s_score, step * 2 + (c + 1))
                ins = dve.tensor_reduce(mx[:, c:c + 1], flat[:, c, 0:keys], AX, ALU.max)
            v.settle(dve, ins)
            dve.tensor_scalar(nmax, mx, -SCALE, None, ALU.mult).then_inc(s_nmax, 1)

        def weights(step, i):
            keys = (i + 1) * P
            dve.wait_ge(s_exp, step * 2 + 4)
            v.settle(dve, dve.reciprocal(inv, total))
            v.settle(dve, dve.tensor_scalar(lr[:, 0:1], inv[:, 1:2], k.lam, None, ALU.mult))
            v.settle(dve, dve.tensor_scalar(p[:, 1, 0:keys], p[:, 1, 0:keys], lr[:, 0:1], None, ALU.mult))
            dve.scalar_tensor_tensor(p[:, 0, 0:keys], p[:, 0, 0:keys], inv[:, 0:1], p[:, 1, 0:keys], ALU.mult, ALU.subtract).then_inc(s_w, 1)

        def turned(turns):
            dve.wait_ge(s_turned, turns.next())

        def values(turns, par):
            for a in range(2):
                turned(turns)
                dve.tensor_copy(vtok[:, par, 4 * a:4 * a + 4, :].rearrange("p a b -> p (a b)"), turn).then_inc(s_turn_free, 1)

        def statistics(turns, h):
            turned(turns)
            dve.tensor_scalar(k.stat, turn[:, 0:TT], 1.0 / P, EPS, ALU.mult, ALU.add).then_inc(s_turn_free, 1)
            dve.wait_ge(s_turn_free, turns.done() + 1)
            dve.sem_inc(s_var, 1)
            dve.wait_ge(s_root, h + 1)
            dve.reciprocal(k.rstd, k.stat).then_inc(s_col, 1)

        def spread(turns, h):
            yt = k.y[:, ds(h, 1), :].rearrange("p a b -> p (a b)")
            for a in range(2):
                cols = slice(a * HALF, (a + 1) * HALF)
                turned(turns)
                ins = dve.scalar_tensor_tensor(o[:, cols], o[:, cols], k.subg, turn, ALU.mult, ALU.mult)
                ins.then_inc(s_turn_free, 1)
            dve.wait_ge(s_turn_free, turns.done() + 1)
            dve.tensor_tensor(yt, yt, o[:], ALU.mult).then_inc(s_y, 1)

        def one(h, par, after, more):
            turns = Turns(h)
            for i in range(TT):
                for a in range(0, i + 1, 4):
                    n = min(4, i + 1 - a)
                    turned(turns)
                    dve.tensor_copy(wt[:, a:a + n, :].rearrange("p a b -> p (a b)"), turn[:, 0:n * P]).then_inc(s_turn_free, 1)
                if i < TT - 1:
                    maxima(h * TT + (i + 1), i + 1)
                    weights(h * TT + (i + 1), i + 1)
                elif more:
                    maxima(h * TT + TT, 0)
                    weights(h * TT + TT, 0)
                if after and i == 0:
                    statistics(turns, h - 1)
                if after and i == 2:
                    spread(turns, h - 1)
                if more and i == 6:
                    values(turns, 1 - par)

        first = Turns(0)
        first.start = 0
        values(first, 0)
        maxima(0, 0)
        weights(0, 0)
        one(0, 0, False, True)
        with dve.Fori(0, (HEADS - 2) // 2) as m:
            v.enter(m, 2 * TT * 4)
            for b in range(2):
                one(m * 2 + (1 + b), 1 - b, True, True)
        v.leave((HEADS - 2) // 2)
        one(HEADS - 1, 1, True, False)
        last = Turns(HEADS)
        last.start = uses(HEADS) - 2
        statistics(last, HEADS - 1)
        spread(last, HEADS - 1)
        end(k, dve)

    k.stage += 1




def out_project_stage(k, block):
    k.yhi = k.at("y_hi", k.H, [P, 2 * KT, T], F32R)
    k.ylo = k.at("y_lo", k.Y, [P, 2 * KT, T], F32R)
    k.o1 = k.at("out1", k.W, [P, KT, T])
    sq = k.at("out1_squared", k.W + 32, [P, T])
    k.ssum = k.at("out1_sum", k.W + 36, [P, T])
    s_hi, s_lo = k.sem("y_high"), k.sem("y_low")
    s_evac, s_added = k.sem("out1_evacuated"), k.sem("out1_added")

    @block.tensor
    def _(pe):
        begin(k, pe)
        with pe.Fori(0, KT) as f:
            for s in range(2):
                pe.wait_ge(s_lo, KT * (s + 1))
                for c in range(2):
                    if s == 0:
                        pe.wait_ge(s_evac, f * 2 + (c + 1))
                    project(k, pe, f * 2 + (OUT1_0 + s), s, c, k.bank[c][:], k.yhi, k.ylo,
                            [(i, i + KT * s) for i in range(KT)], s == 0, s == 1)
        end(k, pe)

    @block.scalar
    def _(act):
        begin(k, act)
        act.sem_inc(s_evac, 2)
        for t in range(2 * KT):
            act.activation(k.yhi[:, t, :], k.y[:, t, :], ACT.Copy).then_inc(s_hi, 1)
        with act.Fori(0, KT) as f:
            act.wait_ge(s_added, f + 1)
            for c in range(2):
                cols = slice(c * HALF, (c + 1) * HALF)
                act.wait_ge(k.s_proj, f * 4 + (2 * OUT1_0 + 3 + c))
                act.activation(sq[:, cols], k.bank[c][:], ACT.Square)
                act.activation(k.o1[:, ds(f, 1), cols].rearrange("p a b -> p (a b)"), k.bank[c][:], ACT.Copy).then_inc(s_evac, 1)
        end(k, act)

    @block.vector
    def _(dve):
        begin(k, dve)
        for t in range(2 * KT):
            dve.wait_ge(s_hi, t + 1)
            dve.tensor_tensor(k.ylo[:, t, :], k.y[:, t, :], k.yhi[:, t, :].bitcast(F32), ALU.subtract).then_inc(s_lo, 1)
        dve.memset(k.ssum, 0.0).then_inc(s_added, 1)
        with dve.Fori(0, KT) as f:
            dve.wait_ge(s_added, f + 1)
            dve.wait_ge(s_evac, f * 2 + 4)
            dve.tensor_tensor(k.ssum, k.ssum, sq, ALU.add).then_inc(s_added, 1)
        end(k, dve)

    k.stage += 1


def post_norm_stage(k, block, xT):
    spread, rb = rstd_stage(k, block, k.ssum, D, 0)
    xr = k.at("x_again", k.H, [P, KT, T])
    k.x1 = k.at("x1", k.Y, [P, KT, T])
    tmp = k.at("post_tmp", k.W + 40, [P, 2, T])
    sq = k.at("x1_squared", k.Y + 32, [P, 2, T])
    k.ssum1 = k.at("x1_sum", k.Y + 40, [P, T])
    s_t, s_x1, s_sq, s_add = k.sem("post_normed"), k.sem("x1_made"), k.sem("x1_squares"), k.sem("x1_added")

    @block.tensor
    def _(pe):
        end(k, pe)

    @block.scalar
    def _(act):
        for i in range(KT // X_TILES):
            act.dma_start(xr[:, i * X_TILES:(i + 1) * X_TILES], xT[i * X_TILES:(i + 1) * X_TILES].rearrange("k p t -> p k t")).then_inc(k.s_x[i], 16)
        for t in range(KT):
            act.wait_ge(s_x1, t + 1)
            if t >= 3:
                act.wait_ge(s_add, t - 2)
            act.activation(k.ssum1 if t == 0 else sq[:, t % 2], k.x1[:, t], ACT.Square).then_inc(s_sq, 1)
        end(k, act)

    @block.vector
    def _(dve):
        dve.wait_ge(k.s_spread, spread)

        def add(t):
            dve.wait_ge(s_sq, t + 1)
            if t >= 2:
                dve.wait_ge(s_add, t - 1)
            dve.tensor_tensor(k.ssum1, k.ssum1, sq[:, t % 2], ALU.add).then_inc(s_add, 1)

        for t in range(KT):
            dve.scalar_tensor_tensor(tmp[:, t % 2], k.o1[:, t, :], param(k, "post_g", t), rb, ALU.mult, ALU.mult).then_inc(s_t, 1)
            dve.wait_ge(s_t, t + 1)
            dve.wait_ge(k.s_x[t // X_TILES], 32)
            dve.tensor_tensor(k.x1[:, t], tmp[:, t % 2], xr[:, t], ALU.add).then_inc(s_x1, 1)
            if t >= 2:
                add(t - 1)
        add(KT - 1)
        end(k, dve)

    k.stage += 1


def rest_of_slabs(k, block, wts):

    @block.sync
    def _(sp):
        with sp.Fori(LRU_SLABS // 2 + 1, N_SLABS // 2) as i:
            for q in range(2):
                load_slab(k, sp, wts, i * 2 + q, q, True)
        if N_SLABS % 2:
            load_slab(k, sp, wts, N_SLABS - 1, 0, True)


def block2_gains(k, block):
    k.gain1, k.gain2 = k.small[:, 72:80], k.small[:, 80:88]
    s_gain = k.sem("gains_made")

    @block.vector
    def _(dve):
        dve.scalar_tensor_tensor(k.gain1, k.mod[:, 8:16], 1.0, param(k, "norm1", 0, 8), ALU.add, ALU.mult).then_inc(s_gain, 1)
        dve.scalar_tensor_tensor(k.gain2, k.mod[:, 32:40], 1.0, param(k, "norm2", 0, 8), ALU.add, ALU.mult).then_inc(s_gain, 1)
        dve.wait_ge(s_gain, 2)


def ssd_norm_stage(k, block):
    F = k.F
    k.shi = k.at("ssd_y_hi", F + 48, [P, KT, T], F32R)
    k.slo = k.at("ssd_y_lo", F + 80, [P, KT, T], F32R)
    tmp = k.at("ssd_normed", F, [P, 2, T])
    GT = KT // 2
    s_sum, s_var, s_root, s_col, s_b = (k.sem(f"ssd_norm_{n}") for n in ("summed", "var", "root", "rstd", "spread"))
    s_h, s_hi, s_lo = k.sem("ssd_normed"), k.sem("ssd_high"), k.sem("ssd_low")
    stat, rstd = k.small[:, 27:43], k.small[:, 100:116]

    @block.tensor
    def _(pe):
        begin(k, pe)
        for g in range(2):
            for j in range(TT):
                mm = pe.matmul(k.aux[:, 4, g * TT + j:g * TT + j + 1], k.gsum[:, g, j * P:(j + 1) * P], k.ones, start=True, stop=True)
        mm.then_inc(s_sum, 1)
        pe.wait_ge(s_col, 1)
        for g in range(2):
            for j in range(TT):
                mm = pe.matmul(k.aux[:, 2 * g + j // 4, (j % 4) * P:(j % 4 + 1) * P],
                               rstd[:, g * TT + j:g * TT + j + 1].to_broadcast([P, P]), k.ident, start=True, stop=True)
            mm.then_inc(s_b, 1)
        end(k, pe)

    @block.scalar
    def _(act):
        begin(k, act)
        act.wait_ge(s_var, 1)
        act.activation(stat, stat, ACT.Sqrt).then_inc(s_root, 1)
        for t in range(KT):
            act.wait_ge(s_h, t + 1)
            act.activation(k.shi[:, t], tmp[:, t % 2], ACT.Copy).then_inc(s_hi, 1)
        end(k, act)

    @block.vector
    def _(dve):
        begin(k, dve)
        dve.wait_ge(s_sum, 1)
        dve.tensor_scalar(stat, k.aux[:, 4, 0:2 * TT], 1.0 / (GT * P), EPS, ALU.mult, ALU.add).then_inc(s_var, 1)
        dve.wait_ge(s_root, 1)
        dve.reciprocal(rstd, stat).then_inc(s_col, 1)

        def low(t):
            dve.wait_ge(s_hi, t + 1)
            dve.tensor_tensor(k.slo[:, t], tmp[:, t % 2], k.shi[:, t].bitcast(F32), ALU.subtract).then_inc(s_lo, 1)

        for t in range(KT):
            if t % GT == 0:
                dve.wait_ge(s_b, t // GT + 1)
            if t >= 2:
                dve.wait_ge(s_lo, t - 1)
            rb = k.aux[:, 2 * (t // GT):2 * (t // GT) + 2, :].rearrange("p a b -> p (a b)")
            dve.scalar_tensor_tensor(tmp[:, t % 2], k.cv[:, 4 + t], param(k, "ssd_norm", t), rb, ALU.mult, ALU.mult).then_inc(s_h, 1)
            if t >= 1:
                low(t - 1)
        low(KT - 1)
        end(k, dve)

    k.stage += 1




def ssd_inputs_stage(k, block):
    F = k.F
    k.cv = k.at("ssd_conv_out", F, [P, CV_TILES, T])
    xpad = k.at("ssd_x", F + 48, [P, 2, T + 8])
    cx = k.at("ssd_conv", F + 57, [P, 2, T])
    x, e, relu, s, s2, p, dtr, acr = (k.at(n, F + 66 + 4 * i, [SSD_HEADS, T]) for i, n in enumerate(
        ("dt_x", "dt_exp", "dt_relu", "dt_s", "dt_s2", "dt_poly", "dt_rows", "decay_rows")))
    reset = k.at("chunk_reset", F + 98, [SSD_HEADS, T])
    a_neg = k.small[0:SSD_HEADS, 96:97]
    k.dtc, k.acol, k.dlast = (k.at(n, 28.25 + 0.5 * i, [P, CHUNKS, SSD_HEADS]) for i, n in enumerate(("dt_cols", "decay_cols", "to_chunk_end")))
    k.cdec, k.eac = (k.at(n, F + 112 + 0.5 * i, [P, CHUNKS, SSD_HEADS]) for i, n in enumerate(("chunk_decay", "from_chunk_start")))
    s_evac, s_conv, s_silu = k.sem("ssd_evacuated"), k.sem("ssd_convolved"), k.sem("ssd_silu")
    s_dt, s_exp, s_rows = k.sem("dt_evacuated"), k.sem("dt_exponentials"), k.sem("dt_rows_made")
    s_cols, s_read, s_diff, s_dec = k.sem("dt_cols_turned"), k.sem("dt_cols_read"), k.sem("decay_diff"), k.sem("decays_made")
    k.s_acd = k.sem("decay_rows_stored")
    v = k.vstep
    cols_of = lambda a: a.rearrange("p c h -> p (c h)")
    CW, CB = PARAM_COLS["conv2_w"][0], PARAM_COLS["conv2_b"][0]

    @block.tensor
    def _(pe):
        begin(k, pe)
        for c in range(2):
            pe.wait_ge(k.s_split, DT_0 + 1)
            cols = slice(c * HALF, (c + 1) * HALF)
            for i in range(KT):
                w, wl = k.whi[:, DT_0 % 2, i, 0:SSD_HEADS], k.wlo[:, DT_0 % 2, i, 0:SSD_HEADS]
                bank = k.bank[c][0:SSD_HEADS, :]
                pe.matmul(bank, w, k.hhi[:, i, cols], start=i == 0, stop=False)
                pe.matmul(bank, w, k.hlo[:, i, cols], start=False, stop=False)
                mm = pe.matmul(bank, wl, k.hhi[:, i, cols], start=False, stop=i == KT - 1)
            mm.then_inc(k.s_proj, 1)
        with pe.Fori(0, CV_TILES // 2) as m:
            for b in range(2):
                for c in range(2):
                    pe.wait_ge(s_evac, m * 4 + (2 * b + c + 1))
                    project(k, pe, m * 2 + (CV_0 + b), (CV_0 + b) % 2, c, k.bank[c][:], k.hhi, k.hlo)
        pe.wait_ge(s_rows, 2)
        for i, rows in enumerate((dtr, acr)):
            for c in range(CHUNKS):
                mm = pe.transpose(k.aux[:, i, c * SSD_HEADS:(c + 1) * SSD_HEADS], rows[:, c * P:(c + 1) * P], k.ident[0:SSD_HEADS, 0:SSD_HEADS])
        mm.then_inc(s_cols, 1)
        pe.wait_ge(s_read, 2)
        pe.matmul(k.aux[:, 2, 0:CHUNKS * SSD_HEADS], k.lastrow, cols_of(k.acol), start=True, stop=True).then_inc(s_cols, 1)
        end(k, pe)

    @block.scalar
    def _(act):
        begin(k, act)
        for t in range(KT):
            act.dma_start(k.x1d[t], k.x1[:, t]).then_inc(k.s_spill, 16)
        for c in range(2):
            act.wait_ge(k.s_proj, 2 * DT_0 + c + 1)
            act.activation(x[:, c * HALF:(c + 1) * HALF], k.bank[c][0:SSD_HEADS, :], ACT.Identity, bias=param(k, "dt_bias")[0:SSD_HEADS]).then_inc(s_evac, 1)
        act.wait_ge(s_evac, 2)
        act.activation(e, x, ACT.Abs).then_inc(s_dt, 1)
        act.wait_ge(s_dt, 1)
        act.activation(e, e, ACT.Exp, scale=-1.0).then_inc(s_exp, 1)
        act.activation(a_neg, param(k, "a_log")[0:SSD_HEADS], ACT.Exp).then_inc(s_exp, 1)
        act.wait_ge(k.s_spill, 16 * KT)

        def tile_in(i, b, m):
            act.wait_ge(s_conv, i + 1)
            for c in range(2):
                act.wait_ge(k.s_proj, i * 2 + (2 * CV_0 + c + 1))
                act.activation(xpad[:, b, 3 + c * HALF:3 + (c + 1) * HALF], k.bank[c][:], ACT.Copy).then_inc(s_evac, 1)

        def tile_out(i, b):
            act.wait_ge(s_conv, i + 3)
            act.activation(k.cv[:, ds(i, 1), :].rearrange("p a b -> p (a b)"), cx[:, b], ACT.Silu).then_inc(s_silu, 1)

        tile_in(0, 0, 0)
        with act.Fori(0, CV_TILES // 2 - 1) as m:
            for b in range(2):
                tile_in(m * 2 + (b + 1), 1 - b, m)
                tile_out(m * 2 + b, b)
        tile_in(CV_TILES - 1, 1, 0)
        tile_out(CV_TILES - 2, 0)
        tile_out(CV_TILES - 1, 1)
        act.wait_ge(s_rows, 2)
        act.dma_start(k.acd, acr).then_inc(k.s_acd, 16)
        act.wait_ge(s_cols, 2)
        act.activation(cols_of(k.eac), cols_of(k.acol), ACT.Exp)
        act.wait_ge(s_diff, 1)
        act.activation(cols_of(k.cdec), k.aux[:, 2, 0:CHUNKS * SSD_HEADS], ACT.Exp)
        act.activation(cols_of(k.dlast), cols_of(k.dlast), ACT.Exp).then_inc(s_dec, 1)
        act.wait_ge(k.s_acd, 16)
        end(k, act)

    @block.vector
    def _(dve):
        begin(k, dve)
        dve.sem_inc(s_conv, 2)
        dve.sem_inc(s_silu, 2)
        dve.wait_ge(k.s_spill, 16 * KT)
        dve.memset(xpad[:, :, 0:3], 0.0)
        v.settle(dve, dve.memset(reset, 1.0))
        v.settle(dve, dve.memset(reset.rearrange("h (c l) -> h c l", c=CHUNKS)[:, :, 0:1], 0.0))
        dve.wait_ge(s_evac, 2)
        v.settle(dve, dve.tensor_scalar(relu, x, 0.0, None, ALU.max))
        softplus_dve(k, dve, (s_exp, 2), dtr, e, relu, s, s2, p)
        v.settle(dve, dve.tensor_scalar(a_neg, a_neg, -1.0, None, ALU.mult))
        v.settle(dve, dve.tensor_scalar(s, dtr, a_neg, None, ALU.mult))
        dve.tensor_tensor_scan(acr, reset, s, 0.0, ALU.mult, ALU.add).then_inc(s_rows, 2)
        with dve.Fori(0, CV_TILES // 2) as m:
            v.enter(m, 6)
            for b in range(2):
                dve.wait_ge(s_evac, m * 4 + (2 * b + 4))
                dve.wait_ge(s_silu, m * 2 + (b + 1))
                taps = lambda t: k.par[:, ds(m * (2 * TAPS) + (CW + b * TAPS + t), 1)]
                v.settle(dve, dve.tensor_scalar(cx[:, b], xpad[:, b, 0:T], taps(0), k.par[:, ds(m * 2 + (CB + b), 1)], ALU.mult, ALU.add))
                for t in range(1, TAPS):
                    ins = dve.scalar_tensor_tensor(cx[:, b], xpad[:, b, t:t + T], taps(t), cx[:, b], ALU.mult, ALU.add)
                    if t < TAPS - 1:
                        v.settle(dve, ins)
                ins.then_inc(s_conv, 1)
        v.leave(CV_TILES // 2)
        dve.wait_ge(s_cols, 1)
        dve.tensor_copy(cols_of(k.dtc), k.aux[:, 0, 0:CHUNKS * SSD_HEADS]).then_inc(s_read, 1)
        dve.tensor_copy(cols_of(k.acol), k.aux[:, 1, 0:CHUNKS * SSD_HEADS]).then_inc(s_read, 1)
        dve.wait_ge(s_cols, 2)
        dve.wait_ge(s_read, 2)
        dve.tensor_tensor(cols_of(k.dlast), k.aux[:, 2, 0:CHUNKS * SSD_HEADS], cols_of(k.acol), ALU.subtract).then_inc(s_diff, 1)
        end(k, dve)

    k.stage += 1


def ssd_mix_stage(k, block):
    F = k.F
    GH = SSD_HEADS // 2
    W = GH * SSD_P
    btok = k.at("ssd_b_tokens", F + 48, [P, CHUNKS, P])
    xs = k.at("ssd_x_tokens", F + 52, [P, CHUNKS, W])
    state = k.at("ssd_state", F + 68, [P, 2, W])
    xd = k.at("ssd_x_decayed", F + 72, [P, 2, W])
    ytok = k.at("ssd_y_tokens", F + 76, [P, CHUNKS, W])
    ab = k.at("ssd_decay_rows", F + 92, [P, 2, T])
    m = k.at("ssd_weights", F + 100, [P, 2, T])
    cb = k.at("ssd_cb", F + 108, [P, CHUNKS, P])
    s_turn, s_x, s_bc, s_bread = k.sem("ssd_x_turned"), k.sem("ssd_x_made"), k.sem("ssd_bc_made"), k.sem("ssd_bc_read")
    s_st, s_state, s_off = k.sem("ssd_states_made"), k.sem("ssd_state_carried"), k.sem("ssd_off_read")
    s_ab, s_seg, s_exp, s_m = [k.sem(f"ssd_rows_loaded_{i}") for i in range(2)], k.sem("ssd_seg"), k.sem("ssd_seg_exp"), k.sem("ssd_m")
    s_diag, s_y = k.sem("ssd_diag"), k.sem("ssd_y_added")
    s_back, s_out = k.sem("ssd_y_turned"), k.sem("ssd_y_read")
    v = k.vstep

    def per_head(a, c, g):
        return a[:, c, g * GH:(g + 1) * GH].unsqueeze(2).broadcast_to([P, GH, SSD_P])

    heads_of = lambda a: a.rearrange("p (h e) -> p h e", h=GH)

    @block.tensor
    def _(pe):
        begin(k, pe)
        for g in range(2):
            ct, bt = k.cv[:, g, :], k.cv[:, 2 + g, :]

            def turn(c):
                n = g * CHUNKS + c
                cols = slice(c * P, (c + 1) * P)
                if n >= 2:
                    pe.wait_ge(s_x, n - 1)
                for f in range(4):
                    mm = pe.transpose(k.aux[:, c % 2, f * P:(f + 1) * P], k.cv[:, 4 + 4 * g + f, cols], k.ident)
                mm.then_inc(s_turn, 1)
                if n >= 1:
                    pe.wait_ge(s_bread, n)
                pe.transpose(k.aux[:, 2, 0:P], bt[:, cols], k.ident)
                pe.matmul(k.aux[:, 2, P:2 * P], bt[:, cols], ct[:, cols], start=True, stop=True).then_inc(s_bc, 1)

            if g:
                pe.wait_ge(s_y, GH)
                pe.wait_ge(s_out, 8)
            turn(0)
            for c in range(CHUNKS):
                n = g * CHUNKS + c
                if c + 1 < CHUNKS:
                    turn(c + 1)
                pe.wait_ge(s_bread, n + 1)
                if n >= 1:
                    pe.wait_ge(s_off, n)
                pe.matmul(k.aux[:, 3, :], btok[:, c, :], xd[:, c % 2], start=True, stop=True)
                pe.wait_ge(s_state, n + g + 1)
                pe.matmul(k.aux[:, 4, :], ct[:, c * P:(c + 1) * P], state[:, c % 2], start=True, stop=True).then_inc(s_st, 1)
            with pe.Fori(0, GH // 2) as i:
                for b in range(2):
                    h = i * 2 + (g * GH + b)
                    pe.wait_ge(s_m, h + 1)
                    pe.wait_ge(s_y, h + 1)
                    for c in range(CHUNKS):
                        mm = pe.matmul(k.aux[:, b, c * SSD_P:(c + 1) * SSD_P], m[:, b, c * P:(c + 1) * P],
                                       xs[:, c, ds(i * (2 * SSD_P) + b * SSD_P, SSD_P)], start=True, stop=True)
                    mm.then_inc(s_diag, 1)
            pe.wait_ge(s_y, (g + 1) * GH + 2)
            for f in range(4):
                for a in range(2):
                    n = g * 8 + 2 * f + a
                    if n >= 2:
                        pe.wait_ge(s_out, n - 1)
                    for c in range(4):
                        mm = pe.transpose(k.aux[:, a, c * P:(c + 1) * P], ytok[:, 4 * a + c, f * P:(f + 1) * P], k.ident)
                    mm.then_inc(s_back, 1)
        end(k, pe)

    @block.scalar
    def _(act):
        begin(k, act)

        def load(h, b):
            row = k.acd[ds(h, 1), :] if not isinstance(h, int) else k.acd[h:h + 1, :]
            act.dma_start(ab[:, b], row.broadcast_to([P, T])).then_inc(s_ab[b], 16)

        load(0, 0)
        load(1, 1)

        def decays(h, b):
            act.wait_ge(s_seg, h + 1)
            act.activation(m[:, b], m[:, b], ACT.Exp).then_inc(s_exp, 1)

        with act.Fori(0, SSD_HEADS // 2 - 1) as i:
            for b in range(2):
                decays(i * 2 + b, b)
                load(i * 2 + (b + 2), b)
        for b in range(2):
            decays(SSD_HEADS - 2 + b, b)
        end(k, act)

    @block.vector
    def _(dve):
        begin(k, dve)
        dve.sem_inc(s_y, 2)

        for g in range(2):

            def take(c):
                n = g * CHUNKS + c
                dve.wait_ge(s_turn, n + 1)
                dve.tensor_tensor(heads_of(xs[:, c, :]), heads_of(k.aux[:, c % 2, :]), per_head(k.dtc, c, g), ALU.mult).then_inc(s_x, 1)
                dve.wait_ge(s_bc, n + 1)
                dve.tensor_copy(btok[:, c, :], k.aux[:, 2, 0:P])
                dve.tensor_tensor(cb[:, c, :], k.aux[:, 2, P:2 * P], k.tri, ALU.mult)
                dve.wait_ge(s_x, n + 1)
                if n >= 2:
                    dve.wait_ge(s_st, n - 1)
                dve.tensor_tensor(heads_of(xd[:, c % 2]), heads_of(xs[:, c, :]), per_head(k.dlast, c, g), ALU.mult).then_inc(s_bread, 1)

            dve.memset(state[:, 0], 0.0).then_inc(s_state, 1)
            take(0)
            for c in range(CHUNKS):
                n = g * CHUNKS + c
                if c + 1 < CHUNKS:
                    take(c + 1)
                dve.wait_ge(s_st, n + 1)
                dve.wait_ge(s_state, n + g + 1)
                nxt = state[:, (c + 1) % 2]
                v.settle(dve, dve.tensor_tensor(heads_of(nxt), heads_of(state[:, c % 2]), per_head(k.cdec, c, g), ALU.mult))
                dve.tensor_tensor(nxt, nxt, k.aux[:, 3, :], ALU.add).then_inc(s_state, 1)
                dve.tensor_tensor(heads_of(ytok[:, c, :]), heads_of(k.aux[:, 4, :]), per_head(k.eac, c, g), ALU.mult).then_inc(s_off, 1)
            dve.wait_ge(s_off, (g + 1) * CHUNKS)
            with dve.Fori(0, GH // 2) as i:
                v.enter(i, 2)
                for b in range(2):
                    h = i * 2 + (g * GH + b)
                    dve.wait_ge(s_ab[b], i * 16 + 16 * (g * GH // 2 + 1))
                    dve.wait_ge(s_y, h + 1)
                    col = k.acol[:, :, ds(i * 2 + (g * GH + b), 1)].broadcast_to([P, CHUNKS, P])
                    mc = m[:, b].rearrange("p (c l) -> p c l", c=CHUNKS)
                    v.settle(dve, dve.tensor_tensor(mc, ab[:, b].rearrange("p (c l) -> p c l", c=CHUNKS), col, ALU.subtract))
                    dve.tensor_scalar(m[:, b], m[:, b], 0.0, None, ALU.min).then_inc(s_seg, 1)
                for b in range(2):
                    h = i * 2 + (g * GH + b)
                    dve.wait_ge(s_exp, h + 1)
                    dve.tensor_tensor(m[:, b], m[:, b], cb.rearrange("p c l -> p (c l)"), ALU.mult).then_inc(s_m, 1)
                for b in range(2):
                    h = i * 2 + (g * GH + b)
                    dve.wait_ge(s_diag, h + 1)
                    yh = ytok[:, :, ds(i * (2 * SSD_P) + b * SSD_P, SSD_P)]
                    dve.tensor_tensor(yh, yh, k.aux[:, b, :].rearrange("p (c e) -> p c e", c=CHUNKS), ALU.add).then_inc(s_y, 1)
            v.leave(GH // 2)
            for f in range(4):
                for a in range(2):
                    n = g * 8 + 2 * f + a
                    dve.wait_ge(s_back, n + 1)
                    yt = k.cv[:, 4 + 4 * g + f, a * HALF:(a + 1) * HALF]
                    dve.scalar_tensor_tensor(yt, yt, param(k, "d_skip", 4 * g + f), k.aux[:, a, :], ALU.mult, ALU.add).then_inc(s_out, 1)
        end(k, dve)

    k.stage += 1


def ssd_gate_stage(k, block):
    F = k.F
    sz = k.at("ssd_silu_z", F + 48, [P, 2, HALF])
    sq = k.at("ssd_squared", F + 52, [P, T])
    k.gsum = k.at("ssd_sums", F + 8, [P, 2, T])
    s_z, s_y, s_sq = k.sem("ssd_z_made"), k.sem("ssd_gated"), k.sem("ssd_squares")
    v = k.vstep

    @block.tensor
    def _(pe):
        begin(k, pe)
        with pe.Fori(0, KT // 2) as m:
            for b in range(2):
                for c in range(2):
                    pe.wait_ge(s_z, m * 4 + (2 * b + c + 1))
                    project(k, pe, m * 2 + (Z_0 + b), (Z_0 + b) % 2, c, k.bank[c][:], k.hhi, k.hlo)
        end(k, pe)

    @block.scalar
    def _(act):
        begin(k, act)
        act.sem_inc(s_z, 2)
        with act.Fori(0, KT) as f:
            for c in range(2):
                act.wait_ge(k.s_proj, f * 2 + (2 * Z_0 + c + 1))
                act.wait_ge(s_y, f * 2 + (c + 1))
                act.activation(sz[:, c], k.bank[c][:], ACT.Silu).then_inc(s_z, 1)
        end(k, act)

    @block.vector
    def _(dve):
        begin(k, dve)
        dve.sem_inc(s_y, 2)
        v.settle(dve, dve.memset(k.gsum[:, :, :], 0.0))
        for g in range(2):
            with dve.Fori(0, KT // 2) as f:
                v.enter(f, 2)
                for c in range(2):
                    cols = slice(c * HALF, (c + 1) * HALF)
                    dve.wait_ge(s_z, f * 2 + (KT * g + c + 3))
                    yt = k.cv[:, ds(f + (4 + 4 * g), 1), cols].rearrange("p a b -> p (a b)")
                    dve.tensor_tensor(yt, yt, sz[:, c], ALU.mult).then_inc(s_y, 1)
                dve.wait_ge(s_y, f * 2 + (KT * g + 4))
                yt = k.cv[:, ds(f + (4 + 4 * g), 1), :].rearrange("p a b -> p (a b)")
                v.settle(dve, dve.tensor_tensor(sq, yt, yt, ALU.mult))
                v.settle(dve, dve.tensor_tensor(k.gsum[:, g], k.gsum[:, g], sq, ALU.add))
            v.leave(KT // 2)
        end(k, dve)

    k.stage += 1


def gated_out_stage(k, block, first, hi, lo, tiles, mix, gate, opens=False):
    done = 2 * KT * k.branches
    k.branches += 1
    v = k.vstep

    @block.tensor
    def _(pe):
        begin(k, pe)
        with pe.Fori(0, KT) as f:
            for c in range(2):
                pe.wait_ge(k.s_gates, f * 2 + (done + c + 1))
                project(k, pe, f * 2 + first, first % 2, c, k.bank[c][:], k.hhi, k.hlo)
            for c in range(2):
                pe.wait_ge(k.s_mixed, f * 2 + (done + c + 1))
                project(k, pe, f * 2 + (first + 1), (first + 1) % 2, c, k.aux[:, c, :], hi, lo, range(tiles))
        end(k, pe)

    @block.scalar
    def _(act):
        begin(k, act)
        if opens:
            act.sem_inc(k.s_gates, 2)
        with act.Fori(0, KT) as f:
            for c in range(2):
                act.wait_ge(k.s_proj, f * 4 + (2 * first + c + 1))
                act.wait_ge(k.s_mixed, f * 2 + (done + c + 1))
                act.activation(gate[:, c], k.bank[c][:], ACT.Sigmoid).then_inc(k.s_gates, 1)
        end(k, act)

    @block.vector
    def _(dve):
        begin(k, dve)
        if opens:
            dve.sem_inc(k.s_mixed, 2)
        with dve.Fori(0, KT) as f:
            v.enter(f, 0 if opens else 2)
            for c in range(2):
                dve.wait_ge(k.s_proj, f * 4 + (2 * first + c + 3))
                dve.wait_ge(k.s_gates, f * 2 + (done + c + 3))
                mt = mix[:, ds(f, 1), c * HALF:(c + 1) * HALF].rearrange("p a b -> p (a b)")
                if opens:
                    dve.tensor_tensor(mt, gate[:, c], k.aux[:, c, :], ALU.mult).then_inc(k.s_mixed, 1)
                else:
                    v.settle(dve, dve.tensor_tensor(gate[:, c], gate[:, c], k.aux[:, c, :], ALU.mult))
                    dve.tensor_tensor(mt, mt, gate[:, c], ALU.add).then_inc(k.s_mixed, 1)
        v.leave(KT)
        end(k, dve)

    k.stage += 1




DILATIONS = (1, 4, 16)
GROUPS = len(DILATIONS)
OUT_W = P + 2


def blocks_before(g):
    per = TT // DILATIONS[g]
    return [b for b in range(TT) if per and b % per]


def spans(g, a):
    if g == 0:
        return [(a[:, 0:1, P:], slice(0, 1), slice(P, 2 * P)), (a[:, 1:, :], slice(1, TT), slice(0, 2 * P))]
    if g == 1:
        pairs = a.rearrange("p (r b) w -> p r b w", b=2)
        return [(pairs[:, :, 0, P:], slice(0, TT, 2), slice(P, 2 * P)), (pairs[:, :, 1, :], slice(1, TT, 2), slice(0, 2 * P))]
    return [(a[:, :, P:], slice(0, TT), slice(P, 2 * P))]


def dilated_stage(k, block, bias):
    F = k.F
    q, kk, vtok = (k.at(f"dil_{n}", F + 32 + 12 * i, [P, GROUPS, T]) for i, n in enumerate(("q", "k", "v")))
    vt = k.at("dil_v_features", F + 68, [P, T])
    sq = k.at("dil_squared", F + 72, [P, 2, T])
    p = k.at("dil_p", F + 80, [P, TT, 2 * P])
    pt = k.at("dil_p_turned", F + 88, [P, TT, 2 * P])
    oext = k.at("dil_out", F + 96, [P, GROUPS, TT, OUT_W])
    bias_in = k.at("dil_bias", F + 108.25, [P, GROUPS, 2 * P])
    nmax = k.at("dil_max", F + 111.25, [P, TT])
    stat, rstd = k.at("dil_var", F + 111.5, [P, 2 * TT]), k.at("dil_rstd", F + 111.75, [P, 2 * TT])
    score = k.aux[:, 0:4, :].rearrange("p a (b w) -> p (a b) w", b=2)
    spread_banks = k.aux[:, 0:4, :].rearrange("p a b -> p (a b)")
    out = k.aux[:, 4:6, :].rearrange("p a (b e) -> p (a b) e", b=4)
    s_evac = k.sem("dil_evacuated")
    s_stat, s_var, s_root, s_col = (k.sem(f"dil_{n}") for n in ("summed", "var", "root", "rstd"))
    s_spread, s_norm = k.sem("dil_spread"), k.sem("dil_normed")
    s_vt, s_vtok = k.sem("dil_v_turned"), k.sem("dil_v_read")
    s_score, s_bias, s_max, s_exp = k.sem("dil_scored"), k.sem("dil_biased"), k.sem("dil_max_made"), k.sem("dil_exp")
    s_turn, s_pt = k.sem("dil_p_turns"), k.sem("dil_p_read")
    s_pv, s_o = k.sem("dil_product"), k.sem("dil_out_read")
    s_bin, s_stored = [k.sem(f"dil_bias_loaded_{g}") for g in range(GROUPS)], [k.sem(f"dil_stored_{g}") for g in range(GROUPS)]
    STORES = (1, 4, 2)
    SCALE = P ** -0.5
    v = k.vstep

    def after(j, g):
        return (j, g + 1) if g + 1 < GROUPS else (j + 1, 0)

    def rounds(eng, one):
        with eng.Fori(0, DL_ROUNDS - 1) as j:
            if eng is k.nc.vector:
                v.enter(j, GROUPS * PER_HEAD)
            for g in range(GROUPS):
                one(j, g, True)
        if eng is k.nc.vector:
            v.leave(DL_ROUNDS - 1)
        for g in range(GROUPS):
            one(DL_ROUNDS - 1, g, g + 1 < GROUPS)

    PER_HEAD = 1

    def head(j, g):
        return j * GROUPS + g

    @block.tensor
    def _(pe):
        begin(k, pe)

        def half(j, g, i):
            first = DL_0 + 3 * g + i // 2
            pe.wait_ge(s_evac, j * 18 + (6 * g + i + 1))
            project(k, pe, j * DL_ROUND + first, first % 2, i % 2, k.bank[i % 2][:], k.hhi, k.hlo)

        def statistics(j, g):
            pe.wait_ge(s_evac, j * 18 + (6 * g + 4 + 2))
            pe.wait_ge(s_o, j * 3 + (g + 1))
            for i in range(2):
                for b in range(TT):
                    mm = pe.matmul(k.aux[:, 5, i * TT + b:i * TT + b + 1], sq[:, i, b * P:(b + 1) * P], k.ones, start=True, stop=True)
            mm.then_inc(s_stat, 1)

        def spread(j, g):
            pe.wait_ge(s_col, j * 3 + (g + 1))
            pe.wait_ge(s_pt, j * 3 + (g + 1))
            for b in range(2 * TT):
                mm = pe.matmul(spread_banks[:, b * P:(b + 1) * P], rstd[:, b:b + 1].to_broadcast([P, P]), k.ident, start=True, stop=True)
                if g == GROUPS - 1 and b < 2:
                    mm.then_inc(k.s_proj, 1)
            mm.then_inc(s_spread, 1)

        def values(j, g):
            pe.wait_ge(s_evac, j * 18 + (6 * g + 6 + 2))
            for b in range(TT):
                mm = pe.transpose(out[:, b, :], vt[:, b * P:(b + 1) * P], k.ident)
            mm.then_inc(s_vt, 1)

        def scores(j, g):
            pe.wait_ge(s_norm, j * 3 + (g + 1))
            before = blocks_before(g)
            for b in range(TT):
                qb = q[:, g, b * P:(b + 1) * P]
                if b in before:
                    pe.matmul(score[:, b, 0:P], qb, kk[:, g, (b - 1) * P:b * P], start=True, stop=True)
                mm = pe.matmul(score[:, b, P:], qb, kk[:, g, b * P:(b + 1) * P], start=True, stop=True)
            mm.then_inc(s_score, 1)

        def turns(j, g):
            pe.wait_ge(s_exp, j * 3 * TT + (g + 1) * TT)
            before = blocks_before(g)
            for b in range(TT):
                if b in before:
                    pe.transpose(score[:, b, 0:P], p[:, b, 0:P], k.ident)
                mm = pe.transpose(score[:, b, P:], p[:, b, P:], k.ident)
            mm.then_inc(s_turn, 1)

        def product(j, g):
            pe.wait_ge(s_vtok, j * 3 + (g + 1))
            pe.wait_ge(s_pt, j * 3 + (g + 2))
            before = blocks_before(g)
            for b in range(TT):
                if b in before:
                    pe.matmul(out[:, b, :], pt[:, b, 0:P], vtok[:, g, (b - 1) * P:b * P], start=True, stop=False)
                mm = pe.matmul(out[:, b, :], pt[:, b, P:], vtok[:, g, b * P:(b + 1) * P], start=b not in before, stop=True)
            mm.then_inc(s_pv, 1)

        def one(j, g, more):
            scores(j, g)
            if more:
                for i in range(3):
                    half(*after(j, g), i)
            turns(j, g)
            if more:
                half(*after(j, g), 3)
            product(j, g)
            if more:
                half(*after(j, g), 4)
                statistics(*after(j, g))
                half(*after(j, g), 5)
                spread(*after(j, g))
                values(*after(j, g))

        for i in range(6):
            half(0, 0, i)
        statistics(0, 0)
        spread(0, 0)
        values(0, 0)
        rounds(pe, one)
        end(k, pe)

    @block.scalar
    def _(act):
        begin(k, act)
        act.sem_inc(s_evac, 2)
        act.sem_inc(s_o, 1)

        def load_bias(j, g):
            act.dma_start(bias_in[:, g], bias[DL_ROUNDS * g + j] if isinstance(j, int) else bias[ds(j + DL_ROUNDS * g, 1)].rearrange("a p w -> (a p) w")).then_inc(s_bin[g], 16)

        def half(j, g, i):
            d = DILATIONS[g]
            n = HALF // d
            act.wait_ge(k.s_proj, j * (2 * DL_ROUND) + (2 * DL_0 + 6 * g + i + 1))
            own = lambda a: a.rearrange("p (r i) -> p r i", r=d)[:, :, (i % 2) * n:(i % 2 + 1) * n]
            bank = k.bank[i % 2][:].rearrange("p (i r) -> p r i", r=d)
            if i // 2 == 2:
                act.activation(own(vt), bank, ACT.Copy).then_inc(s_evac, 1)
            else:
                act.activation(own((q, kk)[i // 2][:, g]), bank, ACT.Copy)
                act.activation(own(sq[:, i // 2]), bank, ACT.Square).then_inc(s_evac, 1)

        def root(j, g):
            act.wait_ge(s_var, j * 3 + (g + 1))
            act.activation(stat, stat, ACT.Sqrt).then_inc(s_root, 1)

        def softmax(j, g):
            act.wait_ge(s_max, j * 3 + (g + 1))
            before = blocks_before(g)
            for b in range(TT):
                row = p[:, b, :] if b in before else p[:, b, P:]
                act.activation(row, row, ACT.Exp, bias=nmax[:, b:b + 1], accum_out=oext[:, g, b, P + 1:P + 2]).then_inc(s_exp, 1)

        def store(j, g):
            act.wait_ge(s_pv, j * 3 + (g + 1))
            act.activation(oext[:, g, :, 0:P], out, ACT.Copy).then_inc(s_o, 1)
            act.wait_ge(s_o, j * 3 + (g + 2))
            n = DL_ROUNDS * g + j
            rows = k.dild[n:n + 1] if isinstance(n, int) else k.dild[ds(n, 1)]
            if g == 0:
                act.dma_start(rows.rearrange("a (b p) w -> p (a b) w", p=P), oext[:, g]).then_inc(s_stored[g], 16)
            elif g == 1:
                by_residue = rows.rearrange("a (b p r) w -> r p (a b) w", p=P, r=DILATIONS[g])
                for r in range(DILATIONS[g]):
                    act.dma_start(by_residue[r], oext[:, g, 2 * r:2 * r + 2]).then_inc(s_stored[g], 16)
            else:
                by_half = rows.rearrange("a (i b s) w -> s (a i) b w", b=TT, s=2)
                for s in range(2):
                    act.dma_start(by_half[s], oext[s * 64:(s + 1) * 64, g]).then_inc(s_stored[g], 16)

        def one(j, g, more):
            nxt = after(j, g)
            if more:
                half(*nxt, 0)
            softmax(j, g)
            if not (isinstance(j, int) and j == DL_ROUNDS - 1):
                load_bias(j + 1, g)
            if more:
                for i in (1, 2, 3):
                    half(*nxt, i)
            store(j, g)
            if more:
                half(*nxt, 4)
                root(*nxt)
                half(*nxt, 5)

        for g in range(GROUPS):
            load_bias(0, g)
        for i in range(6):
            half(0, 0, i)
        root(0, 0)
        rounds(act, one)
        for g in range(GROUPS):
            act.wait_ge(s_stored[g], 16 * STORES[g] * DL_ROUNDS + 1)
        end(k, act)

    @block.vector
    def _(dve):
        begin(k, dve)
        dve.sem_inc(s_pt, 1)
        dve.sem_inc(s_bias, 1)
        for g in range(GROUPS):
            dve.sem_inc(s_stored[g], 1)

        def statistics(j, g):
            dve.wait_ge(s_stat, j * 3 + (g + 1))
            dve.tensor_scalar(stat, k.aux[:, 5, 0:2 * TT], 1.0 / P, EPS, ALU.mult, ALU.add).then_inc(s_var, 1)
            dve.wait_ge(s_root, j * 3 + (g + 1))
            dve.reciprocal(rstd, stat).then_inc(s_col, 1)

        def norm(j, g):
            dve.wait_ge(s_spread, j * 3 + (g + 1))
            for i, (a, w) in enumerate(((q, "q_norm"), (kk, "k_norm"))):
                ins = dve.scalar_tensor_tensor(a[:, g], a[:, g], param(k, w), spread_banks[:, i * T:(i + 1) * T], ALU.mult, ALU.mult)
            ins.then_inc(s_norm, 1)
            dve.wait_ge(s_vt, j * 3 + (g + 1))
            dve.tensor_copy(vtok[:, g], k.aux[:, 4:6, :].rearrange("p a b -> p (a b)")).then_inc(s_vtok, 1)

        def softmax(j, g):
            dve.wait_ge(s_score, j * 3 + (g + 1))
            dve.wait_ge(s_bin[g], j * 16 + 16)
            dve.wait_ge(s_stored[g], j * (16 * STORES[g]) + 1)
            parts = list(zip(spans(g, score), spans(g, p)))
            for (s, blocks, cols), (x, _, _) in parts:
                w = cols.stop - cols.start
                n = s.shape[1]
                b = bias_in[:, g, cols].unsqueeze(1).broadcast_to([P, n, w])
                ins = dve.scalar_tensor_tensor(x, s, SCALE, b, ALU.mult, ALU.add)
            ins.then_inc(s_bias, 1)
            dve.wait_ge(s_bias, j * 3 + (g + 2))
            for x, blocks, _ in spans(g, p):
                ins = dve.tensor_reduce(oext[:, g, blocks, P], x, AX, ALU.max)
            v.settle(dve, ins)
            dve.tensor_scalar(nmax, oext[:, g, :, P], -1.0, None, ALU.mult).then_inc(s_max, 1)

        def turned(j, g):
            dve.wait_ge(s_turn, j * 3 + (g + 1))
            for (s, _, _), (x, _, _) in zip(spans(g, score), spans(g, pt)):
                ins = dve.tensor_copy(x, s)
            ins.then_inc(s_pt, 1)

        def one(j, g, more):
            softmax(j, g)
            turned(j, g)
            if more:
                statistics(*after(j, g))
                norm(*after(j, g))

        statistics(0, 0)
        norm(0, 0)
        rounds(dve, one)
        end(k, dve)

    k.stage += 1


def combine_stage(k, block):
    F = k.F
    k.ahi, k.alo = (k.at(f"dil_{n}", F + 32 + 16 * i, [P, DL_ROUNDS, T], F32R) for i, n in enumerate(("hi", "lo")))
    rows = k.at("dil_rows", F + 64, [P, 2, GROUPS, TT, OUT_W])
    o = k.at("dil_sum", F + 88.5, [P, TT, P])
    part = k.at("dil_part", F + 92.5, [P, TT, P])
    mx, den, inv = (k.at(f"dil_all_{n}", F + 96.5 + 0.25 * i, [P, TT]) for i, n in enumerate(("max", "sum", "inv")))
    e, es = (k.at(n, F + 97.5 + 0.25 * i, [P, TT, GROUPS]) for i, n in enumerate(("dil_factor", "dil_factor_sum")))
    s_in, s_e = [k.sem(f"dil_rows_loaded_{i}") for i in range(2)], k.sem("dil_factors")
    s_d, s_o, s_t = k.sem("dil_from_max"), k.sem("dil_summed_over"), k.sem("dil_summed_turned")
    s_hi, s_lo = k.sem("dil_high"), k.sem("dil_low")
    v = k.vstep
    turn = k.aux[:, 0:2, :].rearrange("p a b -> p (a b)")

    @block.tensor
    def _(pe):
        begin(k, pe)
        for j in range(DL_ROUNDS):
            pe.wait_ge(s_o, j + 1)
            if j:
                pe.wait_ge(s_lo, j)
            for b in range(TT):
                mm = pe.transpose(turn[:, b * P:(b + 1) * P], o[:, b, :], k.ident)
            mm.then_inc(s_t, 1)
        end(k, pe)

    @block.scalar
    def _(act):
        begin(k, act)

        def load(j):
            for g in range(GROUPS):
                act.dma_start(rows[:, j % 2, g], k.dild[DL_ROUNDS * g + j].rearrange("(b p) w -> p b w", p=P)).then_inc(s_in[j % 2], 16)

        load(0)
        load(1)
        for j in range(DL_ROUNDS):
            act.wait_ge(s_d, j + 1)
            act.activation(e, e, ACT.Exp).then_inc(s_e, 1)
            act.wait_ge(s_t, j + 1)
            act.activation(k.ahi[:, j], turn, ACT.Copy).then_inc(s_hi, 1)
            if j + 2 < DL_ROUNDS:
                act.wait_ge(s_o, j + 1)
                load(j + 2)
        end(k, act)

    @block.vector
    def _(dve):
        begin(k, dve)

        def low(j):
            dve.wait_ge(s_hi, j + 1)
            dve.tensor_tensor(k.alo[:, j], turn, k.ahi[:, j].bitcast(F32), ALU.subtract).then_inc(s_lo, 1)

        for j in range(DL_ROUNDS):
            dve.wait_ge(s_in[j % 2], 16 * GROUPS * (j // 2 + 1))
            by_token = rows[:, j % 2].rearrange("p g b w -> p b g w")
            v.settle(dve, dve.tensor_reduce(mx, by_token[:, :, :, P], AX, ALU.max))
            dve.tensor_tensor(e, by_token[:, :, :, P], mx.unsqueeze(2).broadcast_to([P, TT, GROUPS]), ALU.subtract).then_inc(s_d, 1)
            dve.wait_ge(s_e, j + 1)
            v.settle(dve, dve.tensor_tensor(es, e, by_token[:, :, :, P + 1], ALU.mult))
            v.settle(dve, dve.tensor_reduce(den, es, AX, ALU.add))
            v.settle(dve, dve.reciprocal(inv, den))
            v.settle(dve, dve.tensor_tensor(e, e, inv.unsqueeze(2).broadcast_to([P, TT, GROUPS]), ALU.mult))
            if j:
                dve.wait_ge(s_t, j)
            for g in range(GROUPS):
                w = e[:, :, g:g + 1].broadcast_to([P, TT, P])
                v.settle(dve, dve.tensor_tensor(o if g == 0 else part, rows[:, j % 2, g, :, 0:P], w, ALU.mult))
                if g:
                    ins = dve.tensor_tensor(o, o, part, ALU.add)
                    if g < GROUPS - 1:
                        v.settle(dve, ins)
            ins.then_inc(s_o, 1)
            dve.wait_ge(s_o, j + 1)
            low(j)
        end(k, dve)

    k.stage += 1




def pool_stage(k, block):
    F = k.F
    PAD = 16
    k.phi, k.plo = (k.at(f"pool_{n}", F + 32 + 32 * i, [P, KT, T], F32R) for i, n in enumerate(("hi", "lo")))
    u = k.at("pool_u", F + 96, [P, 2, PAD + T])
    tmp = k.at("pool_tmp", F + 104.25, [P, 2, PAD + T])
    k.s_phi, k.s_plo = k.sem("pool_high"), k.sem("pool_low")
    s_u, s_diff = k.sem("pool_u_in"), k.sem("pool_diff")
    v = k.vstep

    @block.tensor
    def _(pe):
        begin(k, pe)
        with pe.Fori(0, KT // 2) as m:
            for b in range(2):
                for c in range(2):
                    pe.wait_ge(s_u, m * 4 + (2 * b + c + 1))
                    project(k, pe, m * 2 + (U_0 + b), (U_0 + b) % 2, c, k.bank[c][:], k.hhi, k.hlo)
        end(k, pe)

    @block.scalar
    def _(act):
        begin(k, act)
        act.sem_inc(s_u, 2)

        def u_in(f):
            if f >= 2:
                act.wait_ge(s_diff, f - 1)
            for c in range(2):
                act.wait_ge(k.s_proj, 2 * U_0 + 2 * f + c + 1)
                act.activation(u[:, f % 2, PAD + c * HALF:PAD + (c + 1) * HALF], k.bank[c][:], ACT.Copy).then_inc(s_u, 1)

        u_in(0)
        for f in range(KT):
            if f + 1 < KT:
                u_in(f + 1)
            act.wait_ge(s_diff, f + 1)
            act.activation(k.phi[:, f], tmp[:, (f // 2 + 1) % 2, PAD:], ACT.Copy).then_inc(k.s_phi, 1)
        end(k, act)

    @block.vector
    def _(dve):
        begin(k, dve)
        v.settle(dve, dve.memset(u[:, :, 0:PAD], 0.0))
        for f in range(KT):
            levels = f // 2 + 1
            w = 2 ** levels
            dve.wait_ge(s_u, 2 * f + 4)
            if f:
                dve.wait_ge(k.s_plo, f)
            src = u[:, f % 2]
            for level in range(levels):
                step = 2 ** level
                at = 2 * step - 1
                dst = tmp[:, level % 2]
                v.settle(dve, dve.tensor_tensor(dst[:, at:], src[:, at:], src[:, at - step:PAD + T - step], ALU.add))
                src = dst
            own, diff = u[:, f % 2, PAD:], tmp[:, levels % 2, PAD:]
            v.settle(dve, dve.scalar_tensor_tensor(diff, src[:, PAD:], 1.0 / w, own, ALU.mult, ALU.subtract))
            v.settle(dve, dve.tensor_tensor(diff[:, 0:w - 1], src[:, PAD:PAD + w - 1], k.inv_count[:, 0:w - 1], ALU.mult))
            dve.tensor_tensor(diff[:, 0:w - 1], diff[:, 0:w - 1], own[:, 0:w - 1], ALU.subtract).then_inc(s_diff, 1)
            dve.wait_ge(k.s_phi, f + 1)
            dve.tensor_tensor(k.plo[:, f], diff, k.phi[:, f].bitcast(F32), ALU.subtract).then_inc(k.s_plo, 1)
        end(k, dve)

    k.stage += 1


def pool_mix_stage(k, block):
    s_mix = k.sem("pool_mixed")
    GT = 2
    GROUPS_OF_SLAB = 2

    def banks(i):
        return [k.aux[:, n, :] for n in range(4)] if i % 2 == 0 else [k.aux[:, 4, :], k.aux[:, 5, :], k.bank[0][:], k.bank[1][:]]

    @block.tensor
    def _(pe):
        begin(k, pe)
        for i in range(KT // GT):
            slab, gg = MX_0 + i // GROUPS_OF_SLAB, i % GROUPS_OF_SLAB
            pe.wait_ge(k.s_split, slab + 1)
            if i >= 2:
                pe.wait_ge(k.s_plo, KT + 4 * (i - 1))
            for t in range(GT):
                for c in range(2):
                    project(k, pe, slab, slab % 2, c, banks(i)[2 * t + c], k.phi, k.plo, [(4 * gg + 2 * a + t, GT * i + a) for a in range(GT)],
                            counts=t == GT - 1 and c == 1)
            pe.drain().then_inc(s_mix, 1)
        end(k, pe)

    @block.scalar
    def _(act):
        begin(k, act)
        for i in range(KT // GT):
            act.wait_ge(s_mix, i + 1)
            for t in range(GT):
                f = GT * i + t
                for c in range(2):
                    act.activation(k.phi[:, f, c * HALF:(c + 1) * HALF], banks(i)[2 * t + c], ACT.Copy, scale=param(k, "pool_scale", f)).then_inc(k.s_phi, 1)
        end(k, act)

    @block.vector
    def _(dve):
        begin(k, dve)
        for i in range(KT // GT):
            for t in range(GT):
                f = GT * i + t
                for c in range(2):
                    cols = slice(c * HALF, (c + 1) * HALF)
                    dve.wait_ge(k.s_phi, KT + 4 * i + 2 * t + c + 1)
                    dve.scalar_tensor_tensor(k.plo[:, f, cols], banks(i)[2 * t + c], param(k, "pool_scale", f), k.phi[:, f, cols].bitcast(F32),
                                             ALU.mult, ALU.subtract).then_inc(k.s_plo, 1)
        end(k, dve)

    k.stage += 1




def mixer_out_stage(k, block, mix):
    F = k.F
    k.x2 = k.at("x2", F + 32, [P, KT, T])
    k.ssum2, sq = k.at("x2_sum", F, [P, T]), k.at("x2_squared", F + 4, [P, T])
    s_hi, s_lo, s_x1, s_read = k.sem("mix_high"), k.sem("mix_low"), k.sem("x1_again"), k.sem("mixer_out_read")
    v = k.vstep

    @block.tensor
    def _(pe):
        begin(k, pe)
        pe.wait_ge(s_lo, KT)
        with pe.Fori(0, KT // 2) as m:
            for b in range(2):
                for c in range(2):
                    pe.wait_ge(s_read, m * 4 + (2 * b + c + 1))
                    project(k, pe, m * 2 + (WO_0 + b), (WO_0 + b) % 2, c, k.bank[c][:], k.hhi, k.hlo)
        end(k, pe)

    @block.scalar
    def _(act):
        begin(k, act)
        for t in range(KT):
            act.dma_start(k.x2[:, t], k.x1d[t]).then_inc(s_x1, 16)
        for t in range(KT):
            act.activation(k.hhi[:, t], mix[:, t], ACT.Copy).then_inc(s_hi, 1)
        end(k, act)

    @block.vector
    def _(dve):
        begin(k, dve)
        dve.sem_inc(s_read, 2)
        for t in range(KT):
            dve.wait_ge(s_hi, t + 1)
            dve.tensor_tensor(k.hlo[:, t], mix[:, t], k.hhi[:, t].bitcast(F32), ALU.subtract).then_inc(s_lo, 1)
        dve.wait_ge(s_lo, KT)
        v.settle(dve, dve.memset(k.ssum2, 0.0))
        dve.wait_ge(s_x1, 16 * KT)
        with dve.Fori(0, KT) as f:
            v.enter(f, 2)
            for c in range(2):
                dve.wait_ge(k.s_proj, f * 2 + (2 * WO_0 + c + 1))
                xt = k.x2[:, ds(f, 1), c * HALF:(c + 1) * HALF].rearrange("p a b -> p (a b)")
                dve.scalar_tensor_tensor(xt, k.bank[c][:], k.mod[:, ds(f + 16, 1)], xt, ALU.mult, ALU.add).then_inc(s_read, 1)
            dve.wait_ge(s_read, f * 2 + 4)
            xt = k.x2[:, ds(f, 1), :].rearrange("p a b -> p (a b)")
            v.settle(dve, dve.tensor_tensor(sq, xt, xt, ALU.mult))
            v.settle(dve, dve.tensor_tensor(k.ssum2, k.ssum2, sq, ALU.add))
        v.leave(KT)
        end(k, dve)

    k.stage += 1


def ffn_stage(k, block, out):
    F = k.F
    fhi, flo = k.at("ffn_hi", F, [P, KT, T], F32R), k.at("ffn_lo", F + 64, [P, KT, T], F32R)
    act2 = k.at("ffn_relu_squared", F + 96, [P, 2, T])
    s_read, s_sq, s_hi, s_lo = k.sem("ffn_read"), k.sem("ffn_squared"), k.sem("ffn_high"), k.sem("ffn_low")
    s_x2, s_out = k.sem("x2_added"), k.sem("out_written")
    ROUND = 2 * 2 * KT

    @block.tensor
    def _(pe):
        begin(k, pe)
        with pe.Fori(0, FF_QUARTERS) as r:
            for f in range(KT):
                for c in range(2):
                    if f == 0:
                        pe.wait_ge(s_x2, r * (2 * KT) + (c + 1))
                    else:
                        pe.wait_ge(s_read, r * (2 * KT) + (2 * f + c - 1))
                    project(k, pe, r * (2 * KT) + (FF_0 + f), (FF_0 + f) % 2, c, k.bank[c][:], k.hhi, k.hlo)
            for f in range(KT):
                slab, slot = r * (2 * KT) + (FF_0 + KT + f), (FF_0 + KT + f) % 2
                for c in range(2):
                    if f == 0:
                        pe.wait_ge(s_read, r * (2 * KT) + (2 * KT + c - 1))
                    else:
                        pe.wait_ge(s_x2, r * (2 * KT) + (2 * f + c + 1))
                    if f == 0 and c == 0:
                        pe.wait_ge(s_lo, r * KT + (KT + 1))
                        project(k, pe, slab, slot, c, k.bank[c][:], fhi, flo, range(KT - 1), last=False, counts=False)
                        pe.wait_ge(s_lo, r * KT + (KT + 2))
                        project(k, pe, slab, slot, c, k.bank[c][:], fhi, flo, [KT - 1], first=False)
                    else:
                        project(k, pe, slab, slot, c, k.bank[c][:], fhi, flo)
        end(k, pe)

    @block.scalar
    def _(act):
        begin(k, act)
        with act.Fori(0, FF_QUARTERS) as r:

            def high(f):
                act.wait_ge(s_sq, r * KT + (f + 1))
                act.activation(fhi[:, f], act2[:, f % 2], ACT.Copy).then_inc(s_hi, 1)

            for f in range(KT):
                act.wait_ge(s_lo, r * KT + (f + 1))
                for c in range(2):
                    act.wait_ge(k.s_proj, r * ROUND + (2 * FF_0 + 2 * f + c + 1))
                    act.activation(act2[:, f % 2, c * HALF:(c + 1) * HALF], k.bank[c][:], ACT.Copy).then_inc(s_read, 1)
                if f:
                    high(f - 1)
            high(KT - 1)
        end(k, act)

    @block.vector
    def _(dve):
        begin(k, dve)
        dve.sem_inc(s_x2, 2)
        dve.sem_inc(s_lo, 2)
        with dve.Fori(0, FF_QUARTERS) as r:

            def low(f):
                dve.wait_ge(s_hi, r * KT + (f + 1))
                dve.tensor_tensor(flo[:, f], act2[:, f % 2], fhi[:, f].bitcast(F32), ALU.subtract).then_inc(s_lo, 1)

            for f in range(KT):
                dve.wait_ge(s_read, r * (2 * KT) + (2 * f + 2))
                dve.scalar_tensor_tensor(act2[:, f % 2], act2[:, f % 2], 0.0, act2[:, f % 2], ALU.max, ALU.mult).then_inc(s_sq, 1)
                if f:
                    low(f - 1)
            low(KT - 1)
            dve.wait_ge(s_lo, r * KT + (KT + 2))
            dve.wait_ge(s_x2, r * (2 * KT) + 2)
            for f in range(KT):
                for c in range(2):
                    dve.wait_ge(k.s_proj, r * ROUND + (2 * FF_0 + 2 * KT + 2 * f + c + 1))
                    xt = k.x2[:, f, c * HALF:(c + 1) * HALF]
                    dve.scalar_tensor_tensor(xt, k.bank[c][:], k.mod[:, 40 + f:41 + f], xt, ALU.mult, ALU.add).then_inc(s_x2, 1)
        end(k, dve)

    @block.sync
    def _(sp):
        for f in range(KT):
            sp.wait_ge(s_x2, 2 + 2 * KT * (FF_QUARTERS - 1) + 2 * f + 2)
            sp.dma_start(out[:, f], k.x2[:, f]).then_inc(s_out, 16)
        sp.wait_ge(s_out, 16 * KT)

    k.stage += 1




def build(nc, ins, out, scratch):
    with ExitStack() as ctx:
        k = make_core(nc, ctx)
        xT, wts, params, consts, gate_w, ada_w, bias = ins
        k.x1d, k.mixd, k.acd, k.dild = scratch
        k.s_spill = k.sem("x1_stored")
        block = ctx.enter_context(nc.Block())
        setup_stage(k, block, xT, params, consts, wts)
        weight_split(k, block)
        sq = k.at("pre_sq", k.Y + 2, [P, 2, T])
        ssum = k.at("pre_sum", k.Y + 10, [P, T])
        square_sum_stage(k, "pre_squares", block, lambda t: k.xt[:, t], sq, ssum, k.s_x)
        tmp = k.at("pre_tmp", k.Y + 14, [P, 2, T])
        norm_split_stage(k, block, lambda t: k.xt[:, t], ssum, lambda t: param(k, "pre_g", t), None, tmp)
        lru_stage(k, block, wts, gate_w, ada_w)
        rest_of_slabs(k, block, wts)
        attention_stage(k, block)
        out_project_stage(k, block)
        post_norm_stage(k, block, xT)
        block2_gains(k, block)
        tmp = k.at("norm1_tmp", k.W, [P, 2, T])
        norm_split_stage(k, block, lambda t: k.x1[:, t], k.ssum1, lambda t: k.gain1[:, t:t + 1], lambda t: k.mod[:, t:t + 1], tmp)
        ssd_inputs_stage(k, block)
        ssd_mix_stage(k, block)
        ssd_gate_stage(k, block)
        ssd_norm_stage(k, block)
        mix = k.at("ssd_mix", k.F, [P, KT, T])
        gate = k.at("ssd_gate", k.F + 32, [P, 2, HALF])
        gated_out_stage(k, block, SO_0, k.shi, k.slo, KT, mix, gate, True)
        dilated_stage(k, block, bias)
        combine_stage(k, block)
        gate = k.at("dil_gate", k.F + 101, [P, 2, HALF])
        gated_out_stage(k, block, AO_0, k.ahi, k.alo, DL_ROUNDS, mix, gate)
        pool_stage(k, block)
        pool_mix_stage(k, block)
        gate = k.at("pool_gate", k.F + 96, [P, 2, HALF])
        gated_out_stage(k, block, PO_0, k.phi, k.plo, KT, mix, gate)
        mixer_out_stage(k, block, mix)
        tmp = k.at("norm2_tmp", k.F + 8, [P, 2, T])
        norm_split_stage(k, block, lambda t: k.x2[:, t], k.ssum2, lambda t: k.gain2[:, t:t + 1], lambda t: k.mod[:, 24 + t:25 + t], tmp)
        ffn_stage(k, block, out)


def slab(w, r0, c0, cols=P):
    part = w[r0:r0 + D, c0:c0 + cols]
    part = np.pad(part, ((0, D - part.shape[0]), (0, P - part.shape[1])))
    return part.reshape(KT, P, P).transpose(1, 0, 2)


def pack(i):
    w1, w2 = i["w_in"][0], i["w_in_2"][0]
    at_z, at_x, at_b, at_c, at_dt, at_q, at_k, at_v, at_u, at_g = 0, 1024, 2048, 2304, 2560, 2576, 4112, 5648, 7184, 8208
    tiles = lambda w, r0, c0: [slab(w, r0, c0 + t * P) for t in range(KT)]
    slabs = []
    for n in range(LRU_BLOCKS):
        slabs += [slab(w1, 0, 4 * D + n * P), slab(w1, 0, 5 * D + n * P)]
    for h in range(HEADS):
        slabs += [slab(w1, 0, part * D + h * P) for part in range(4)]
    for f in range(KT):
        slabs += [slab(i["w_out"][0], half * D, f * P) for half in range(2)]
    slabs += [slab(w2, 0, at_dt, SSD_HEADS)]
    slabs += [slab(w2, 0, c) for c in (at_c, at_c + P, at_b, at_b + P)] + tiles(w2, 0, at_x)
    slabs += tiles(w2, 0, at_z)

    def gated(n, w):
        return [s for f in range(KT) for s in (slab(w2, 0, at_g + n * D + f * P), slab(w, 0, f * P))]

    slabs += gated(0, i["w_ssd_out_2"][0])
    for j in range(DL_ROUNDS):
        for g in range(DIL_HEADS // DL_ROUNDS):
            slabs += [slab(w2, 0, a + (DL_ROUNDS * g + j) * P) for a in (at_q, at_k, at_v)]
        slabs += [np.zeros((P, KT, P), np.float32)]
    slabs += gated(1, i["w_attn_out_2"][0])
    slabs += tiles(w2, 0, at_u)
    pool = i["w_pool_mix_2"][0].reshape(2, 2, 2, P, 2, P)
    slabs += [pool[a].transpose(2, 0, 1, 3, 4).reshape(P, KT, P) for a in range(2)]
    slabs += gated(2, i["w_pool_out_2"][0])
    slabs += tiles(i["w_out_2"][0], 0, 0)
    for q in range(FF_QUARTERS):
        slabs += tiles(i["w_ff1_2"][0], 0, q * D) + tiles(i["w_ff2_2"][0], q * D, 0)
    wts = np.stack(slabs)
    assert len(wts) == N_SLABS
    col = lambda a: a.reshape(-1, P).T
    pair = lambda a, b: np.pad(np.stack([a.reshape(-1), b.reshape(-1)], 1), ((0, P - QK), (0, 0)))
    rows = lambda a: np.pad(a.reshape(-1, 1), ((0, P - a.size), (0, 0)))
    conv = i["conv_w"][0].reshape(TAPS, KT, P).transpose(2, 1, 0).reshape(P, -1)
    order = [10, 11, 8, 9, 0, 1, 2, 3, 4, 5, 6, 7]
    conv2 = i["conv_w_2"][0].reshape(TAPS, CV_TILES, P)[:, order].transpose(2, 1, 0).reshape(P, -1)
    params = np.concatenate([
        col(i["pre_norm_g"]), conv, col(i["conv_b"]), col(i["b_rgate"]), col(i["b_igate"]), col(i["lru_lambda"]), col(i["post_norm_g"]),
        col(i["subln_g"]), pair(i["lambda_q1"], i["lambda_q2"]), pair(i["lambda_k1"], i["lambda_k2"]), col(i["c_2"]), col(i["b_ada_2"]),
        conv2, col(i["conv_b_2"])[:, order], rows(i["dt_bias_2"]), rows(i["a_log_2"]), col(np.repeat(i["d_skip_2"].reshape(-1), SSD_P)),
        col(i["ssd_norm_w_2"]), col(i["norm1_w_2"]), col(i["norm2_w_2"]), col(i["q_norm_w_2"]), col(i["k_norm_w_2"]), col(i["pool_scale_2"]),
    ], 1)
    gate = np.stack([i["w_rgate"][0], i["w_igate"][0]], 2).transpose(1, 0, 2, 3)
    ada = i["w_ada_2"][0].reshape(KT, P, LRU_BLOCKS, ADA_COLS).transpose(2, 0, 1, 3)
    xT = i["x"][0].T.reshape(KT, P, T)
    return {"xT": xT, "wts": wts, "params": params, "consts": constants(), "gate_w": gate, "ada_w": ada, "bias": dilated_bias()}


def constants():
    a, b = np.arange(P)[:, None], np.arange(P)[None, :]
    last = np.broadcast_to(a == P - 1, (P, P))
    return np.concatenate([np.eye(P), np.where(b <= a, 0.0, NEG), a <= b, last, 1.0 / np.broadcast_to(np.arange(1, N_CONST - INV + 1), (P, N_CONST - INV))], 1).astype(np.float32)


def dilated_bias():
    base = 2.0 ** (-8.0 / 8)
    more = 2.0 ** (-8.0 / 16)
    slopes = [base ** (n + 1) for n in range(8)] + [more ** (n + 1) for n in range(0, 8, 2)]
    slopes = np.sort(np.asarray(slopes, np.float32))[::-1]
    out = np.empty((DIL_HEADS, P, 2 * P), np.float32)
    for head in range(DIL_HEADS):
        group, dilation = head // DL_ROUNDS, (1, 4, 16)[head // DL_ROUNDS]
        q, key = np.arange(P)[:, None], np.arange(2 * P)[None, :]
        if group == 2:
            rel = np.where(key >= P, q % 64 - (key - P) % 64, -1)
            rel = np.where(q // 64 == (key - P) // 64, rel, -1)
        else:
            rel = q + P - key
        valid = (rel >= 0) & (rel <= P)
        out[head] = np.where(valid, -slopes[head] * (rel * dilation).astype(np.float32), NEG)
    return out


def kernel(**inputs):
    import concourse.bacc as bacc
    from concourse.bass_utils import run_bass_kernel_spmd

    nc = bacc.Bacc("TRN2", target_bir_lowering=False, num_devices=1)
    arrays = {n: np.ascontiguousarray(a) for n, a in pack({n: np.asarray(a) for n, a in inputs.items()}).items()}
    aps = [nc.dram_tensor(n, a.shape, F32, kind="ExternalInput").ap() for n, a in arrays.items()]
    out = nc.dram_tensor("outT", (P, KT, T), F32, kind="ExternalOutput").ap()
    scratch = [nc.dram_tensor(n, s, F32, kind="Internal").ap() for n, s in (
        ("x1_kept", (KT, P, T)), ("mix_kept", (KT, P, T)), ("decay_sums", (SSD_HEADS, T)), ("dilated_out", (DIL_HEADS, T, P + 2)))]
    build(nc, aps, out, scratch)
    r = run_bass_kernel_spmd(nc, [arrays], core_ids=[0])
    return np.ascontiguousarray(r.results[0]["outT"].transpose(2, 1, 0)).reshape(1, T, D)
```

```python
import math
from contextlib import ExitStack

import concourse.bass as bass
import numpy as np
from concourse import mybir

F32 = mybir.dt.float32
F32R = mybir.dt.float32r
BF16 = mybir.dt.bfloat16
ALU = mybir.AluOpType
ACT = mybir.ActivationFunctionType
AX = mybir.AxisListType.X
ds = bass.ds

P = 128
D = 1024
T = 1024
KT = D // P
TT = T // P
HALF = 512
HEADS = 8
QK = 64
LRU_BLOCKS = 8
TAPS = 4
EPS = 1e-6
LAM_INIT = 0.8 - 0.6 * math.exp(0.0)
NEG = -1e30
ADA = 6 * D
X_TILES = 2
ADA_COLS = ADA // LRU_BLOCKS

LRU_SLABS = 2 * LRU_BLOCKS
ATT_SLABS = 4 * HEADS
OUT1_SLABS = 2 * KT
LRU_0 = 0
ATT_0 = LRU_0 + LRU_SLABS
OUT1_0 = ATT_0 + ATT_SLABS
DT_0 = OUT1_0 + OUT1_SLABS
CV_TILES = 12
CV_0 = DT_0 + 1
Z_0 = CV_0 + CV_TILES
SO_0 = Z_0 + KT
DIL_HEADS = 12
DL_0 = SO_0 + 2 * KT
DL_ROUNDS = 4
DL_ROUND = 10
AO_0 = DL_0 + DL_ROUNDS * DL_ROUND
U_0 = AO_0 + 2 * KT
MX_0 = U_0 + KT
PO_0 = MX_0 + 2
WO_0 = PO_0 + 2 * KT
FF_0 = WO_0 + KT
FF_QUARTERS = 4
N_SLABS = FF_0 + FF_QUARTERS * 2 * KT

SSD_HEADS = 16
SSD_P = 64
CHUNKS = T // P

PARAM_COLS = {}


def _columns():
    at = 0
    for name, n in (
        ("pre_g", 8), ("conv1_w", 32), ("conv1_b", 8), ("b_r", 8), ("b_i", 8), ("lru_lam", 8), ("post_g", 8),
        ("subln_g", 1), ("lq", 2), ("lk", 2), ("c", 8), ("b_ada", 48),
        ("conv2_w", CV_TILES * TAPS), ("conv2_b", CV_TILES), ("dt_bias", 1), ("a_log", SSD_HEADS), ("d_skip", 8), ("ssd_norm", 8),
        ("norm1", 8), ("norm2", 8), ("q_norm", 1), ("k_norm", 1), ("pool_scale", 8),
    ):
        PARAM_COLS[name] = (at, n)
        at += n
    return at


N_PARAMS = _columns()
IDENT, CAUSAL, TRI, LASTROW, INV, N_CONST = 0, 128, 256, 384, 512, 528


class Count:

    def __init__(self, sem):
        self.sem, self.base, self.off, self.var, self.per = sem, 0, 0, None, 0

    def enter(self, var, per):
        self.base, self.off, self.var, self.per = self.base + self.off, 0, var, per

    def leave(self, rounds):
        assert self.off == self.per, (self.sem, self.off, self.per)
        self.base, self.off, self.var = self.base + self.per * rounds, 0, None

    def up(self, ins):
        ins.then_inc(self.sem, 1)
        self.off += 1

    def value(self):
        fixed = self.base + self.off
        return fixed if self.var is None else self.var * self.per + fixed

    def settle(self, eng, ins):
        self.up(ins)
        eng.wait_ge(self.sem, self.value())


class Core:
    pass


def make_core(nc, ctx):
    k = Core()
    k.nc = nc
    base = -(-nc.sbuf_base // 64) * 64
    k.top = 207 * 1024

    def at(name, kb, shape, dt=F32):
        size = 4 * int(np.prod(shape[1:]))
        assert kb * 1024 + size <= k.top, (name, kb, size)
        return nc.alloc_sbuf_tensor_at(name, shape, dt, offset=base + int(kb * 1024))[:]

    def sem(name):
        return ctx.enter_context(nc.semaphore(name))

    k.at, k.sem = at, sem
    k.raw = at("slab_raw", 0, [P, 2, KT, P])
    k.whi = at("slab_hi", 8, [P, 2, KT, P], F32R)
    k.wlo = at("slab_lo", 16, [P, 2, KT, P], F32R)
    k.const = at("const", 24, [P, N_CONST])
    k.par = at("params", 26.0625, [P, N_PARAMS])
    k.mod_all = at("mod", 27.5, [P, ADA_COLS // P + 48])
    k.mod = k.mod_all[:, ADA_COLS // P:]
    k.small = at("small", 27.75, [P, 128])
    k.H, k.Y, k.W = 30, 94, 158
    k.F = k.Y
    k.hhi = at("h_hi", k.H, [P, KT, T], F32R)
    k.hlo = at("h_lo", k.H + 32, [P, KT, T], F32R)
    k.bank = [ctx.enter_context(nc.psum_tensor(f"proj_bank{c}", [P, HALF], F32)) for c in range(2)]
    k.aux = ctx.enter_context(nc.psum_tensor("aux_banks", [P, 6, HALF], F32))
    k.ident = k.const[:, IDENT:IDENT + P]
    k.causal = k.const[:, CAUSAL:CAUSAL + P]
    k.mask = at("mask_operands", 28.25, [P, 2, P], BF16)
    k.tri = k.const[:, TRI:TRI + P]
    k.lastrow = k.const[:, LASTROW:LASTROW + P]
    k.inv_count = k.const[:, INV:N_CONST]
    k.ones = k.small[:, 0:1]
    k.cn, k.ncn = k.small[:, 1:9], k.small[:, 9:17]
    k.cond, k.lam, k.subg = k.small[:, 17:25], k.small[:, 25:26], k.small[:, 26:27]
    k.stat, k.rstd = k.small[:, 27:35], k.small[:, 35:43]
    k.s_raw = [sem("raw_loaded_0"), sem("raw_loaded_1")]
    k.s_hi = sem("slab_hi_made")
    k.s_begun = sem("slab_begun")
    k.s_split = sem("slab_split")
    k.s_proj = sem("chunk_projected")
    k.s_stage = sem("stage_ended")
    k.s_vstep = sem("dve_step")
    k.s_astep = sem("act_step")
    k.vstep, k.astep = Count(k.s_vstep), Count(k.s_astep)
    k.s_sum, k.s_var, k.s_col, k.s_spread = sem("norm_summed"), sem("norm_var"), sem("norm_rstd"), sem("norm_spread")
    k.s_normed, k.s_high, k.s_low = sem("normed"), sem("normed_high"), sem("normed_low")
    k.s_gates, k.s_mixed = sem("branch_gates"), sem("branch_mixed")
    k.s_x = [sem(f"x_loaded_{i}") for i in range(KT // X_TILES)]
    k.norms, k.splits, k.branches = 0, 0, 0
    k.stage = 0
    return k


def param(k, name, i=0, n=1):
    a, _ = PARAM_COLS[name]
    return k.par[:, a + i:a + i + n]


def param_dyn(k, name, i, step=1):
    a, _ = PARAM_COLS[name]
    return k.par[:, ds(i * step + a, 1)]


def begin(k, eng):
    if k.stage:
        eng.wait_ge(k.s_stage, 3 * k.stage)


def end(k, eng):
    eng.drain().then_inc(k.s_stage, 1)


def project(k, pe, slab, slot, chunk, bank, hi, lo, ks=range(KT), first=True, last=True, counts=True, ready=None):
    if chunk == 0:
        pe.wait_ge(k.s_split, slab + 1)
    cols = slice(chunk * HALF, (chunk + 1) * HALF)
    ks = list(ks)
    for a, (wk, xk) in enumerate((i, i) if isinstance(i, int) else i for i in ks):
        if ready is not None and chunk == 0 and (a == 0 or len(ready) == 2):
            pe.wait_ge(ready[0], ready[1] + (xk + 1 if len(ready) == 2 else ready[2]))
        pe.matmul(bank, k.whi[:, slot, wk, :], hi[:, xk, cols], start=first and a == 0, stop=False)
        pe.matmul(bank, k.whi[:, slot, wk, :], lo[:, xk, cols], start=False, stop=False)
        mm = pe.matmul(bank, k.wlo[:, slot, wk, :], hi[:, xk, cols], start=False, stop=last and a == len(ks) - 1)
    if counts:
        mm.then_inc(k.s_proj, int(counts))


def weight_split(k, block):
    nc = k.nc

    @block.gpsimd
    def _(pool):
        def one(slab, slot, round_, reuse):
            pool.wait_ge(k.s_raw[slot], (round_ + 1) * 16)
            if reuse:
                pool.wait_ge(k.s_proj, slab * 2 - 2)
            pool.sem_inc(k.s_begun, 1)
            pool.tensor_copy(k.whi[:, slot], k.raw[:, slot]).then_inc(k.s_hi, 1)
            pool.wait_ge(k.s_hi, slab + 1)
            pool.tensor_tensor(k.wlo[:, slot], k.raw[:, slot], k.whi[:, slot].bitcast(F32), ALU.subtract).then_inc(k.s_split, 1)

        one(0, 0, 0, False)
        one(1, 1, 0, False)
        with pool.Fori(1, N_SLABS // 2) as i:
            for s in range(2):
                one(i * 2 + s, s, i, True)
        if N_SLABS % 2:
            one(N_SLABS - 1, 0, N_SLABS // 2, True)


def load_slab(k, sp, wts, slab, slot, reuse):
    if reuse:
        sp.wait_ge(k.s_split, slab - 1)
    src = wts[slab] if isinstance(slab, int) else wts[ds(slab, 1)].rearrange("a p k m -> (a p) k m")
    sp.dma_start(k.raw[:, slot], src).then_inc(k.s_raw[slot], 16)




def softplus_dve(k, dve, act_exp_done, out, e, relu, s, s2, p):
    v = k.vstep
    dve.wait_ge(*act_exp_done)
    v.settle(dve, dve.tensor_scalar(s, e, 2.0, None, ALU.add))
    v.settle(dve, dve.reciprocal(s2, s))
    v.settle(dve, dve.tensor_tensor(s, e, s2, ALU.mult))
    v.settle(dve, dve.tensor_tensor(s2, s, s, ALU.mult))
    v.settle(dve, dve.tensor_scalar(p, s2, 2.0 / 19.0, None, ALU.mult))
    for n in range(17, 1, -2):
        v.settle(dve, dve.scalar_tensor_tensor(p, p, 2.0 / n, s2, ALU.add, ALU.mult))
    v.settle(dve, dve.scalar_tensor_tensor(p, p, 2.0, s, ALU.add, ALU.mult))
    v.settle(dve, dve.tensor_tensor(out, p, relu, ALU.add))


def rstd_stage(k, block, ssum, feats, bank0):
    n = k.norms
    k.norms += 1
    rows = ssum.shape[0]

    @block.tensor
    def _(pe):
        begin(k, pe)
        for j in range(TT):
            mm = pe.matmul(k.aux[:, bank0 + 1, j:j + 1], ssum[:, j * P:(j + 1) * P], k.ones[0:rows], start=True, stop=True)
        mm.then_inc(k.s_sum, 1)
        pe.wait_ge(k.s_col, n + 1)
        for j in range(TT):
            mm = pe.matmul(k.aux[:, bank0 + j // 4, (j % 4) * P:(j % 4 + 1) * P],
                           k.rstd[:, j:j + 1].to_broadcast([P, P]), k.ident, start=True, stop=True)
        mm.then_inc(k.s_spread, 1)

    @block.vector
    def _(dve):
        begin(k, dve)
        dve.wait_ge(k.s_sum, n + 1)
        dve.tensor_scalar(k.stat, k.aux[:, bank0 + 1, 0:TT], 1.0 / feats, EPS, ALU.mult, ALU.add).then_inc(k.s_var, 1)
        dve.wait_ge(k.s_var, 2 * n + 2)
        dve.reciprocal(k.rstd, k.stat).then_inc(k.s_col, 1)

    @block.scalar
    def _(act):
        begin(k, act)
        act.wait_ge(k.s_var, 2 * n + 1)
        act.activation(k.stat, k.stat, ACT.Sqrt).then_inc(k.s_var, 1)

    return n + 1, k.aux[:, bank0:bank0 + 2, :].rearrange("p a b -> p (a b)")


def sum_squares(k, pe, sq, t, bank0, s_sq, s_used):
    pe.wait_ge(s_sq, t + 1)
    for c in range(2):
        mm = pe.matmul(k.aux[0:1, bank0 + c, :], k.ones, sq[:, t % 2, c * HALF:(c + 1) * HALF], start=t == 0, stop=t == KT - 1)
    mm.then_inc(s_used, 1)


def sums_out(k, act, row, bank0, s_used):
    act.wait_ge(s_used, KT)
    act.activation(row, k.aux[0:1, bank0:bank0 + 2, :].rearrange("p a b -> p (a b)"), ACT.Copy)


def square_sum_stage(k, block, src, sq, ssum):
    s_sq, s_free = k.sem("x_squared"), k.sem("x_square_used")

    @block.scalar
    def _(act):
        begin(k, act)
        act.wait_ge(k.s_ones, 1)
        act.activation(k.rstd[:, 0:1], k.ones, ACT.Sqrt)
        for t in range(KT):
            act.wait_ge(k.s_x[t // X_TILES], 16)
            if t >= 2:
                act.wait_ge(s_free, t - 1)
            act.activation(ssum if t == 0 else sq[:, t % 2], src(t), ACT.Square).then_inc(s_sq, 1)
        end(k, act)

    @block.vector
    def _(dve):
        begin(k, dve)
        dve.wait_ge(s_sq, 1)
        for t in range(1, KT):
            dve.wait_ge(s_sq, t + 1)
            ins = dve.tensor_tensor(ssum, ssum, sq[:, t % 2], ALU.add)
            ins.then_inc(s_free, 2 if t == 1 else 1)
            dve.wait_ge(s_free, t + 1)
        end(k, dve)

    @block.tensor
    def _(pe):
        begin(k, pe)
        end(k, pe)

    k.stage += 1


def norm_split_stage(k, block, src, ssum, gain, shift, tmp):
    spread, rb = rstd_stage(k, block, ssum, D, 0)
    done = k.splits * KT
    k.splits += 1
    k.h_ready = (k.s_low, done)

    @block.tensor
    def _(pe):
        end(k, pe)

    @block.vector
    def _(dve):
        dve.wait_ge(k.s_spread, spread)

        def low(t):
            dve.wait_ge(k.s_high, done + t + 1)
            hi = k.hhi[:, t, :].bitcast(F32)
            if shift is None:
                ins = dve.tensor_tensor(k.hlo[:, t, :], tmp[:, t % 2], hi, ALU.subtract)
            else:
                ins = dve.scalar_tensor_tensor(k.hlo[:, t, :], tmp[:, t % 2], shift(t), hi, ALU.add, ALU.subtract)
            ins.then_inc(k.s_low, 1)

        for t in range(KT):
            if t >= 2:
                dve.wait_ge(k.s_low, done + t - 1)
            dve.scalar_tensor_tensor(tmp[:, t % 2], src(t), gain(t), rb, ALU.mult, ALU.mult).then_inc(k.s_normed, 1)
            if t >= 1:
                low(t - 1)
        low(KT - 1)
        end(k, dve)

    @block.scalar
    def _(act):
        for t in range(KT):
            act.wait_ge(k.s_normed, done + t + 1)
            if shift is None:
                ins = act.activation(k.hhi[:, t, :], tmp[:, t % 2], ACT.Copy)
            else:
                ins = act.activation(k.hhi[:, t, :], tmp[:, t % 2], ACT.Identity, bias=shift(t))
            ins.then_inc(k.s_high, 1)
        end(k, act)

    k.stage += 1




def setup_stage(k, block, xT, params, consts, wts):
    k.xt = k.at("x_first", k.W, [P, KT, T])
    k.s_par = k.sem("params_loaded")
    k.s_ones = k.sem("ones_made")
    k.lamt = k.at("lambda_tmp", k.Y, [P, 8])
    k.one64 = k.at("ones_square", k.Y + 1, [P, P])

    @block.sync
    def _(sp):
        for i in range(KT // X_TILES):
            sp.dma_start(k.xt[:, i * X_TILES:(i + 1) * X_TILES], xT[i * X_TILES:(i + 1) * X_TILES].rearrange("k p t -> p k t")).then_inc(k.s_x[i], 16)
        load_slab(k, sp, wts, 0, 0, False)
        load_slab(k, sp, wts, 1, 1, False)

    @block.scalar
    def _(act):
        act.dma_start(k.par[:], params).then_inc(k.s_par, 16)
        act.dma_start(k.const[:], consts).then_inc(k.s_par, 16)

    @block.vector
    def _(dve):
        dve.memset(k.ones, 1.0).then_inc(k.s_ones, 1)
        dve.memset(k.one64[:], 1.0).then_inc(k.s_ones, 1)


def params_in(k, block):

    @block.vector
    def _(dve):
        dve.wait_ge(k.s_par, 32)
        dve.wait_ge(k.s_ones, 2)


def vectors_stage(k, block):
    tmp = k.at("setup_tmp", k.Y + 0.25, [P, 7, 8])
    k.s_vec, s_e = k.sem("vectors_made"), k.sem("vectors_exp")
    x, ab, e, relu, s, s2, p = (tmp[:, i] for i in range(7))

    @block.scalar
    def _(act):
        act.wait_ge(k.s_par, 32)
        act.activation(k.cond, param(k, "c", 0, 8), ACT.Silu).then_inc(s_e, 1)
        act.activation(ab, param(k, "lru_lam", 0, 8), ACT.Abs).then_inc(s_e, 1)
        act.wait_ge(s_e, 2)
        act.activation(e, ab, ACT.Exp, scale=-1.0).then_inc(s_e, 1)

    @block.vector
    def _(dve):
        dve.tensor_copy(k.mask.rearrange("p a b -> p (a b)"), k.const[:, IDENT:CAUSAL + P])
        dve.tensor_tensor(k.lamt[0:QK, 2:4], param(k, "lq", 0, 2)[0:QK], param(k, "lk", 0, 2)[0:QK], ALU.mult).then_inc(k.s_vec, 1)
        dve.tensor_scalar(k.subg, param(k, "subln_g"), 1.0 - LAM_INIT, None, ALU.mult)
        k.vstep.settle(dve, dve.tensor_scalar(relu, param(k, "lru_lam", 0, 8), -1.0, 0.0, ALU.mult, ALU.max))
        softplus_dve(k, dve, (s_e, 3), x, e, relu, s, s2, p)
        dve.tensor_scalar(k.cn, x, -8.0, None, ALU.mult)
        dve.tensor_scalar(k.ncn, x, 8.0, None, ALU.mult).then_inc(k.s_vec, 1)
        dve.wait_ge(k.s_vec, 2)




def lru_stage(k, block, wts, gate_w, ada_w):
    xpad = k.at("lru_x", k.W, [P, T + 8])
    xc, r, g, a, u = (k.at(n, k.W + 4.25 + 4 * i, [P, T]) for i, n in enumerate(("lru_conv", "lru_r", "lru_i", "lru_a", "lru_u")))
    gw_all = k.at("gate_w_all", k.W + 24.25, [P, LRU_BLOCKS, 2, P])
    gw = k.at("gate_w", k.W + 32.25, [P, 2, P])
    adaw = k.at("ada_w", k.W + 33.25, [P, 2, ADA_COLS])
    acc = k.at("ada_acc", k.W + 39.25, [P, ADA_COLS])
    k.y = k.at("y", k.Y, [P, 2 * KT, T])
    s_gw, s_ada, s_ada_used = k.sem("gate_w_loaded"), [k.sem(f"ada_loaded_{i}") for i in range(2)], k.sem("ada_used")
    s_evac, s_conv, s_gates, s_sig = k.sem("lru_evacuated"), k.sem("lru_conv_made"), k.sem("lru_gates"), k.sem("lru_sigmoids")
    s_au, s_m2, s_mult, s_col, s_y = k.sem("lru_a_made"), k.sem("lru_m2"), k.sem("lru_root"), k.sem("ada_columns"), k.sem("lru_y_made")
    v = k.vstep
    h_ready = k.h_ready
    s_lam = k.sem("lambda_summed")
    k.banks_read = (s_evac, 2 * LRU_SLABS + 2)
    EV, AD = 2, 6

    @block.sync
    def _(sp):
        with sp.Fori(0, LRU_BLOCKS) as n:
            for s in range(2):
                load_slab(k, sp, wts, n * 2 + (2 + s), s, True)
            for kt in range(KT):
                sp.wait_ge(s_ada_used, n * KT + (kt + 2))
                sp.dma_start(adaw[:, kt % 2], ada_w[ds(n, 1), kt].rearrange("a p m -> (a p) m")).then_inc(s_ada[kt % 2], 16)

    @block.tensor
    def _(pe):
        def columns(n):
            pe.wait_ge(s_ada_used, n * KT + 3)
            pe.wait_ge(s_col, n * 2 + 1)
            for j in range(AD):
                mm = pe.matmul(k.aux[:, 4, j:j + 1], acc[:, j * P:(j + 1) * P], k.ones, start=True, stop=True)
            mm.then_inc(s_col, 1)

        pe.sem_inc(s_evac, EV)
        with pe.Fori(0, LRU_BLOCKS) as n:
            for s in range(2):
                for c in range(2):
                    pe.wait_ge(s_evac, n * 4 + (2 * s + c + 1))
                    project(k, pe, n * 2 + (LRU_0 + s), s, c, k.bank[c][:], k.hhi, k.hlo, ready=h_ready)
                    if s == 1 and c == 0:
                        columns(n)
            pe.wait_ge(s_conv, n + 2)
            pe.wait_ge(s_sig, n + 1)
            for i in range(2):
                for c in range(2):
                    mm = pe.matmul(k.aux[:, 2 * i + c, :], gw[:, i, :], xc[:, c * HALF:(c + 1) * HALF], start=True, stop=True)
            mm.then_inc(s_gates, 1)
        end(k, pe)

        def last_sums():
            columns(LRU_BLOCKS)
            pe.wait_ge(k.s_vec, 1)
            pe.matmul(k.aux[:, 5, 0:2], k.one64[0:QK, :], k.lamt[0:QK, 2:4], start=True, stop=True).then_inc(s_lam, 1)

        k.last_sums = last_sums

    @block.scalar
    def _(act):
        begin(k, act)
        act.wait_ge(k.s_vec, 2)
        act.dma_start(gw_all[:], gate_w).then_inc(s_gw, 16)
        act.sem_inc(s_sig, 1)
        flat = k.aux[:].rearrange("p a b -> p (a b)")

        def x_in(n, c):
            act.wait_ge(s_conv, n + 1)
            act.wait_ge(k.s_proj, n * 4 + (2 * LRU_0 + c + 1))
            act.activation(xpad[:, 3 + c * HALF:3 + (c + 1) * HALF], k.bank[c][:], ACT.Copy).then_inc(s_evac, 1)

        def rest(n, last):
            for c in range(2):
                act.wait_ge(k.s_proj, n * 4 + (2 * LRU_0 + 3 + c))
                act.activation(k.y[:, ds(n + KT, 1), c * HALF:(c + 1) * HALF].rearrange("p a b -> p (a b)"),
                               k.bank[c][:], ACT.Silu).then_inc(s_evac, 1)
            act.wait_ge(s_gates, n + 1)
            act.wait_ge(s_y, n + 1)
            act.activation(r[:], flat[:, 0:T], ACT.Sigmoid, bias=param_dyn(k, "b_r", n))
            act.activation(g[:], flat[:, T:2 * T], ACT.Sigmoid, bias=param_dyn(k, "b_i", n)).then_inc(s_sig, 1)
            act.wait_ge(s_sig, n + 2)
            act.activation(a[:], r[:], ACT.Exp, scale=k.cn[:, ds(n, 1)])
            act.activation(u[:], r[:], ACT.Tanh, scale=k.ncn[:, ds(n, 1)]).then_inc(s_au, 1)
            if not last:
                x_in(n + 1, 0)
            act.wait_ge(s_m2, n + 1)
            act.activation(r[:], u[:], ACT.Sqrt).then_inc(s_mult, 1)
            if not last:
                x_in(n + 1, 1)

        for c in range(2):
            x_in(0, c)
        with act.Fori(0, LRU_BLOCKS - 1) as n:
            rest(n, False)
        rest(LRU_BLOCKS - 1, True)
        act.wait_ge(s_lam, 1)
        act.activation(k.lamt[:, 0:2], k.aux[:, 5, 0:2], ACT.Exp).then_inc(s_lam, 1)
        end(k, act)

    @block.vector
    def _(dve):
        begin(k, dve)
        dve.sem_inc(s_ada_used, 2)
        dve.memset(acc[:], 0.0).then_inc(s_ada_used, 1)
        dve.sem_inc(s_conv, 1)
        dve.sem_inc(s_y, 1)
        dve.sem_inc(s_col, 1)
        v.settle(dve, dve.memset(xpad[:, 0:3], 0.0))
        dve.wait_ge(s_gw, 16)

        def columns(n):
            dve.wait_ge(s_col, n * 2 + 2)
            b0, _ = PARAM_COLS["b_ada"]
            ins = dve.tensor_tensor(k.mod_all[:, ds(n * AD, AD)], k.aux[:, 4, 0:AD], k.par[:, ds(n * AD + (b0 - AD), AD)], ALU.add)
            ins.then_inc(s_col, 1)

        def modulation(n, pieces):
            for kt in pieces:
                dve.wait_ge(s_ada[kt % 2], n * 64 + 16 * (kt // 2 + 1))
                if kt == 0:
                    ins = dve.tensor_scalar(acc[:], adaw[:, 0], k.cond[:, 0:1], None, ALU.mult)
                else:
                    ins = dve.scalar_tensor_tensor(acc[:], adaw[:, kt % 2], k.cond[:, kt:kt + 1], acc[:], ALU.mult, ALU.add)
                ins.then_inc(s_ada_used, 1)
                dve.wait_ge(s_ada_used, n * KT + (kt + 4))

        with dve.Fori(0, LRU_BLOCKS) as n:
            v.enter(n, 7)
            dve.wait_ge(s_evac, n * 4 + (EV + 2))
            dve.tensor_copy(gw[:], gw_all[:, ds(n, 1)].rearrange("p a i d -> p (a i) d"))
            v.settle(dve, dve.tensor_scalar(xc[:], xpad[:, 0:T], param_dyn(k, "conv1_w", n, TAPS), param_dyn(k, "conv1_b", n), ALU.mult, ALU.add))
            for tap in range(1, TAPS):
                a0, _ = PARAM_COLS["conv1_w"]
                ins = dve.scalar_tensor_tensor(xc[:], xpad[:, tap:tap + T], k.par[:, ds(n * TAPS + (a0 + tap), 1)], xc[:], ALU.mult, ALU.add)
                if tap < TAPS - 1:
                    v.settle(dve, ins)
            ins.then_inc(s_conv, 1)
            columns(n)
            modulation(n, range(KT - 2))
            dve.wait_ge(s_au, n + 1)
            v.settle(dve, dve.tensor_tensor(r[:], a[:], a[:], ALU.mult))
            ins = dve.scalar_tensor_tensor(u[:], r[:], 1.0, u[:], ALU.add, ALU.mult)
            ins.then_inc(s_m2, 1)
            v.settle(dve, dve.tensor_tensor(g[:], g[:], xc[:], ALU.mult))
            modulation(n, range(KT - 2, KT))
            dve.wait_ge(s_mult, n + 1)
            ins = dve.tensor_tensor(g[:], g[:], r[:], ALU.mult)
            v.settle(dve, ins)
            v.settle(dve, dve.tensor_tensor_scan(u[:], a[:], g[:], 0.0, ALU.mult, ALU.add))
            dve.wait_ge(s_evac, n * 4 + (EV + 4))
            yt = k.y[:, ds(n + KT, 1), :].rearrange("p a b -> p (a b)")
            dve.tensor_tensor(yt, u[:], yt, ALU.mult).then_inc(s_y, 1)
        v.leave(LRU_BLOCKS)
        columns(LRU_BLOCKS)
        dve.wait_ge(s_lam, 2)
        v.settle(dve, dve.tensor_scalar(k.lamt[:, 4:5], k.lamt[:, 1:2], -1.0, LAM_INIT, ALU.mult, ALU.add))
        dve.tensor_tensor(k.lam, k.lamt[:, 4:5], k.lamt[:, 0:1], ALU.add)
        end(k, dve)

    k.stage += 1




def attention_stage(k, block):
    qt = k.at("att_q", k.W, [P, 2, T])
    kt = k.at("att_k", k.W + 8, [P, 2, T])
    vtok = k.at("att_v", k.W + 16, [P, 2, TT, P])
    vt = k.at("att_v_features", k.W + 24, [P, T])
    p = k.at("att_p", k.W + 28, [P, 2, T])
    wt = k.at("att_w_turned", k.W + 36, [P, TT, P])
    o = k.at("att_o", k.W + 40, [P, T])
    sq = k.at("att_o_squared", k.W + 44, [P, T])
    nmax, total, inv, lr = (k.small[:, 48 + 4 * i:50 + 4 * i] for i in range(4))
    mx = k.small[:, 64:66]
    score, turn, out = k.aux[:, 0:4, :], k.aux[:, 4, :], k.aux[:, 5, :]
    s_evac = k.sem("att_evacuated")
    s_score = k.sem("att_scored")
    s_nmax = k.sem("att_max")
    s_exp = k.sem("att_exp")
    s_w = k.sem("att_w")
    s_turned, s_turn_free = k.sem("att_turned"), k.sem("att_turn_read")
    s_out, s_out_free = k.sem("att_out"), k.sem("att_out_read")
    s_sq, s_root = k.sem("att_squared"), k.sem("att_root")
    s_var, s_col = k.sem("att_var"), k.sem("att_rstd")
    s_y = k.sem("att_y")
    k.yhi = k.at("y_hi", k.H, [P, 2 * KT, T], F32R)
    k.ylo = k.at("y_lo", k.Y, [P, 2 * KT, T], F32R)
    k.s_yhi, k.s_ylo = k.sem("y_high"), k.sem("y_low")
    SCALE = QK ** -0.5
    STATS, SPREADS, VALUES = 1, (2, 3), (6, 7)
    GROUPS = [-(-(i + 1) // 4) for i in range(TT)]
    FIRST, EACH = 2, sum(GROUPS) + 5

    def uses(h):
        return FIRST if isinstance(h, int) and h == 0 else h * EACH + (FIRST - 3)

    class Turns:

        def __init__(self, h):
            self.start, self.n = uses(h), 0

        def next(self):
            self.n += 1
            return self.start + self.n

        def done(self):
            return self.start + self.n

    def heads(eng, one):
        one(0, 0, False, True)
        with eng.Fori(0, (HEADS - 2) // 2) as m:
            for b in range(2):
                one(m * 2 + (1 + b), 1 - b, True, True)
        one(HEADS - 1, 1, True, False)

    @block.tensor
    def _(pe):
        pe.wait_ge(*k.banks_read)
        pe.sem_inc(s_evac, 2)

        def half(h, i):
            use = h * 8 + i
            pe.wait_ge(s_evac, use + 1)
            project(k, pe, h * 4 + (ATT_0 + i // 2), (i // 2) % 2, i % 2, k.bank[i % 2][:], k.hhi, k.hlo)

        def scores(h, par, i, step):
            if i == 0:
                pe.wait_ge(s_evac, h * 8 + (2 + 4))
            pe.wait_ge(s_exp, step * 2 + 2)
            keys = (i + 1) * P
            for c in range(2):
                rows = slice(c * QK, (c + 1) * QK)
                q = qt[rows, par, i * P:(i + 1) * P]
                for a in range(0, i * P, HALF):
                    n = min(HALF, i * P - a)
                    pe.matmul(score[:, 2 * c + a // HALF, 0:n], q, kt[rows, par, a:a + n], start=True, stop=True)
                a = (i * P) % HALF
                own = score[:, 2 * c + i * P // HALF, a:a + P]
                pe.matmul(own, q, kt[rows, par, i * P:keys], start=True, stop=False)
                mm = pe.matmul(own, k.mask[:, 0], k.mask[:, 1], start=False, stop=True)
                mm.then_inc(s_score, 1)

        def turn_group(turns, ins):
            pe.wait_ge(s_turn_free, turns.next())
            for a, x in enumerate(ins):
                mm = pe.transpose(turn[:, a * P:(a + 1) * P], x, k.ident)
            mm.then_inc(s_turned, 1)

        def values(turns, h, a):
            pe.wait_ge(s_evac, h * 8 + (2 + 6))
            turn_group(turns, [vt[:, j * P:(j + 1) * P] for j in range(4 * a, 4 * a + 4)])

        def statistics(turns, h):
            pe.wait_ge(s_sq, h + 1)
            pe.wait_ge(s_turn_free, turns.next())
            for j in range(TT):
                mm = pe.matmul(turn[:, j:j + 1], sq[:, j * P:(j + 1) * P], k.ones, start=True, stop=True)
            mm.then_inc(s_turned, 1)

        def spread(turns, h, a):
            pe.wait_ge(s_col, h + 1)
            pe.wait_ge(s_turn_free, turns.next())
            for j in range(4):
                mm = pe.matmul(turn[:, j * P:(j + 1) * P], k.rstd[:, 4 * a + j:4 * a + j + 1].to_broadcast([P, P]),
                               k.ident, start=True, stop=True)
            mm.then_inc(s_turned, 1)

        def recurrent(t):
            if t == 0:
                pe.wait_ge(s_evac, HEADS * 8 + 2)
            pe.wait_ge(k.s_ylo, t + 1)
            for c in range(2):
                project(k, pe, OUT1_0 + 1, 1, c, k.bank[c][:], k.yhi, k.ylo, [(t, t + KT)], first=t == 0, last=False, counts=False)

        def one(h, par, after, more):
            turns = Turns(h)
            for i in range(TT):
                pe.wait_ge(s_w, h * TT + (i + 1))
                for a in range(0, i + 1, 4):
                    turn_group(turns, [p[:, 0, j * P:(j + 1) * P] for j in range(a, min(a + 4, i + 1))])
                    if a == 0:
                        if i < TT - 1:
                            scores(h, par, i + 1, h * TT + (i + 1))
                        elif more:
                            scores(h + 1, 1 - par, 0, h * TT + TT)
                turned = turns.done()
                if after and i == STATS:
                    statistics(turns, h - 1)
                if more:
                    half(h + 1, i)
                else:
                    recurrent(i)
                if after and i in SPREADS:
                    spread(turns, h - 1, i - SPREADS[0])
                if more and i in VALUES:
                    values(turns, h + 1, i - VALUES[0])
                if i % 4 == 0:
                    pe.wait_ge(s_out_free, h * 2 + (i // 4 + 1))
                pe.wait_ge(s_turn_free, turned + 1)
                for j in range(i + 1):
                    mm = pe.matmul(out[:, (i % 4) * P:(i % 4 + 1) * P], vtok[:, par, j, :], wt[:, j, :], start=j == 0, stop=j == i)
                if i % 4 == 3:
                    mm.then_inc(s_out, 1)

        for i in range(8):
            half(0, i)
            if i == 1:
                k.last_sums()
        first = Turns(0)
        first.start = 0
        for a in range(2):
            values(first, 0, a)
        scores(0, 0, 0, 0)
        heads(pe, one)
        last = Turns(HEADS)
        last.start = uses(HEADS) - 2
        statistics(last, HEADS - 1)
        for a in range(2):
            spread(last, HEADS - 1, a)
        end(k, pe)

    @block.scalar
    def _(act):
        begin(k, act)
        act.sem_inc(s_exp, 2)
        act.sem_inc(s_out_free, 1)

        def half(h, par, i):
            act.wait_ge(k.s_proj, h * 8 + (2 * ATT_0 + i + 1))
            cols = slice((i % 2) * HALF, (i % 2 + 1) * HALF)
            bank = k.bank[i % 2][:]
            if i // 2 == 3:
                ins = act.activation(k.y[:, ds(h, 1), cols].rearrange("p a b -> p (a b)"), bank, ACT.Silu)
            else:
                ins = act.activation((qt[:, par, cols], kt[:, par, cols], vt[:, cols])[i // 2], bank, ACT.Copy)
            ins.then_inc(s_evac, 1)

        def softmax(step, i, used):
            keys = (i + 1) * P
            act.wait_ge(s_nmax, step + 1)
            act.wait_ge(s_turned, used)
            flat = score.rearrange("p (c a) b -> p c (a b)", c=2)
            for c in range(2):
                act.activation(p[:, c, 0:keys], flat[:, c, 0:keys], ACT.Exp, bias=nmax[:, c:c + 1], scale=SCALE,
                               accum_out=total[:, c:c + 1]).then_inc(s_exp, 1)

        def square(h):
            act.wait_ge(s_out_free, h * 2 + 3)
            act.activation(sq[:], o[:], ACT.Square).then_inc(s_sq, 1)

        def root(h):
            act.wait_ge(s_var, h + 1)
            act.activation(k.stat, k.stat, ACT.Sqrt).then_inc(s_root, 1)

        def high(t):
            act.activation(k.yhi[:, KT + t, :], k.y[:, KT + t, :], ACT.Copy).then_inc(k.s_yhi, 1)

        def one(h, par, after, more):
            used = uses(h)
            if not more:
                high(0)
            for i in range(TT):
                used = used + GROUPS[i]
                if i < TT - 1:
                    softmax(h * TT + (i + 1), i + 1, used)
                elif more:
                    softmax(h * TT + TT, 0, used)
                if more:
                    half(h + 1, 1 - par, i)
                elif i < TT - 1:
                    high(i + 1)
                if i % 4 == 3:
                    act.wait_ge(s_out, h * 2 + (i // 4 + 1))
                    if i == 3:
                        act.wait_ge(s_y, h + 1)
                    act.activation(o[:, (i // 4) * HALF:(i // 4 + 1) * HALF], out, ACT.Copy).then_inc(s_out_free, 1)
                if after and i == STATS:
                    root(h - 1)
                    used = used + 1
                if after and i in SPREADS:
                    used = used + 1
                if more and i in VALUES:
                    used = used + 1
            square(h)

        for i in range(8):
            half(0, 0, i)
        softmax(0, 0, 2)
        heads(act, one)
        root(HEADS - 1)
        end(k, act)

    @block.vector
    def _(dve):
        begin(k, dve)
        dve.sem_inc(s_turn_free, 1)
        dve.sem_inc(s_y, 1)
        v = k.vstep

        def maxima(step, i):
            keys = (i + 1) * P
            flat = score.rearrange("p (c a) b -> p c (a b)", c=2)
            for c in range(2):
                dve.wait_ge(s_score, step * 2 + (c + 1))
                ins = dve.tensor_reduce(mx[:, c:c + 1], flat[:, c, 0:keys], AX, ALU.max)
            v.settle(dve, ins)
            dve.tensor_scalar(nmax, mx, -SCALE, None, ALU.mult).then_inc(s_nmax, 1)

        def weights(step, i):
            keys = (i + 1) * P
            dve.wait_ge(s_exp, step * 2 + 4)
            v.settle(dve, dve.reciprocal(inv, total))
            v.settle(dve, dve.tensor_scalar(lr[:, 0:1], inv[:, 1:2], k.lam, None, ALU.mult))
            v.settle(dve, dve.tensor_scalar(p[:, 1, 0:keys], p[:, 1, 0:keys], lr[:, 0:1], None, ALU.mult))
            dve.scalar_tensor_tensor(p[:, 0, 0:keys], p[:, 0, 0:keys], inv[:, 0:1], p[:, 1, 0:keys], ALU.mult, ALU.subtract).then_inc(s_w, 1)

        def turned(turns):
            dve.wait_ge(s_turned, turns.next())

        def values(turns, par, a):
            turned(turns)
            dve.tensor_copy(vtok[:, par, 4 * a:4 * a + 4, :].rearrange("p a b -> p (a b)"), turn).then_inc(s_turn_free, 1)

        def statistics(turns, h):
            turned(turns)
            dve.tensor_scalar(k.stat, turn[:, 0:TT], 1.0 / P, EPS, ALU.mult, ALU.add).then_inc(s_turn_free, 1)
            dve.wait_ge(s_turn_free, turns.done() + 1)
            dve.sem_inc(s_var, 1)

        def inverse(h):
            dve.wait_ge(s_root, h + 1)
            dve.reciprocal(k.rstd, k.stat).then_inc(s_col, 1)

        def spread(turns, h, a):
            cols = slice(a * HALF, (a + 1) * HALF)
            yt = k.y[:, ds(h, 1), cols].rearrange("p a b -> p (a b)")
            turned(turns)
            ins = dve.scalar_tensor_tensor(o[:, cols], o[:, cols], k.subg, turn, ALU.mult, ALU.mult)
            ins.then_inc(s_turn_free, 1)
            dve.wait_ge(s_turn_free, turns.done() + 1)
            ins = dve.tensor_tensor(yt, yt, o[:, cols], ALU.mult)
            if a == 1:
                ins.then_inc(s_y, 1)

        def low(t):
            dve.wait_ge(k.s_yhi, t + 1)
            dve.tensor_tensor(k.ylo[:, KT + t, :], k.y[:, KT + t, :], k.yhi[:, KT + t, :].bitcast(F32), ALU.subtract).then_inc(k.s_ylo, 1)

        def one(h, par, after, more):
            turns = Turns(h)
            if not more:
                low(0)
            for i in range(TT):
                step, nxt = (h * TT + (i + 1), i + 1) if i < TT - 1 else (h * TT + TT, 0)
                goes_on = i < TT - 1 or more
                for a in range(0, i + 1, 4):
                    n = min(4, i + 1 - a)
                    turned(turns)
                    dve.tensor_copy(wt[:, a:a + n, :].rearrange("p a b -> p (a b)"), turn[:, 0:n * P]).then_inc(s_turn_free, 1)
                    if a == 0 and goes_on:
                        maxima(step, nxt)
                if after and i == STATS:
                    statistics(turns, h - 1)
                if goes_on:
                    weights(step, nxt)
                    if not more:
                        low(i + 1)
                if after and i in SPREADS:
                    spread(turns, h - 1, i - SPREADS[0])
                if more and i in VALUES:
                    values(turns, 1 - par, i - VALUES[0])
                if after and i == STATS:
                    inverse(h - 1)

        first = Turns(0)
        first.start = 0
        for a in range(2):
            values(first, 0, a)
        maxima(0, 0)
        weights(0, 0)
        one(0, 0, False, True)
        with dve.Fori(0, (HEADS - 2) // 2) as m:
            v.enter(m, 2 * TT * 4)
            for b in range(2):
                one(m * 2 + (1 + b), 1 - b, True, True)
        v.leave((HEADS - 2) // 2)
        one(HEADS - 1, 1, True, False)
        last = Turns(HEADS)
        last.start = uses(HEADS) - 2
        statistics(last, HEADS - 1)
        inverse(HEADS - 1)
        for a in range(2):
            spread(last, HEADS - 1, a)
        end(k, dve)

    k.stage += 1




def out_project_stage(k, block):
    k.o1 = k.at("out1", k.W, [P, KT, T])
    sq = k.at("out1_squared", k.W + 32, [P, T])
    k.ssum = k.at("out1_sum", k.W + 36, [P, T])
    s_evac, s_added = k.sem("out1_evacuated"), k.sem("out1_added")

    @block.tensor
    def _(pe):
        begin(k, pe)
        for c in range(2):
            project(k, pe, OUT1_0, 0, c, k.bank[c][:], k.yhi, k.ylo, first=False, ready=(k.s_ylo, KT),
                    counts=4 * c)
        with pe.Fori(0, KT - 1) as f:
            for s in range(2):
                for c in range(2):
                    if s == 0:
                        pe.wait_ge(s_evac, f * 2 + (c + 3))
                    project(k, pe, f * 2 + (OUT1_0 + 2 + s), s, c, k.bank[c][:], k.yhi, k.ylo,
                            [(i, i + KT * s) for i in range(KT)], s == 0, s == 1)
        end(k, pe)

    @block.scalar
    def _(act):
        begin(k, act)
        act.sem_inc(s_evac, 2)
        for t in range(KT):
            act.activation(k.yhi[:, t, :], k.y[:, t, :], ACT.Copy).then_inc(k.s_yhi, 1)
        with act.Fori(0, KT) as f:
            act.wait_ge(s_added, f + 1)
            for c in range(2):
                cols = slice(c * HALF, (c + 1) * HALF)
                act.wait_ge(k.s_proj, f * 4 + (2 * OUT1_0 + 3 + c))
                act.activation(sq[:, cols], k.bank[c][:], ACT.Square)
                act.activation(k.o1[:, ds(f, 1), cols].rearrange("p a b -> p (a b)"), k.bank[c][:], ACT.Copy).then_inc(s_evac, 1)
        end(k, act)

    @block.vector
    def _(dve):
        begin(k, dve)
        for t in range(KT):
            dve.wait_ge(k.s_yhi, KT + t + 1)
            dve.tensor_tensor(k.ylo[:, t, :], k.y[:, t, :], k.yhi[:, t, :].bitcast(F32), ALU.subtract).then_inc(k.s_ylo, 1)
        dve.memset(k.ssum, 0.0).then_inc(s_added, 1)
        with dve.Fori(0, KT) as f:
            dve.wait_ge(s_added, f + 1)
            dve.wait_ge(s_evac, f * 2 + 4)
            dve.tensor_tensor(k.ssum, k.ssum, sq, ALU.add).then_inc(s_added, 1)
        end(k, dve)

    k.stage += 1


def post_norm_stage(k, block, xT):
    spread, rb = rstd_stage(k, block, k.ssum, D, 0)
    xr = k.at("x_again", k.H, [P, KT, T])
    k.x1 = k.at("x1", k.Y, [P, KT, T])
    tmp = k.at("post_tmp", k.W + 40, [P, 2, T])
    sq = k.at("x1_squared", k.Y + 32, [P, 2, T])
    k.ssum1 = k.at("x1_sum", k.Y + 40, [1, T])
    s_t, s_x1, s_sq, s_add = k.sem("post_normed"), k.sem("x1_made"), k.sem("x1_squares"), k.sem("x1_added")

    @block.tensor
    def _(pe):
        for t in range(KT):
            sum_squares(k, pe, sq, t, 2, s_sq, s_add)
        end(k, pe)

    @block.scalar
    def _(act):
        for i in range(KT // X_TILES):
            act.dma_start(xr[:, i * X_TILES:(i + 1) * X_TILES], xT[i * X_TILES:(i + 1) * X_TILES].rearrange("k p t -> p k t")).then_inc(k.s_x[i], 16)
        for t in range(KT):
            act.wait_ge(s_x1, t + 1)
            act.dma_start(k.x1d[t], k.x1[:, t]).then_inc(k.s_spill, 16)
            if t >= 2:
                act.wait_ge(s_add, t - 1)
            act.activation(sq[:, t % 2], k.x1[:, t], ACT.Square).then_inc(s_sq, 1)
        sums_out(k, act, k.ssum1, 2, s_add)
        end(k, act)

    @block.vector
    def _(dve):
        dve.wait_ge(k.s_spread, spread)

        for t in range(KT):
            dve.scalar_tensor_tensor(tmp[:, t % 2], k.o1[:, t, :], param(k, "post_g", t), rb, ALU.mult, ALU.mult).then_inc(s_t, 1)
            dve.wait_ge(s_t, t + 1)
            dve.wait_ge(k.s_x[t // X_TILES], 32)
            dve.tensor_tensor(k.x1[:, t], tmp[:, t % 2], xr[:, t], ALU.add).then_inc(s_x1, 1)
        end(k, dve)

    k.stage += 1


def rest_of_slabs(k, block, wts):

    @block.sync
    def _(sp):
        with sp.Fori(LRU_SLABS // 2 + 1, N_SLABS // 2) as i:
            for q in range(2):
                load_slab(k, sp, wts, i * 2 + q, q, True)
        if N_SLABS % 2:
            load_slab(k, sp, wts, N_SLABS - 1, 0, True)


def block2_gains(k, block):
    k.gain1, k.gain2 = k.small[:, 72:80], k.small[:, 80:88]
    s_gain = k.sem("gains_made")

    @block.vector
    def _(dve):
        dve.scalar_tensor_tensor(k.gain1, k.mod[:, 8:16], 1.0, param(k, "norm1", 0, 8), ALU.add, ALU.mult).then_inc(s_gain, 1)
        dve.scalar_tensor_tensor(k.gain2, k.mod[:, 32:40], 1.0, param(k, "norm2", 0, 8), ALU.add, ALU.mult).then_inc(s_gain, 1)
        dve.wait_ge(s_gain, 2)


def ssd_norm_stage(k, block):
    F = k.F
    k.shi = k.at("ssd_y_hi", F + 48, [P, KT, T], F32R)
    k.slo = k.at("ssd_y_lo", F + 80, [P, KT, T], F32R)
    tmp = k.at("ssd_normed", F, [P, 2, T])
    GT = KT // 2
    s_var, s_root, s_col, s_b = (k.sem(f"ssd_norm_{n}") for n in ("var", "root", "rstd", "spread"))
    s_h, s_hi, k.s_slo = k.sem("ssd_normed"), k.sem("ssd_high"), k.sem("ssd_low")
    stat, rstd = k.small[:, 27:43], k.small[:, 100:116]

    @block.tensor
    def _(pe):
        begin(k, pe)
        pe.wait_ge(s_col, 1)
        for g in range(2):
            for j in range(TT):
                mm = pe.matmul(k.aux[:, 2 * g + j // 4, (j % 4) * P:(j % 4 + 1) * P],
                               rstd[:, g * TT + j:g * TT + j + 1].to_broadcast([P, P]), k.ident, start=True, stop=True)
            mm.then_inc(s_b, 1)
        end(k, pe)

    @block.scalar
    def _(act):
        begin(k, act)
        act.wait_ge(s_var, 1)
        act.activation(stat, stat, ACT.Sqrt).then_inc(s_root, 1)
        for t in range(KT):
            act.wait_ge(s_h, t + 1)
            act.activation(k.shi[:, t], tmp[:, t % 2], ACT.Copy).then_inc(s_hi, 1)
        end(k, act)

    @block.vector
    def _(dve):
        begin(k, dve)
        dve.tensor_scalar(stat, k.gsum, 1.0 / (GT * P), EPS, ALU.mult, ALU.add).then_inc(s_var, 1)
        dve.wait_ge(s_root, 1)
        dve.reciprocal(rstd, stat).then_inc(s_col, 1)

        def low(t):
            dve.wait_ge(s_hi, t + 1)
            dve.tensor_tensor(k.slo[:, t], tmp[:, t % 2], k.shi[:, t].bitcast(F32), ALU.subtract).then_inc(k.s_slo, 1)

        for t in range(KT):
            if t % GT == 0:
                dve.wait_ge(s_b, t // GT + 1)
            if t >= 2:
                dve.wait_ge(k.s_slo, t - 1)
            rb = k.aux[:, 2 * (t // GT):2 * (t // GT) + 2, :].rearrange("p a b -> p (a b)")
            dve.scalar_tensor_tensor(tmp[:, t % 2], k.cv[:, 4 + t], param(k, "ssd_norm", t), rb, ALU.mult, ALU.mult).then_inc(s_h, 1)
            if t >= 1:
                low(t - 1)
        low(KT - 1)
        end(k, dve)

    k.stage += 1




def ssd_inputs_stage(k, block):
    F = k.F
    k.cv = k.at("ssd_conv_out", F, [P, CV_TILES, T])
    xpad = k.at("ssd_x", F + 48, [P, 2, T + 8])
    cx = k.at("ssd_conv", F + 57, [P, 2, T])
    COLS = CHUNKS * SSD_HEADS
    dt_rows, acr = k.at("dt_rows", F + 66, [SSD_HEADS, T]), k.at("decay_rows", F + 92, [SSD_HEADS, T])
    e, relu, s, s2, p, dta = (k.at(n, F + 74 + 0.5 * i, [P, COLS]) for i, n in enumerate(
        ("dt_exp", "dt_relu", "dt_s", "dt_s2", "dt_poly", "dt_decay")))
    a_exp = k.at("a_exp", F + 78, [P, SSD_HEADS])
    k.dtc, k.acol, k.dlast = (k.at(n, 28.25 + 0.5 * i, [P, CHUNKS, SSD_HEADS]) for i, n in enumerate(("dt_cols", "decay_cols", "to_chunk_end")))
    k.cdec, k.eac = (k.at(n, F + 112 + 0.5 * i, [P, CHUNKS, SSD_HEADS]) for i, n in enumerate(("chunk_decay", "from_chunk_start")))
    h_ready = k.h_ready
    s_evac, s_conv, s_silu = k.sem("ssd_evacuated"), k.sem("ssd_convolved"), k.sem("ssd_silu")
    s_dt, s_exp, s_relu, s_dta = k.sem("dt_turned"), k.sem("dt_exponentials"), k.sem("dt_relu_made"), k.sem("dt_decays")
    s_cols, s_read, s_diff, s_dec = k.sem("decays_summed"), k.sem("decays_read"), k.sem("decay_diff"), k.sem("decays_made")
    k.s_acd = k.sem("decay_rows_stored")
    v = k.vstep
    cols_of = lambda a: a.rearrange("p c h -> p (c h)")
    CW, CB = PARAM_COLS["conv2_w"][0], PARAM_COLS["conv2_b"][0]
    dt_in = k.aux[:, 0, 0:COLS]
    sums, last = k.aux[:, 1, 0:COLS], k.aux[:, 2, 0:COLS]
    sum_rows = k.aux[0:SSD_HEADS, 3:5, :].rearrange("p a b -> p (a b)")

    @block.tensor
    def _(pe):
        pe.wait_ge(k.s_split, DT_0 + 1)
        for c in range(2):
            cols = slice(c * HALF, (c + 1) * HALF)
            for i in range(KT):
                pe.wait_ge(h_ready[0], h_ready[1] + i + 1)
                w, wl = k.whi[:, DT_0 % 2, i, 0:SSD_HEADS], k.wlo[:, DT_0 % 2, i, 0:SSD_HEADS]
                bank = k.bank[c][0:SSD_HEADS, :]
                pe.matmul(bank, w, k.hhi[:, i, cols], start=i == 0, stop=False)
                pe.matmul(bank, w, k.hlo[:, i, cols], start=False, stop=False)
                mm = pe.matmul(bank, wl, k.hhi[:, i, cols], start=False, stop=i == KT - 1)
            mm.then_inc(k.s_proj, 1)
        pe.wait_ge(s_evac, 2)
        for c in range(CHUNKS):
            mm = pe.transpose(dt_in[:, c * SSD_HEADS:(c + 1) * SSD_HEADS], dt_rows[:, c * P:(c + 1) * P], k.ident[0:SSD_HEADS, 0:SSD_HEADS])
        mm.then_inc(s_dt, 1)
        with pe.Fori(0, CV_TILES // 2) as m:
            for b in range(2):
                for c in range(2):
                    pe.wait_ge(s_evac, m * 4 + (2 * b + c + 1))
                    project(k, pe, m * 2 + (CV_0 + b), (CV_0 + b) % 2, c, k.bank[c][:], k.hhi, k.hlo)
        pe.wait_ge(s_dta, 1)
        pe.matmul(sums, k.tri, dta, start=True, stop=True).then_inc(s_cols, 1)
        pe.wait_ge(s_evac, 2 * CV_TILES + 1)
        project(k, pe, Z_0, Z_0 % 2, 0, k.bank[0][:], k.hhi, k.hlo)
        pe.wait_ge(s_read, 1)
        pe.matmul(last, k.lastrow, cols_of(k.acol), start=True, stop=True).then_inc(s_cols, 1)
        for c in range(CHUNKS):
            mm = pe.transpose(sum_rows[:, c * P:(c + 1) * P], k.acol[:, c, :], k.ident)
        mm.then_inc(s_cols, 1)
        end(k, pe)

    @block.scalar
    def _(act):
        begin(k, act)
        for c in range(2):
            act.wait_ge(k.s_proj, 2 * DT_0 + c + 1)
            act.activation(dt_rows[:, c * HALF:(c + 1) * HALF], k.bank[c][0:SSD_HEADS, :], ACT.Identity, bias=param(k, "dt_bias")[0:SSD_HEADS]).then_inc(s_evac, 1)
        act.activation(a_exp, param(k, "a_log", 0, SSD_HEADS), ACT.Exp)
        act.wait_ge(s_relu, 1)
        act.activation(e, dt_in, ACT.Abs).then_inc(s_exp, 1)
        act.wait_ge(s_exp, 1)
        act.activation(e, e, ACT.Exp, scale=-1.0).then_inc(s_exp, 1)
        act.wait_ge(k.s_spill, 16 * KT)

        def tile_in(i, b):
            act.wait_ge(s_conv, i + 1)
            for c in range(2):
                act.wait_ge(k.s_proj, i * 2 + (2 * CV_0 + c + 1))
                act.activation(xpad[:, b, 3 + c * HALF:3 + (c + 1) * HALF], k.bank[c][:], ACT.Copy).then_inc(s_evac, 1)

        def tile_out(i, b):
            act.wait_ge(s_conv, i + 3)
            act.activation(k.cv[:, ds(i, 1), :].rearrange("p a b -> p (a b)"), cx[:, b], ACT.Silu).then_inc(s_silu, 1)

        tile_in(0, 0)
        with act.Fori(0, CV_TILES // 2 - 1) as m:
            for b in range(2):
                tile_in(m * 2 + (b + 1), 1 - b)
                tile_out(m * 2 + b, b)
        tile_in(CV_TILES - 1, 1)
        tile_out(CV_TILES - 2, 0)
        tile_out(CV_TILES - 1, 1)
        act.wait_ge(s_diff, 1)
        act.activation(cols_of(k.dlast), cols_of(k.dlast), ACT.Exp)
        act.activation(cols_of(k.eac), cols_of(k.acol), ACT.Exp)
        act.activation(cols_of(k.cdec), last, ACT.Exp)
        act.wait_ge(s_cols, 3)
        act.activation(acr, sum_rows, ACT.Copy).then_inc(s_dec, 1)
        act.wait_ge(s_dec, 1)
        act.dma_start(k.acd, acr).then_inc(k.s_acd, 16)
        end(k, act)

    @block.vector
    def _(dve):
        begin(k, dve)
        dve.sem_inc(s_conv, 2)
        dve.sem_inc(s_silu, 2)
        v.settle(dve, dve.memset(xpad[:, :, 0:3], 0.0))
        dve.wait_ge(s_dt, 1)
        dve.tensor_scalar(relu, dt_in, 0.0, None, ALU.max).then_inc(s_relu, 1)
        softplus_dve(k, dve, (s_exp, 2), cols_of(k.dtc), e, relu, s, s2, p)
        rates = a_exp.unsqueeze(1).broadcast_to([P, CHUNKS, SSD_HEADS])
        dve.scalar_tensor_tensor(dta.rearrange("p (c h) -> p c h", c=CHUNKS), k.dtc, -1.0, rates, ALU.mult, ALU.mult).then_inc(s_dta, 1)
        dve.wait_ge(k.s_spill, 16 * KT)
        with dve.Fori(0, CV_TILES // 2) as m:
            v.enter(m, 6)
            for b in range(2):
                dve.wait_ge(s_evac, m * 4 + (2 * b + 4))
                dve.wait_ge(s_silu, m * 2 + (b + 1))
                taps = lambda t: k.par[:, ds(m * (2 * TAPS) + (CW + b * TAPS + t), 1)]
                v.settle(dve, dve.tensor_scalar(cx[:, b], xpad[:, b, 0:T], taps(0), k.par[:, ds(m * 2 + (CB + b), 1)], ALU.mult, ALU.add))
                for t in range(1, TAPS):
                    ins = dve.scalar_tensor_tensor(cx[:, b], xpad[:, b, t:t + T], taps(t), cx[:, b], ALU.mult, ALU.add)
                    if t < TAPS - 1:
                        v.settle(dve, ins)
                ins.then_inc(s_conv, 1)
        v.leave(CV_TILES // 2)
        dve.wait_ge(s_cols, 1)
        dve.tensor_copy(cols_of(k.acol), sums).then_inc(s_read, 1)
        dve.wait_ge(s_cols, 2)
        dve.wait_ge(s_read, 1)
        dve.tensor_tensor(cols_of(k.dlast), last, cols_of(k.acol), ALU.subtract).then_inc(s_diff, 1)
        end(k, dve)

    k.stage += 1


def ssd_mix_stage(k, block):
    F = k.F
    GH = SSD_HEADS // 2
    W = GH * SSD_P
    btok = k.at("ssd_b_tokens", F + 48, [P, CHUNKS, P])
    xs = k.at("ssd_x_tokens", F + 52, [P, CHUNKS, W])
    state = k.at("ssd_state", F + 68, [P, 2, W])
    xd = k.at("ssd_x_decayed", F + 72, [P, 2, W])
    ytok = k.at("ssd_y_tokens", F + 76, [P, CHUNKS, W])
    ab = k.at("ssd_decay_rows", F + 92, [P, 2, T])
    m = k.at("ssd_weights", F + 100, [P, 2, T])
    cb = k.at("ssd_cb", F + 108, [P, CHUNKS, P])
    s_turn, s_x, s_bc, s_bread = k.sem("ssd_x_turned"), k.sem("ssd_x_made"), k.sem("ssd_bc_made"), k.sem("ssd_bc_read")
    s_st, s_state, s_off = k.sem("ssd_states_made"), k.sem("ssd_state_carried"), k.sem("ssd_off_read")
    s_ab, s_seg, s_exp, s_m = [k.sem(f"ssd_rows_loaded_{i}") for i in range(2)], k.sem("ssd_seg"), k.sem("ssd_seg_exp"), k.sem("ssd_m")
    s_diag, s_y = k.sem("ssd_diag"), k.sem("ssd_y_added")
    s_back, s_out = k.sem("ssd_y_turned"), k.sem("ssd_y_read")
    szb = k.at("ssd_silu_z", F + 68, [P, 2, T])
    sq = k.at("ssd_y_squared", F + 52, [P, 4, T])
    s_z, s_gated, s_sq, s_gsum = k.sem("ssd_z_made"), k.sem("ssd_gated"), k.sem("ssd_squares"), k.sem("ssd_squares_summed")
    GT = KT // 2
    k.gsum = k.aux[:, 5, 0:2 * TT]
    v = k.vstep

    def per_head(a, c, g):
        return a[:, c, g * GH:(g + 1) * GH].unsqueeze(2).broadcast_to([P, GH, SSD_P])

    heads_of = lambda a: a.rearrange("p (h e) -> p h e", h=GH)

    @block.tensor
    def _(pe):
        def z_half(n, c):
            if n:
                pe.wait_ge(s_z, 2 * n + c - 1)
            project(k, pe, Z_0 + n, (Z_0 + n) % 2, c, k.bank[c][:], k.hhi, k.hlo)

        begin(k, pe)
        for g in range(2):
            ct, bt = k.cv[:, g, :], k.cv[:, 2 + g, :]

            def turn(c):
                n = g * CHUNKS + c
                cols = slice(c * P, (c + 1) * P)
                if n >= 2:
                    pe.wait_ge(s_x, n - 1)
                for f in range(4):
                    mm = pe.transpose(k.aux[:, c % 2, f * P:(f + 1) * P], k.cv[:, 4 + 4 * g + f, cols], k.ident)
                mm.then_inc(s_turn, 1)
                if n >= 1:
                    pe.wait_ge(s_bread, n)
                pe.transpose(k.aux[:, 2, 0:P], bt[:, cols], k.ident)
                pe.matmul(k.aux[:, 2, P:2 * P], bt[:, cols], ct[:, cols], start=True, stop=True).then_inc(s_bc, 1)

            if g:
                pe.wait_ge(s_y, GH)
                pe.wait_ge(s_out, 8)
            turn(0)
            for c in range(CHUNKS):
                n = g * CHUNKS + c
                if c + 1 < CHUNKS:
                    turn(c + 1)
                pe.wait_ge(s_bread, n + 1)
                if n >= 1:
                    pe.wait_ge(s_off, n)
                pe.matmul(k.aux[:, 3, :], btok[:, c, :], xd[:, c % 2], start=True, stop=True)
                pe.wait_ge(s_state, n + g + 1)
                pe.matmul(k.aux[:, 4, :], ct[:, c * P:(c + 1) * P], state[:, c % 2], start=True, stop=True).then_inc(s_st, 1)
            for n in range(GT):
                z_half(GT * g + n, 1)
                for b in range(2):
                    h = g * GH + 2 * n + b
                    pe.wait_ge(s_m, h + 1)
                    pe.wait_ge(s_y, h + 1)
                    for c in range(CHUNKS):
                        mm = pe.matmul(k.aux[:, b, c * SSD_P:(c + 1) * SSD_P], m[:, b, c * P:(c + 1) * P],
                                       xs[:, c, (2 * n + b) * SSD_P:(2 * n + b + 1) * SSD_P], start=True, stop=True)
                    mm.then_inc(s_diag, 1)
                if n < GT - 1:
                    z_half(GT * g + n + 1, 0)
            pe.wait_ge(s_y, (g + 1) * GH + 2)
            for f in range(4):
                for a in range(2):
                    n = g * 8 + 2 * f + a
                    if n >= 2:
                        pe.wait_ge(s_out, n - 1)
                    for c in range(4):
                        mm = pe.transpose(k.aux[:, a, c * P:(c + 1) * P], ytok[:, 4 * a + c, f * P:(f + 1) * P], k.ident)
                    mm.then_inc(s_back, 1)
            z_half(GT * (g + 1), 0)
            pe.wait_ge(s_sq, GT * (g + 1))
            for j in range(TT):
                for f in range(GT):
                    mm = pe.matmul(k.gsum[:, g * TT + j:g * TT + j + 1], sq[:, f, j * P:(j + 1) * P], k.ones, start=f == 0, stop=f == GT - 1)
            mm.then_inc(s_gsum, 1)
        z_half(KT, 1)
        pe.sem_inc(k.s_gates, 2)
        pe.sem_inc(k.s_mixed, 2)
        end(k, pe)

    @block.scalar
    def _(act):
        begin(k, act)

        def load(h, b):
            row = k.acd[ds(h, 1), :] if not isinstance(h, int) else k.acd[h:h + 1, :]
            act.dma_start(ab[:, b], row.broadcast_to([P, T])).then_inc(s_ab[b], 16)

        act.wait_ge(k.s_acd, 16)
        load(0, 0)
        load(1, 1)

        def pair_of(g, i, pair, last=False):
            for c in range(2):
                cols = slice(c * HALF, (c + 1) * HALF)
                act.wait_ge(k.s_proj, i * 4 + (2 * (Z_0 + GT * g + pair) + c + 1))
                dst = (k.cv[:, ds(i * 2 + g, 1), cols] if pair == 0 else szb[:, ds(i, 1), cols]).rearrange("p a b -> p (a b)")
                act.activation(dst, k.bank[c][:], ACT.Silu).then_inc(s_z, 1)
                for b in range(2 if c == 0 else 0):
                    h = i * 4 + (g * GH + 2 * pair + b)
                    act.wait_ge(s_seg, h + 1)
                    act.activation(m[:, b], m[:, b], ACT.Exp).then_inc(s_exp, 1)
                    if not last:
                        load(h + 2, b)

        def squares(g):
            for f in range(GT):
                act.wait_ge(s_gated, g * GT + f + 1)
                act.activation(sq[:, f], k.cv[:, 4 + GT * g + f, :], ACT.Square).then_inc(s_sq, 1)

        act.wait_ge(s_off, CHUNKS)
        with act.Fori(0, GH // 4) as i:
            for pair in range(2):
                pair_of(0, i, pair)
        squares(0)
        act.wait_ge(s_off, 2 * CHUNKS)
        for i in range(GH // 4):
            for pair in range(2):
                pair_of(1, i, pair, last=i == GH // 4 - 1 and pair == 1)
        squares(1)
        end(k, act)

    @block.vector
    def _(dve):
        begin(k, dve)
        dve.sem_inc(s_y, 2)

        for g in range(2):

            def take(c):
                n = g * CHUNKS + c
                dve.wait_ge(s_turn, n + 1)
                dve.tensor_tensor(heads_of(xs[:, c, :]), heads_of(k.aux[:, c % 2, :]), per_head(k.dtc, c, g), ALU.mult).then_inc(s_x, 1)
                dve.wait_ge(s_bc, n + 1)
                dve.tensor_copy(btok[:, c, :], k.aux[:, 2, 0:P])
                dve.tensor_tensor(cb[:, c, :], k.aux[:, 2, P:2 * P], k.tri, ALU.mult)
                dve.wait_ge(s_x, n + 1)
                if n >= 2:
                    dve.wait_ge(s_st, n - 1)
                dve.tensor_tensor(heads_of(xd[:, c % 2]), heads_of(xs[:, c, :]), per_head(k.dlast, c, g), ALU.mult).then_inc(s_bread, 1)

            if g:
                dve.wait_ge(s_gsum, g)
            dve.memset(state[:, 0], 0.0).then_inc(s_state, 1)
            take(0)
            for c in range(CHUNKS):
                n = g * CHUNKS + c
                if c + 1 < CHUNKS:
                    take(c + 1)
                dve.wait_ge(s_state, n + g + 1)
                nxt = state[:, (c + 1) % 2]
                v.settle(dve, dve.tensor_tensor(heads_of(nxt), heads_of(state[:, c % 2]), per_head(k.cdec, c, g), ALU.mult))
                dve.wait_ge(s_st, n + 1)
                dve.tensor_tensor(nxt, nxt, k.aux[:, 3, :], ALU.add).then_inc(s_state, 1)
                dve.tensor_tensor(heads_of(ytok[:, c, :]), heads_of(k.aux[:, 4, :]), per_head(k.eac, c, g), ALU.mult).then_inc(s_off, 1)
            dve.wait_ge(s_off, (g + 1) * CHUNKS)
            with dve.Fori(0, GH // 2) as i:
                v.enter(i, 2)
                for b in range(2):
                    h = i * 2 + (g * GH + b)
                    dve.wait_ge(s_ab[b], i * 16 + 16 * (g * GH // 2 + 1))
                    dve.wait_ge(s_y, h + 1)
                    col = k.acol[:, :, ds(i * 2 + (g * GH + b), 1)].broadcast_to([P, CHUNKS, P])
                    mc = m[:, b].rearrange("p (c l) -> p c l", c=CHUNKS)
                    v.settle(dve, dve.tensor_tensor(mc, ab[:, b].rearrange("p (c l) -> p c l", c=CHUNKS), col, ALU.subtract))
                    dve.tensor_scalar(m[:, b], m[:, b], 0.0, None, ALU.min).then_inc(s_seg, 1)
                for b in range(2):
                    h = i * 2 + (g * GH + b)
                    dve.wait_ge(s_exp, h + 1)
                    dve.tensor_tensor(m[:, b], m[:, b], cb.rearrange("p c l -> p (c l)"), ALU.mult).then_inc(s_m, 1)
                for b in range(2):
                    h = i * 2 + (g * GH + b)
                    dve.wait_ge(s_diag, h + 1)
                    yh = ytok[:, :, ds(i * (2 * SSD_P) + b * SSD_P, SSD_P)]
                    dve.tensor_tensor(yh, yh, k.aux[:, b, :].rearrange("p (c e) -> p c e", c=CHUNKS), ALU.add).then_inc(s_y, 1)
            v.leave(GH // 2)
            for f in range(4):
                for a in range(2):
                    n = g * 8 + 2 * f + a
                    dve.wait_ge(s_back, n + 1)
                    yt = k.cv[:, 4 + 4 * g + f, a * HALF:(a + 1) * HALF]
                    dve.scalar_tensor_tensor(yt, yt, param(k, "d_skip", 4 * g + f), k.aux[:, a, :], ALU.mult, ALU.add).then_inc(s_out, 1)
                dve.wait_ge(s_out, g * 8 + 2 * f + 2)
                dve.wait_ge(s_z, 2 * (GT * g + f + 1))
                yt = k.cv[:, 4 + GT * g + f, :]
                dve.tensor_tensor(yt, yt, k.cv[:, g + f, :] if f % 2 == 0 else szb[:, f // 2], ALU.mult).then_inc(s_gated, 1)
        end(k, dve)

    k.stage += 1


def open_gates(k, block, first):

    @block.tensor
    def _(pe):
        pe.wait_ge(*k.banks_read)
        for c in range(2):
            project(k, pe, first, first % 2, c, k.bank[c][:], k.hhi, k.hlo)


def gated_out_stage(k, block, first, hi, lo, tiles, mix, gate, ready, opens=False, prior=None):
    out = k.aux[:, 4:6, :]
    done = 2 * KT * k.branches
    k.branches += 1
    k.banks_read = (k.s_gates, done + 2 * KT + 2)
    v = k.vstep

    @block.tensor
    def _(pe):
        def outputs(f):
            for c in range(2):
                pe.wait_ge(k.s_mixed, f * 2 + (done + c + 1))
                project(k, pe, f * 2 + (first + 1), (first + 1) % 2, c, out[:, c, :], hi, lo, range(tiles), ready=ready)

        with pe.Fori(0, KT - 1) as f:
            outputs(f)
            for c in range(2):
                pe.wait_ge(k.s_gates, f * 2 + (done + c + 3))
                project(k, pe, f * 2 + (first + 2), first % 2, c, k.bank[c][:], k.hhi, k.hlo)
        outputs(KT - 1)
        end(k, pe)

    @block.scalar
    def _(act):
        begin(k, act)
        with act.Fori(0, KT) as f:
            for c in range(2):
                act.wait_ge(k.s_proj, f * 4 + (2 * first + c + 1))
                act.wait_ge(k.s_mixed, f * 2 + (done + c + 1))
                act.activation(gate[:, c], k.bank[c][:], ACT.Sigmoid).then_inc(k.s_gates, 1)
        end(k, act)

    @block.vector
    def _(dve):
        begin(k, dve)
        if prior is not None:
            dve.wait_ge(*prior)
        with dve.Fori(0, KT) as f:
            v.enter(f, 0 if opens else 2)
            for c in range(2):
                dve.wait_ge(k.s_proj, f * 4 + (2 * first + c + 3))
                dve.wait_ge(k.s_gates, f * 2 + (done + c + 3))
                mt = mix[:, ds(f, 1), c * HALF:(c + 1) * HALF].rearrange("p a b -> p (a b)")
                if opens:
                    dve.tensor_tensor(mt, gate[:, c], out[:, c, :], ALU.mult).then_inc(k.s_mixed, 1)
                else:
                    v.settle(dve, dve.tensor_tensor(gate[:, c], gate[:, c], out[:, c, :], ALU.mult))
                    dve.tensor_tensor(mt, mt, gate[:, c], ALU.add).then_inc(k.s_mixed, 1)
        v.leave(KT)
        end(k, dve)

    k.stage += 1




DILATIONS = (1, 4, 16)
GROUPS = len(DILATIONS)
OUT_W = P + 2


def blocks_before(g):
    per = TT // DILATIONS[g]
    return [b for b in range(TT) if per and b % per]


def spans(g, a):
    if g == 0:
        return [(a[:, 0:1, P:], slice(0, 1), slice(P, 2 * P)), (a[:, 1:, :], slice(1, TT), slice(0, 2 * P))]
    if g == 1:
        pairs = a.rearrange("p (r b) w -> p r b w", b=2)
        return [(pairs[:, :, 0, P:], slice(0, TT, 2), slice(P, 2 * P)), (pairs[:, :, 1, :], slice(1, TT, 2), slice(0, 2 * P))]
    return [(a[:, :, P:], slice(0, TT), slice(P, 2 * P))]


def dilated_stage(k, block, bias, mix):
    F = k.F
    q, kk, vtok = (k.at(f"dil_{n}", F + 32 + 12 * i, [P, GROUPS, T]) for i, n in enumerate(("q", "k", "v")))
    vt = k.at("dil_v_features", F + 68, [P, T])
    sq = k.at("dil_squared", F + 72, [P, 2, T])
    p = k.at("dil_p", F + 80, [P, TT, 2 * P])
    pt = k.at("dil_p_turned", F + 88, [P, TT, 2 * P])
    oext = k.at("dil_out", F + 96, [P, GROUPS, TT, OUT_W])
    bias_in = k.at("dil_bias", F + 108.25, [P, GROUPS, 2 * P])
    weight = k.small[:, 120:121]
    nmax = k.at("dil_max", F + 111.25, [P, TT])
    stat, rstd = k.at("dil_var", F + 111.5, [P, 2 * TT]), k.at("dil_rstd", F + 111.75, [P, 2 * TT])
    score = k.aux[:, 0:4, :].rearrange("p a (b w) -> p (a b) w", b=2)
    spread_banks = k.aux[:, 0:4, :].rearrange("p a b -> p (a b)")
    out = k.aux[:, 4:6, :].rearrange("p a (b e) -> p (a b) e", b=4)
    s_evac = k.sem("dil_evacuated")
    s_stat, s_var, s_root, s_col = (k.sem(f"dil_{n}") for n in ("summed", "var", "root", "rstd"))
    s_spread, s_norm = k.sem("dil_spread"), k.sem("dil_normed")
    s_vt, s_vtok = k.sem("dil_v_turned"), k.sem("dil_v_read")
    s_score, s_bias, s_max, s_exp = k.sem("dil_scored"), k.sem("dil_biased"), k.sem("dil_max_made"), k.sem("dil_exp")
    s_turn, s_pt = k.sem("dil_p_turns"), k.sem("dil_p_read")
    s_pv, s_o = k.sem("dil_product"), k.sem("dil_out_read")
    s_bin, s_stored = [k.sem(f"dil_bias_loaded_{g}") for g in range(GROUPS)], [k.sem(f"dil_stored_{g}") for g in range(GROUPS)]
    STORES = (1, 4, 2)
    k.s_stored, k.stores = s_stored, STORES
    k.heads = k.at("dil_heads", F, [P, DL_ROUNDS, T])
    k.rows = k.at("dil_rows", F + 16, [P, GROUPS, TT, OUT_W])
    k.rows_small = k.at("dil_rows_small", F + 28.25, [P, 9 * TT])
    k.turned = k.aux[:, 4:6, :].rearrange("p a b -> p (a b)")
    k.s_crows, k.s_cdist, k.s_cexp = k.sem("dil_rows_loaded"), k.sem("dil_from_max"), k.sem("dil_factors")
    k.s_csum, k.s_cturn = k.sem("dil_summed_over"), k.sem("dil_summed_turned")
    s_head, s_kept = k.sem("dil_head_in_place"), k.sem("mix_stored")
    k.banks_read = (s_evac, 6 * DIL_HEADS + 2)
    SCALE = P ** -0.5
    v = k.vstep

    def after(j, g):
        return (j, g + 1) if g + 1 < GROUPS else (j + 1, 0)

    def rounds(eng, one):
        for g in range(GROUPS):
            one(0, g, True)
        with eng.Fori(0, DL_ROUNDS - 2) as m:
            if eng is k.nc.vector:
                v.enter(m, STEPS)
            for g in range(GROUPS):
                one(m + 1, g, True)
        if eng is k.nc.vector:
            v.leave(DL_ROUNDS - 2)
        for g in range(GROUPS):
            one(DL_ROUNDS - 1, g, g + 1 < GROUPS)

    def combines(j, g):
        if isinstance(j, int):
            return j == DL_ROUNDS - 1 and g == GROUPS - 2
        return g == GROUPS - 1

    STEPS = GROUPS + 7

    def head(j, g):
        return j * GROUPS + g

    @block.tensor
    def _(pe):
        begin(k, pe)

        def half(j, g, i):
            first = DL_0 + 3 * g + i // 2
            pe.wait_ge(s_evac, j * 18 + (6 * g + i + 1))
            project(k, pe, j * DL_ROUND + first, first % 2, i % 2, k.bank[i % 2][:], k.hhi, k.hlo)

        def statistics(j, g, i):
            pe.wait_ge(s_evac, j * 18 + (6 * g + 4 + 2))
            pe.wait_ge(s_pt, j * 3 + (g + 1))
            for b in range(TT):
                mm = pe.matmul(k.aux[:, 0, i * TT + b:i * TT + b + 1], sq[:, i, b * P:(b + 1) * P], k.ones, start=True, stop=True)
            if i == 1:
                mm.then_inc(s_stat, 1)

        def spread(j, g):
            pe.wait_ge(s_col, j * 3 + (g + 1))
            for b in range(TT):
                mm = pe.matmul(spread_banks[:, b * P:(b + 1) * P], rstd[:, TT + b:TT + b + 1].to_broadcast([P, P]), k.ident, start=True, stop=True)
            mm.then_inc(s_spread, 1)

        def values(j, g):
            pe.wait_ge(s_evac, j * 18 + (6 * g + 6 + 2))
            pe.wait_ge(s_o, j * 3 + (g + 1))
            for b in range(TT):
                mm = pe.transpose(out[:, b, :], vt[:, b * P:(b + 1) * P], k.ident)
            mm.then_inc(s_vt, 1)

        def scores(j, g):
            pe.wait_ge(s_norm, j * 3 + (g + 1))
            before = blocks_before(g)
            for b in range(TT):
                qb = q[:, g, b * P:(b + 1) * P]
                if b in before:
                    pe.matmul(score[:, b, 0:P], qb, kk[:, g, (b - 1) * P:b * P], start=True, stop=True)
                mm = pe.matmul(score[:, b, P:], qb, kk[:, g, b * P:(b + 1) * P], start=True, stop=True)
                if g == GROUPS - 1 and b < 2:
                    mm.then_inc(k.s_proj, 1)
            mm.then_inc(s_score, 1)

        def turns(j, g):
            pe.wait_ge(s_exp, j * 3 * TT + (g + 1) * TT)
            before = blocks_before(g)
            for b in range(TT):
                if b in before:
                    pe.transpose(score[:, b, 0:P], p[:, b, 0:P], k.ident)
                mm = pe.transpose(score[:, b, P:], p[:, b, P:], k.ident)
            mm.then_inc(s_turn, 1)

        def product(j, g):
            pe.wait_ge(s_vtok, j * 3 + (g + 1))
            pe.wait_ge(s_pt, j * 3 + (g + 2))
            if combines(j, g):
                pe.wait_ge(s_head, j)
            before = blocks_before(g)
            for b in range(TT):
                if b in before:
                    pe.matmul(out[:, b, :], pt[:, b, 0:P], vtok[:, g, (b - 1) * P:b * P], start=True, stop=False)
                mm = pe.matmul(out[:, b, :], pt[:, b, P:], vtok[:, g, b * P:(b + 1) * P], start=b not in before, stop=True)
            mm.then_inc(s_pv, 1)

        def one(j, g, more):
            values(j, g)
            scores(j, g)
            if more:
                for i in range(3):
                    half(*after(j, g), i)
            if combines(j, g):
                pe.wait_ge(k.s_csum, j)
                pe.wait_ge(s_vtok, j * 3 + (g + 1))
                combine_turn(k, pe)
            turns(j, g)
            if more:
                half(*after(j, g), 3)
            product(j, g)
            if more:
                statistics(*after(j, g), 0)
                half(*after(j, g), 4)
                statistics(*after(j, g), 1)
                half(*after(j, g), 5)
                spread(*after(j, g))

        for i in range(4):
            half(0, 0, i)
        statistics(0, 0, 0)
        half(0, 0, 4)
        statistics(0, 0, 1)
        half(0, 0, 5)
        spread(0, 0)
        rounds(pe, one)
        end(k, pe)

    @block.scalar
    def _(act):
        begin(k, act)
        act.sem_inc(s_evac, 2)
        act.sem_inc(s_o, 1)

        def load_bias(j, g):
            act.dma_start(bias_in[:, g], bias[DL_ROUNDS * g + j] if isinstance(j, int) else bias[ds(j + DL_ROUNDS * g, 1)].rearrange("a p w -> (a p) w")).then_inc(s_bin[g], 16)

        def half(j, g, i):
            d = DILATIONS[g]
            n = HALF // d
            act.wait_ge(k.s_proj, j * (2 * DL_ROUND) + (2 * DL_0 + 6 * g + i + 1))
            own = lambda a: a.rearrange("p (r i) -> p r i", r=d)[:, :, (i % 2) * n:(i % 2 + 1) * n]
            bank = k.bank[i % 2][:].rearrange("p (i r) -> p r i", r=d)
            if i // 2 == 2:
                act.activation(own(vt), bank, ACT.Copy).then_inc(s_evac, 1)
            else:
                act.activation(own((q, kk)[i // 2][:, g]), bank, ACT.Copy)
                act.activation(own(sq[:, i // 2]), bank, ACT.Square).then_inc(s_evac, 1)

        def root(j, g):
            act.wait_ge(s_var, j * 3 + (g + 1))
            act.activation(stat, stat, ACT.Sqrt).then_inc(s_root, 1)

        def softmax(j, g):
            act.wait_ge(s_max, j * 3 + (g + 1))
            before = blocks_before(g)
            for b in range(TT):
                row = p[:, b, :] if b in before else p[:, b, P:]
                act.activation(row, row, ACT.Exp, bias=nmax[:, b:b + 1], accum_out=oext[:, g, b, P + 1:P + 2]).then_inc(s_exp, 1)

        def store(j, g):
            act.wait_ge(s_pv, j * 3 + (g + 1))
            act.activation(oext[:, g, :, 0:P], out, ACT.Copy).then_inc(s_o, 1)
            act.wait_ge(s_o, j * 3 + (g + 2))
            n = DL_ROUNDS * g + j
            rows = k.dild[n:n + 1] if isinstance(n, int) else k.dild[ds(n, 1)]
            if g == 0:
                act.dma_start(rows.rearrange("a (b p) w -> p (a b) w", p=P), oext[:, g]).then_inc(s_stored[g], 16)
            elif g == 1:
                by_residue = rows.rearrange("a (b p r) w -> r p (a b) w", p=P, r=DILATIONS[g])
                for r in range(DILATIONS[g]):
                    act.dma_start(by_residue[r], oext[:, g, 2 * r:2 * r + 2]).then_inc(s_stored[g], 16)
            else:
                by_half = rows.rearrange("a (i b s) w -> s (a i) b w", b=TT, s=2)
                for s in range(2):
                    act.dma_start(by_half[s], oext[s * 64:(s + 1) * 64, g]).then_inc(s_stored[g], 16)

        def one(j, g, more):
            nxt = after(j, g)
            if more:
                half(*nxt, 0)
            softmax(j, g)
            if not (isinstance(j, int) and j == DL_ROUNDS - 1):
                load_bias(j + 1, g)
            if combines(j, g):
                combine_factors(k, act, j)
            if more:
                for i in (1, 2):
                    half(*nxt, i)
            if combines(j, g):
                act.wait_ge(k.s_cturn, j)
                dst = k.heads[:, j - 1] if isinstance(j, int) else k.heads[:, ds(j - 1, 1)].rearrange("p a b -> p (a b)")
                act.activation(dst, k.turned, ACT.Copy).then_inc(s_head, 1)
            if more:
                half(*nxt, 3)
            store(j, g)
            if g + 1 < GROUPS and combines(j, g + 1):
                combine_load(k, act, j - 1)
            if more:
                half(*nxt, 4)
                root(*nxt)
                half(*nxt, 5)

        for t in range(KT):
            act.dma_start(k.mixd[t], mix[:, t]).then_inc(s_kept, 16)
        for g in range(GROUPS):
            load_bias(0, g)
        for i in range(4):
            half(0, 0, i)
        half(0, 0, 4)
        root(0, 0)
        half(0, 0, 5)
        act.wait_ge(s_kept, 16 * KT)
        rounds(act, one)
        end(k, act)

    @block.vector
    def _(dve):
        begin(k, dve)
        dve.sem_inc(s_pt, 1)
        dve.sem_inc(s_bias, 1)
        for g in range(GROUPS):
            dve.sem_inc(s_stored[g], 1)
        v.settle(dve, dve.scalar_tensor_tensor(weight, param(k, "q_norm"), SCALE, param(k, "k_norm"), ALU.mult, ALU.mult))

        def statistics(j, g):
            dve.wait_ge(s_stat, j * 3 + (g + 1))
            dve.tensor_scalar(stat, k.aux[:, 0, 0:2 * TT], 1.0 / P, EPS, ALU.mult, ALU.add).then_inc(s_var, 1)
            dve.wait_ge(s_root, j * 3 + (g + 1))
            dve.reciprocal(rstd, stat).then_inc(s_col, 1)

        def norm(j, g):
            dve.wait_ge(s_spread, j * 3 + (g + 1))
            dve.scalar_tensor_tensor(kk[:, g], kk[:, g], weight, spread_banks[:, 0:T], ALU.mult, ALU.mult).then_inc(s_norm, 1)

        def values(j, g):
            dve.wait_ge(s_vt, j * 3 + (g + 1))
            dve.tensor_copy(vtok[:, g], k.aux[:, 4:6, :].rearrange("p a b -> p (a b)")).then_inc(s_vtok, 1)

        def softmax(j, g):
            dve.wait_ge(s_score, j * 3 + (g + 1))
            dve.wait_ge(s_bin[g], j * 16 + 16)
            dve.wait_ge(s_stored[g], j * (16 * STORES[g]) + 1)
            for b in range(TT):
                cols = slice(0 if b in blocks_before(g) else P, 2 * P)
                ins = dve.scalar_tensor_tensor(p[:, b, cols], score[:, b, cols], rstd[:, b:b + 1], bias_in[:, g, cols], ALU.mult, ALU.add)
            ins.then_inc(s_bias, 1)
            dve.wait_ge(s_bias, j * 3 + (g + 2))
            for x, blocks, _ in spans(g, p):
                ins = dve.tensor_reduce(oext[:, g, blocks, P], x, AX, ALU.max)
            v.settle(dve, ins)
            dve.tensor_scalar(nmax, oext[:, g, :, P], -1.0, None, ALU.mult).then_inc(s_max, 1)

        def turned(j, g):
            dve.wait_ge(s_turn, j * 3 + (g + 1))
            for (s, _, _), (x, _, _) in zip(spans(g, score), spans(g, pt)):
                ins = dve.tensor_copy(x, s)
            ins.then_inc(s_pt, 1)

        def one(j, g, more):
            values(j, g)
            softmax(j, g)
            if combines(j, g):
                combine_math(k, dve, (k.s_crows, j * 48), (k.s_cexp, j))
            turned(j, g)
            if more:
                statistics(*after(j, g))
                norm(*after(j, g))

        statistics(0, 0)
        norm(0, 0)
        rounds(dve, one)
        end(k, dve)

    k.stage += 1


def combine_math(k, dve, loaded, factors):
    rows, v = k.rows, k.vstep
    by_token = rows.rearrange("p g b w -> p b g w")
    mx, den, inv = (k.rows_small[:, i * TT:(i + 1) * TT] for i in range(3))
    e, es = (k.rows_small[:, (3 + 3 * i) * TT:(6 + 3 * i) * TT].rearrange("p (b g) -> p b g", g=GROUPS) for i in range(2))
    dve.wait_ge(*loaded)
    v.settle(dve, dve.tensor_reduce(mx, by_token[:, :, :, P], AX, ALU.max))
    dve.tensor_tensor(e, by_token[:, :, :, P], mx.unsqueeze(2).broadcast_to([P, TT, GROUPS]), ALU.subtract).then_inc(k.s_cdist, 1)
    dve.wait_ge(*factors)
    v.settle(dve, dve.tensor_tensor(es, e, by_token[:, :, :, P + 1], ALU.mult))
    v.settle(dve, dve.tensor_reduce(den, es, AX, ALU.add))
    v.settle(dve, dve.reciprocal(inv, den))
    v.settle(dve, dve.tensor_tensor(e, e, inv.unsqueeze(2).broadcast_to([P, TT, GROUPS]), ALU.mult))
    for g in range(GROUPS):
        ins = dve.tensor_tensor(rows[:, g, :, 0:P], rows[:, g, :, 0:P], e[:, :, g:g + 1].broadcast_to([P, TT, P]), ALU.mult)
    v.settle(dve, ins)
    v.settle(dve, dve.tensor_tensor(rows[:, 0, :, 0:P], rows[:, 0, :, 0:P], rows[:, 1, :, 0:P], ALU.add))
    dve.tensor_tensor(rows[:, 0, :, 0:P], rows[:, 0, :, 0:P], rows[:, 2, :, 0:P], ALU.add).then_inc(k.s_csum, 1)


def combine_turn(k, pe):
    for b in range(TT):
        mm = pe.transpose(k.turned[:, b * P:(b + 1) * P], k.rows[:, 0, b, 0:P], k.ident)
    mm.then_inc(k.s_cturn, 1)


def combine_load(k, act, j):
    for g in range(GROUPS):
        act.wait_ge(k.s_stored[g], j * (16 * k.stores[g]) + (16 * k.stores[g] + 1))
        n = DL_ROUNDS * g + j
        rows = k.dild[n:n + 1] if isinstance(n, int) else k.dild[ds(n, 1)]
        act.dma_start(k.rows[:, g], rows.rearrange("a (b p) w -> p (a b) w", p=P)).then_inc(k.s_crows, 16)


def combine_factors(k, act, n):
    e = k.rows_small[:, 3 * TT:6 * TT]
    act.wait_ge(k.s_cdist, n)
    act.activation(e, e, ACT.Exp).then_inc(k.s_cexp, 1)


def combine_stage(k, block, mix):
    F = k.F
    k.ahi, k.alo = (k.at(f"dil_{n}", F + 32 + 16 * i, [P, DL_ROUNDS, T], F32R) for i, n in enumerate(("hi", "lo")))
    s_hi, k.s_alo = k.sem("dil_high"), k.sem("dil_low")
    k.s_mix_in = k.sem("mix_again")
    last = DL_ROUNDS - 1
    parts = lambda t: k.heads[:, t] if t < last else k.turned

    @block.tensor
    def _(pe):
        pe.wait_ge(k.s_csum, DL_ROUNDS)
        combine_turn(k, pe)
        end(k, pe)

    @block.scalar
    def _(act):
        begin(k, act)
        combine_load(k, act, last)
        for t in range(DL_ROUNDS):
            if t == last:
                combine_factors(k, act, DL_ROUNDS)
                act.wait_ge(k.s_cturn, DL_ROUNDS)
            act.activation(k.ahi[:, t], parts(t), ACT.Copy).then_inc(s_hi, 1)
        act.wait_ge(k.s_alo, last)
        for t in range(KT):
            act.dma_start(mix[:, t], k.mixd[t]).then_inc(k.s_mix_in, 16)
        end(k, act)

    @block.vector
    def _(dve):
        begin(k, dve)
        for t in range(DL_ROUNDS):
            if t == last:
                combine_math(k, dve, (k.s_crows, 48 * DL_ROUNDS), (k.s_cexp, DL_ROUNDS))
            dve.wait_ge(s_hi, t + 1)
            dve.tensor_tensor(k.alo[:, t], parts(t), k.ahi[:, t].bitcast(F32), ALU.subtract).then_inc(k.s_alo, 1)
        end(k, dve)

    k.stage += 1




def pool_stage(k, block):
    F = k.F
    PAD = 16
    k.phi, k.plo = (k.at(f"pool_{n}", F + 32 + 32 * i, [P, KT, T], F32R) for i, n in enumerate(("hi", "lo")))
    u = k.at("pool_u", F + 96, [P, 2, PAD + T])
    tmp = k.at("pool_tmp", F + 104.25, [P, 2, PAD + T])
    k.s_phi, k.s_plo = k.sem("pool_high"), k.sem("pool_low")
    s_u, s_diff = k.sem("pool_u_in"), k.sem("pool_diff")
    k.banks_read = (s_u, 2 * KT + 2)
    v = k.vstep

    @block.tensor
    def _(pe):
        begin(k, pe)
        with pe.Fori(0, KT // 2) as m:
            for b in range(2):
                for c in range(2):
                    pe.wait_ge(s_u, m * 4 + (2 * b + c + 1))
                    project(k, pe, m * 2 + (U_0 + b), (U_0 + b) % 2, c, k.bank[c][:], k.hhi, k.hlo)
        end(k, pe)

    @block.scalar
    def _(act):
        begin(k, act)
        act.sem_inc(s_u, 2)

        def u_in(f):
            if f >= 2:
                act.wait_ge(s_diff, f - 1)
            for c in range(2):
                act.wait_ge(k.s_proj, 2 * U_0 + 2 * f + c + 1)
                act.activation(u[:, f % 2, PAD + c * HALF:PAD + (c + 1) * HALF], k.bank[c][:], ACT.Copy).then_inc(s_u, 1)

        u_in(0)
        for f in range(KT):
            if f + 1 < KT:
                u_in(f + 1)
            act.wait_ge(s_diff, f + 1)
            act.activation(k.phi[:, f], tmp[:, (f // 2 + 1) % 2, PAD:], ACT.Copy).then_inc(k.s_phi, 1)
        end(k, act)

    @block.vector
    def _(dve):
        begin(k, dve)
        v.settle(dve, dve.memset(u[:, :, 0:PAD], 0.0))
        for f in range(KT):
            levels = f // 2 + 1
            w = 2 ** levels
            dve.wait_ge(s_u, 2 * f + 4)
            if f:
                dve.wait_ge(k.s_plo, f)
            src = u[:, f % 2]
            for level in range(levels):
                step = 2 ** level
                at = 2 * step - 1
                dst = tmp[:, level % 2]
                v.settle(dve, dve.tensor_tensor(dst[:, at:], src[:, at:], src[:, at - step:PAD + T - step], ALU.add))
                src = dst
            own, diff = u[:, f % 2, PAD:], tmp[:, levels % 2, PAD:]
            v.settle(dve, dve.scalar_tensor_tensor(diff, src[:, PAD:], 1.0 / w, own, ALU.mult, ALU.subtract))
            v.settle(dve, dve.tensor_tensor(diff[:, 0:w - 1], src[:, PAD:PAD + w - 1], k.inv_count[:, 0:w - 1], ALU.mult))
            dve.tensor_tensor(diff[:, 0:w - 1], diff[:, 0:w - 1], own[:, 0:w - 1], ALU.subtract).then_inc(s_diff, 1)
            dve.wait_ge(k.s_phi, f + 1)
            dve.tensor_tensor(k.plo[:, f], diff, k.phi[:, f].bitcast(F32), ALU.subtract).then_inc(k.s_plo, 1)
        end(k, dve)

    k.stage += 1


def pool_mix_stage(k, block):
    s_mix = k.sem("pool_mixed")
    GT = 2
    GROUPS_OF_SLAB = 2

    def bank(f, c):
        return k.aux[:, 2 * (f % 3) + c, :]

    @block.tensor
    def _(pe):
        for i in range(KT // GT):
            pe.wait_ge(k.s_plo, GT * (i + 1))
            slab, gg = MX_0 + i // GROUPS_OF_SLAB, i % GROUPS_OF_SLAB
            pe.wait_ge(k.s_split, slab + 1)
            for t in range(GT):
                f = GT * i + t
                if f >= 3:
                    pe.wait_ge(k.s_plo, KT + 2 * (f - 2))
                for c in range(2):
                    project(k, pe, slab, slab % 2, c, bank(f, c), k.phi, k.plo, [(4 * gg + 2 * a + t, GT * i + a) for a in range(GT)],
                            counts=t == GT - 1 and c == 1)
            pe.drain().then_inc(s_mix, 1)
        end(k, pe)

    @block.scalar
    def _(act):
        begin(k, act)
        for i in range(KT // GT):
            act.wait_ge(s_mix, i + 1)
            for t in range(GT):
                f = GT * i + t
                for c in range(2):
                    act.activation(k.phi[:, f, c * HALF:(c + 1) * HALF], bank(f, c), ACT.Copy, scale=param(k, "pool_scale", f)).then_inc(k.s_phi, 1)
        end(k, act)

    @block.vector
    def _(dve):
        begin(k, dve)
        for i in range(KT // GT):
            for t in range(GT):
                f = GT * i + t
                for c in range(2):
                    cols = slice(c * HALF, (c + 1) * HALF)
                    dve.wait_ge(k.s_phi, KT + 4 * i + 2 * t + c + 1)
                    dve.scalar_tensor_tensor(k.plo[:, f, cols], bank(f, c), param(k, "pool_scale", f), k.phi[:, f, cols].bitcast(F32),
                                             ALU.mult, ALU.subtract).then_inc(k.s_plo, 1)
        end(k, dve)

    k.stage += 1




def mixer_out_stage(k, block, mix):
    F = k.F
    k.x2 = k.at("x2", F + 32, [P, KT, T])
    k.ssum2, sq = k.at("x2_sum", F, [P, T]), k.at("x2_squared", F + 4, [P, T])
    s_hi, s_lo, s_x1, s_read = k.sem("mix_high"), k.sem("mix_low"), k.sem("x1_again"), k.sem("mixer_out_read")
    v = k.vstep
    mixed = lambda t: (k.s_mixed, k.banks_read[1] - 2 * (KT - 1 - t))

    @block.tensor
    def _(pe):
        pe.wait_ge(*k.banks_read)
        pe.sem_inc(s_read, 2)
        with pe.Fori(0, KT // 2) as m:
            for b in range(2):
                for c in range(2):
                    pe.wait_ge(s_read, m * 4 + (2 * b + c + 1))
                    project(k, pe, m * 2 + (WO_0 + b), (WO_0 + b) % 2, c, k.bank[c][:], k.hhi, k.hlo, ready=(s_lo, 0))
        end(k, pe)

    @block.scalar
    def _(act):
        act.wait_ge(k.s_proj, 2 * (PO_0 + 2 * (KT - 1)) + 2)
        for t in range(KT):
            act.wait_ge(*mixed(t))
            act.activation(k.hhi[:, t], mix[:, t], ACT.Copy).then_inc(s_hi, 1)
        begin(k, act)
        for t in range(KT):
            act.dma_start(k.x2[:, t], k.x1d[t]).then_inc(s_x1, 16)
        end(k, act)

    @block.vector
    def _(dve):
        for t in range(KT):
            dve.wait_ge(s_hi, t + 1)
            dve.tensor_tensor(k.hlo[:, t], mix[:, t], k.hhi[:, t].bitcast(F32), ALU.subtract).then_inc(s_lo, 1)
        begin(k, dve)
        dve.wait_ge(s_lo, KT)
        v.settle(dve, dve.memset(k.ssum2, 0.0))
        dve.wait_ge(s_x1, 16 * KT)
        with dve.Fori(0, KT) as f:
            v.enter(f, 2)
            for c in range(2):
                dve.wait_ge(k.s_proj, f * 2 + (2 * WO_0 + c + 1))
                xt = k.x2[:, ds(f, 1), c * HALF:(c + 1) * HALF].rearrange("p a b -> p (a b)")
                dve.scalar_tensor_tensor(xt, k.bank[c][:], k.mod[:, ds(f + 16, 1)], xt, ALU.mult, ALU.add).then_inc(s_read, 1)
            dve.wait_ge(s_read, f * 2 + 4)
            xt = k.x2[:, ds(f, 1), :].rearrange("p a b -> p (a b)")
            v.settle(dve, dve.tensor_tensor(sq, xt, xt, ALU.mult))
            v.settle(dve, dve.tensor_tensor(k.ssum2, k.ssum2, sq, ALU.add))
        v.leave(KT)
        end(k, dve)

    k.stage += 1


def ffn_stage(k, block, out):
    F = k.F
    fhi, flo = k.at("ffn_hi", F, [P, KT, T], F32R), k.at("ffn_lo", F + 64, [P, KT, T], F32R)
    act2 = k.at("ffn_relu_squared", F + 96, [P, 2, T])
    s_read, s_sq, s_hi, s_lo = k.sem("ffn_read"), k.sem("ffn_squared"), k.sem("ffn_high"), k.sem("ffn_low")
    s_x2, s_out = k.sem("x2_added"), k.sem("out_written")
    h_ready = k.h_ready
    ROUND = 2 * 2 * KT

    @block.tensor
    def _(pe):
        pe.sem_inc(s_x2, 2)
        with pe.Fori(0, FF_QUARTERS) as r:
            for f in range(KT):
                for c in range(2):
                    if f == 0:
                        pe.wait_ge(s_x2, r * (2 * KT) + (c + 1))
                    else:
                        pe.wait_ge(s_read, r * (2 * KT) + (2 * f + c - 1))
                    project(k, pe, r * (2 * KT) + (FF_0 + f), (FF_0 + f) % 2, c, k.bank[c][:], k.hhi, k.hlo, ready=h_ready if f == 0 else None)
            for f in range(KT):
                slab, slot = r * (2 * KT) + (FF_0 + KT + f), (FF_0 + KT + f) % 2
                if f == 0:
                    pe.wait_ge(s_lo, r * KT + KT)
                    for c in range(2):
                        pe.wait_ge(s_read, r * (2 * KT) + (2 * KT + c - 1))
                        project(k, pe, slab, slot, c, k.bank[c][:], fhi, flo, range(KT - 2), last=False, counts=False)
                    for c in range(2):
                        pe.wait_ge(s_lo, r * KT + (KT + 2))
                        project(k, pe, slab, slot, c, k.bank[c][:], fhi, flo, range(KT - 2, KT), first=False)
                    continue
                for c in range(2):
                    pe.wait_ge(s_x2, r * (2 * KT) + (2 * f + c + 1))
                    project(k, pe, slab, slot, c, k.bank[c][:], fhi, flo)
        end(k, pe)

    @block.scalar
    def _(act):
        begin(k, act)
        with act.Fori(0, FF_QUARTERS) as r:

            def high(f):
                act.wait_ge(s_sq, r * KT + (f + 1))
                act.activation(fhi[:, f], act2[:, f % 2], ACT.Copy).then_inc(s_hi, 1)

            for f in range(KT):
                act.wait_ge(s_lo, r * KT + (f + 1))
                for c in range(2):
                    act.wait_ge(k.s_proj, r * ROUND + (2 * FF_0 + 2 * f + c + 1))
                    act.activation(act2[:, f % 2, c * HALF:(c + 1) * HALF], k.bank[c][:], ACT.Copy).then_inc(s_read, 1)
                if f:
                    high(f - 1)
            high(KT - 1)
        end(k, act)

    @block.vector
    def _(dve):
        begin(k, dve)
        dve.sem_inc(s_lo, 2)
        with dve.Fori(0, FF_QUARTERS) as r:

            def low(f):
                dve.wait_ge(s_hi, r * KT + (f + 1))
                dve.tensor_tensor(flo[:, f], act2[:, f % 2], fhi[:, f].bitcast(F32), ALU.subtract).then_inc(s_lo, 1)

            for f in range(KT):
                dve.wait_ge(s_read, r * (2 * KT) + (2 * f + 2))
                dve.scalar_tensor_tensor(act2[:, f % 2], act2[:, f % 2], 0.0, act2[:, f % 2], ALU.max, ALU.mult).then_inc(s_sq, 1)
                if f:
                    low(f - 1)
            low(KT - 1)
            dve.wait_ge(s_lo, r * KT + (KT + 2))
            dve.wait_ge(s_x2, r * (2 * KT) + 2)
            for f in range(KT):
                for c in range(2):
                    dve.wait_ge(k.s_proj, r * ROUND + (2 * FF_0 + 2 * KT + 2 * f + c + 1))
                    xt = k.x2[:, f, c * HALF:(c + 1) * HALF]
                    dve.scalar_tensor_tensor(xt, k.bank[c][:], k.mod[:, 40 + f:41 + f], xt, ALU.mult, ALU.add).then_inc(s_x2, 1)
        end(k, dve)

    @block.sync
    def _(sp):
        for f in range(KT):
            sp.wait_ge(s_x2, 2 + 2 * KT * (FF_QUARTERS - 1) + 2 * f + 2)
            sp.dma_start(out[:, f], k.x2[:, f]).then_inc(s_out, 16)
        sp.wait_ge(s_out, 16 * KT)

    k.stage += 1




def build(nc, ins, out, scratch):
    with ExitStack() as ctx:
        k = make_core(nc, ctx)
        xT, wts, params, consts, gate_w, ada_w, bias = ins
        k.x1d, k.mixd, k.acd, k.dild = scratch
        k.s_spill = k.sem("x1_stored")
        block = ctx.enter_context(nc.Block())
        setup_stage(k, block, xT, params, consts, wts)
        weight_split(k, block)
        sq = k.at("pre_sq", k.Y + 2, [P, 2, T])
        ssum = k.at("pre_sum", k.Y + 10, [P, T])
        square_sum_stage(k, block, lambda t: k.xt[:, t], sq, ssum)
        params_in(k, block)
        tmp = k.at("pre_tmp", k.Y + 14, [P, 2, T])
        norm_split_stage(k, block, lambda t: k.xt[:, t], ssum, lambda t: param(k, "pre_g", t), None, tmp)
        vectors_stage(k, block)
        lru_stage(k, block, wts, gate_w, ada_w)
        rest_of_slabs(k, block, wts)
        attention_stage(k, block)
        out_project_stage(k, block)
        post_norm_stage(k, block, xT)
        block2_gains(k, block)
        tmp = k.at("norm1_tmp", k.W, [P, 2, T])
        norm_split_stage(k, block, lambda t: k.x1[:, t], k.ssum1, lambda t: k.gain1[:, t:t + 1], lambda t: k.mod[:, t:t + 1], tmp)
        ssd_inputs_stage(k, block)
        ssd_mix_stage(k, block)
        ssd_norm_stage(k, block)
        mix = k.at("ssd_mix", k.F, [P, KT, T])
        gate = k.at("ssd_gate", k.F + 32, [P, 2, HALF])
        gated_out_stage(k, block, SO_0, k.shi, k.slo, KT, mix, gate, (k.s_slo, 0), opens=True)
        dilated_stage(k, block, bias, mix)
        open_gates(k, block, AO_0)
        combine_stage(k, block, mix)
        gate = k.at("dil_gate", k.F + 101, [P, 2, HALF])
        gated_out_stage(k, block, AO_0, k.ahi, k.alo, DL_ROUNDS, mix, gate, (k.s_alo, 0, DL_ROUNDS), prior=(k.s_mix_in, 16 * KT))
        pool_stage(k, block)
        pool_mix_stage(k, block)
        open_gates(k, block, PO_0)
        gate = k.at("pool_gate", k.F + 96, [P, 2, HALF])
        gated_out_stage(k, block, PO_0, k.phi, k.plo, KT, mix, gate, (k.s_plo, KT, 2 * KT))
        mixer_out_stage(k, block, mix)
        tmp = k.at("norm2_tmp", k.F + 8, [P, 2, T])
        norm_split_stage(k, block, lambda t: k.x2[:, t], k.ssum2, lambda t: k.gain2[:, t:t + 1], lambda t: k.mod[:, 24 + t:25 + t], tmp)
        ffn_stage(k, block, out)


def slab(w, r0, c0, cols=P):
    part = w[r0:r0 + D, c0:c0 + cols]
    part = np.pad(part, ((0, D - part.shape[0]), (0, P - part.shape[1])))
    return part.reshape(KT, P, P).transpose(1, 0, 2)


def pack(i):
    w1, w2 = i["w_in"][0], i["w_in_2"][0]
    at_z, at_x, at_b, at_c, at_dt, at_q, at_k, at_v, at_u, at_g = 0, 1024, 2048, 2304, 2560, 2576, 4112, 5648, 7184, 8208
    tiles = lambda w, r0, c0: [slab(w, r0, c0 + t * P) for t in range(KT)]
    slabs = []
    for n in range(LRU_BLOCKS):
        slabs += [slab(w1, 0, 4 * D + n * P), slab(w1, 0, 5 * D + n * P)]
    for h in range(HEADS):
        slabs += [slab(w1, 0, part * D + h * P) for part in range(4)]
    for f in range(KT):
        slabs += [slab(i["w_out"][0], half * D, f * P) for half in range(2)]
    slabs += [slab(w2, 0, at_dt, SSD_HEADS)]
    slabs += [slab(w2, 0, c) for c in (at_c, at_c + P, at_b, at_b + P)] + tiles(w2, 0, at_x)
    slabs += tiles(w2, 0, at_z)

    def gated(n, w):
        return [s for f in range(KT) for s in (slab(w2, 0, at_g + n * D + f * P), slab(w, 0, f * P))]

    slabs += gated(0, i["w_ssd_out_2"][0])
    for j in range(DL_ROUNDS):
        for g in range(DIL_HEADS // DL_ROUNDS):
            slabs += [slab(w2, 0, a + (DL_ROUNDS * g + j) * P) for a in (at_q, at_k, at_v)]
        slabs += [np.zeros((P, KT, P), np.float32)]
    slabs += gated(1, i["w_attn_out_2"][0])
    slabs += tiles(w2, 0, at_u)
    pool = i["w_pool_mix_2"][0].reshape(2, 2, 2, P, 2, P)
    slabs += [pool[a].transpose(2, 0, 1, 3, 4).reshape(P, KT, P) for a in range(2)]
    slabs += gated(2, i["w_pool_out_2"][0])
    slabs += tiles(i["w_out_2"][0], 0, 0)
    for q in range(FF_QUARTERS):
        slabs += tiles(i["w_ff1_2"][0], 0, q * D) + tiles(i["w_ff2_2"][0], q * D, 0)
    wts = np.stack(slabs)
    assert len(wts) == N_SLABS
    col = lambda a: a.reshape(-1, P).T
    pair = lambda a, b: np.pad(np.stack([a.reshape(-1), b.reshape(-1)], 1), ((0, P - QK), (0, 0)))
    rows = lambda a: np.pad(a.reshape(-1, 1), ((0, P - a.size), (0, 0)))
    conv = i["conv_w"][0].reshape(TAPS, KT, P).transpose(2, 1, 0).reshape(P, -1)
    order = [10, 11, 8, 9, 0, 1, 2, 3, 4, 5, 6, 7]
    conv2 = i["conv_w_2"][0].reshape(TAPS, CV_TILES, P)[:, order].transpose(2, 1, 0).reshape(P, -1)
    params = np.concatenate([
        col(i["pre_norm_g"]), conv, col(i["conv_b"]), col(i["b_rgate"]), col(i["b_igate"]), col(i["lru_lambda"]), col(i["post_norm_g"]),
        col(i["subln_g"]), pair(i["lambda_q1"], i["lambda_q2"]), pair(i["lambda_k1"], i["lambda_k2"]), col(i["c_2"]), col(i["b_ada_2"]),
        conv2, col(i["conv_b_2"])[:, order], rows(i["dt_bias_2"]), np.broadcast_to(i["a_log_2"].reshape(1, -1), (P, SSD_HEADS)), col(np.repeat(i["d_skip_2"].reshape(-1), SSD_P)),
        col(i["ssd_norm_w_2"]), col(i["norm1_w_2"]), col(i["norm2_w_2"]), col(i["q_norm_w_2"]), col(i["k_norm_w_2"]), col(i["pool_scale_2"]),
    ], 1)
    gate = np.stack([i["w_rgate"][0], i["w_igate"][0]], 2).transpose(1, 0, 2, 3)
    ada = i["w_ada_2"][0].reshape(KT, P, LRU_BLOCKS, ADA_COLS).transpose(2, 0, 1, 3)
    xT = i["x"][0].T.reshape(KT, P, T)
    return {"xT": xT, "wts": wts, "params": params, "consts": constants(), "gate_w": gate, "ada_w": ada, "bias": dilated_bias()}


def constants():
    a, b = np.arange(P)[:, None], np.arange(P)[None, :]
    last = np.broadcast_to(a == P - 1, (P, P))
    return np.concatenate([np.eye(P), np.where(b <= a, 0.0, NEG), a <= b, last, 1.0 / np.broadcast_to(np.arange(1, N_CONST - INV + 1), (P, N_CONST - INV))], 1).astype(np.float32)


def dilated_bias():
    base = 2.0 ** (-8.0 / 8)
    more = 2.0 ** (-8.0 / 16)
    slopes = [base ** (n + 1) for n in range(8)] + [more ** (n + 1) for n in range(0, 8, 2)]
    slopes = np.sort(np.asarray(slopes, np.float32))[::-1]
    out = np.empty((DIL_HEADS, P, 2 * P), np.float32)
    for head in range(DIL_HEADS):
        group, dilation = head // DL_ROUNDS, (1, 4, 16)[head // DL_ROUNDS]
        q, key = np.arange(P)[:, None], np.arange(2 * P)[None, :]
        if group == 2:
            rel = np.where(key >= P, q % 64 - (key - P) % 64, -1)
            rel = np.where(q // 64 == (key - P) // 64, rel, -1)
        else:
            rel = q + P - key
        valid = (rel >= 0) & (rel <= P)
        out[head] = np.where(valid, -slopes[head] * (rel * dilation).astype(np.float32), NEG)
    return out


def kernel(**inputs):
    import concourse.bacc as bacc
    from concourse.bass_utils import run_bass_kernel_spmd

    nc = bacc.Bacc("TRN2", target_bir_lowering=False, num_devices=1)
    arrays = {n: np.ascontiguousarray(a) for n, a in pack({n: np.asarray(a) for n, a in inputs.items()}).items()}
    aps = [nc.dram_tensor(n, a.shape, F32, kind="ExternalInput").ap() for n, a in arrays.items()]
    out = nc.dram_tensor("outT", (P, KT, T), F32, kind="ExternalOutput").ap()
    scratch = [nc.dram_tensor(n, s, F32, kind="Internal").ap() for n, s in (
        ("x1_kept", (KT, P, T)), ("mix_kept", (KT, P, T)), ("decay_sums", (SSD_HEADS, T)), ("dilated_out", (DIL_HEADS, T, P + 2)))]
    build(nc, aps, out, scratch)
    r = run_bass_kernel_spmd(nc, [arrays], core_ids=[0])
    return np.ascontiguousarray(r.results[0]["outT"].transpose(2, 1, 0)).reshape(1, T, D)
```
